# Optimizing a Trainium2 kernel written in Bass

```python
import math
import jax, jax.numpy as jnp
from jax import lax
import numpy as np

D_MODEL = 1024
BATCH = 1
SEQ = 256
DEPTH = 2

MEM_LEN = 256
ROPE_THETA = 10000.0
EPS = 1e-6
Q_BLOCK = 128
D_FF = 2816
MLA_HEADS = 8
MLA_NOPE = 64
MLA_ROPE = 32
MLA_V = 64
MLA_Q_LORA = 256
MLA_KV_LORA = 128
DIL_PATTERNS = ((128, 1), (512, 4), (2048, 16))
DIL_GROUPS = len(DIL_PATTERNS)
DIL_HEADS = 4
DIL_HD = 64
SPA_HEADS = 16
SPA_HD = 64
IDX_HEADS = 8
IDX_HD = 64
TOPK_MAX = 256
X_HEADS = 4
X_HD = D_MODEL // X_HEADS
FULL_ROPE_DIM = 64

EVEN_IN = MLA_Q_LORA + MLA_KV_LORA + MLA_ROPE + 3 * DIL_GROUPS * DIL_HEADS * DIL_HD
EVEN_MIX = MLA_HEADS * MLA_V + DIL_HEADS * DIL_HD
ODD_IN = SPA_HEADS * SPA_HD + 2 * SPA_HD + IDX_HEADS * IDX_HD + IDX_HD + IDX_HEADS
ODD_MIX = SPA_HEADS * SPA_HD
N_EVEN = (DEPTH + 1) // 2
N_ODD = DEPTH // 2

kernel_name = 'hybrid_mla_dilated_dsa_macaron'

def rms_norm(x, g):
    xf = x.astype(jnp.float32)
    y = xf * lax.rsqrt(jnp.mean(xf * xf, axis=-1, keepdims=True) + EPS)
    return (y * g.astype(jnp.float32)).astype(x.dtype)

def rope_tables(positions, dim):
    inv = jnp.exp(-math.log(ROPE_THETA) * jnp.arange(0, dim, 2, dtype=jnp.float32) / dim)
    ang = positions.astype(jnp.float32)[..., None] * inv
    return jnp.cos(ang), jnp.sin(ang)

def apply_rope(x, cos, sin):
    half = x.shape[-1] // 2
    xf = x.astype(jnp.float32)
    x1, x2 = xf[..., :half], xf[..., half:]
    return jnp.concatenate([x1 * cos - x2 * sin, x2 * cos + x1 * sin], axis=-1).astype(x.dtype)

def swiglu(h, w13, w2):
    gu = h @ w13
    g, u = jnp.split(gu, 2, axis=-1)
    return (jax.nn.silu(g) * u) @ w2

def causal_block_attention(q, k, v, scale):
    B, S, H, _ = q.shape
    nb = S // Q_BLOCK
    qb = q.reshape(B, nb, Q_BLOCK, H, q.shape[-1]).swapaxes(0, 1)
    kpos = jnp.arange(S)

    def blk(args):
        qi, i = args
        qpos = i * Q_BLOCK + jnp.arange(Q_BLOCK)
        s = jnp.einsum('bqhd,bkhd->bhqk', qi, k).astype(jnp.float32) * scale
        s = jnp.where(kpos[None, :] <= qpos[:, None], s, -jnp.inf)
        p = jax.nn.softmax(s, axis=-1).astype(v.dtype)
        return jnp.einsum('bhqk,bkhd->bqhd', p, v)

    out = lax.map(blk, (qb, jnp.arange(nb)))
    return out.swapaxes(0, 1).reshape(B, S, H, v.shape[-1])

def dilated_group_attention(q, k, v, dilation, w_sub):
    B, S, H, E = q.shape
    L = S // dilation
    blk = w_sub
    nb = -(-L // blk)
    Lp = nb * blk

    def to_sub(a):
        a = a.reshape(B, L, dilation, H, E).transpose(0, 2, 1, 3, 4)
        return jnp.pad(a, ((0, 0), (0, 0), (0, Lp - L), (0, 0), (0, 0)))

    def windows(a):
        a = jnp.pad(a, ((0, 0), (0, 0), (blk, 0), (0, 0), (0, 0))).reshape(B, dilation, nb + 1, blk, H, E)
        return jnp.concatenate([a[:, :, :-1], a[:, :, 1:]], axis=3)

    qb = to_sub(q).reshape(B, dilation, nb, blk, H, E)
    kw = windows(to_sub(k))
    vw = windows(to_sub(v))
    s = jnp.einsum('bdnqhe,bdnkhe->bdnhqk', qb, kw).astype(jnp.float32) * (E ** -0.5)
    qi = jnp.arange(blk)[:, None]
    ki = jnp.arange(2 * blk)[None, :]
    rel = blk + qi - ki
    band = (rel >= 0) & (rel <= w_sub)
    kstart = (jnp.arange(nb)[:, None] - 1) * blk + jnp.arange(2 * blk)[None, :]
    mask = band[None] & (kstart >= 0)[:, None, :]
    s = jnp.where(mask[None, None, :, None], s, -jnp.inf)
    lse = jax.nn.logsumexp(s, axis=-1)
    p = jnp.exp(s - lse[..., None]).astype(v.dtype)
    o = jnp.einsum('bdnhqk,bdnkhe->bdnqhe', p, vw).reshape(B, dilation, Lp, H, E)[:, :, :L]
    o = o.transpose(0, 2, 1, 3, 4).reshape(B, S, H, E)
    lse = lse.transpose(0, 1, 2, 4, 3).reshape(B, dilation, Lp, H)[:, :, :L]
    lse = lse.transpose(0, 2, 1, 3).reshape(B, S, H)
    return o, lse

def even_mixer(h, w_in, q_lora_g, kv_lora_g, w_uq, w_ukv, mla_q_g, mla_k_g, dil_q_g, dil_k_g, w_out,
               cos32, sin32, cos64, sin64):
    B, S, _ = h.shape
    cols = h @ w_in
    o1 = MLA_Q_LORA
    o2 = o1 + MLA_KV_LORA
    o3 = o2 + MLA_ROPE
    c_q = rms_norm(cols[..., :o1], q_lora_g)
    c_kv = rms_norm(cols[..., o1:o2], kv_lora_g)
    q = (c_q @ w_uq).reshape(B, S, MLA_HEADS, MLA_NOPE + MLA_ROPE)
    q_nope = rms_norm(q[..., :MLA_NOPE], mla_q_g[:MLA_NOPE])
    q_rope = apply_rope(rms_norm(q[..., MLA_NOPE:], mla_q_g[MLA_NOPE:]), cos32[:, :, None], sin32[:, :, None])
    kv = (c_kv @ w_ukv).reshape(B, S, MLA_HEADS, MLA_NOPE + MLA_V)
    k_nope = rms_norm(kv[..., :MLA_NOPE], mla_k_g[:MLA_NOPE])
    v_a = kv[..., MLA_NOPE:]
    k_rope = apply_rope(rms_norm(cols[..., o2:o3], mla_k_g[MLA_NOPE:]), cos32, sin32)
    q_a = jnp.concatenate([q_nope, q_rope], axis=-1)
    k_a = jnp.concatenate([k_nope, jnp.broadcast_to(k_rope[:, :, None], (B, S, MLA_HEADS, MLA_ROPE))], axis=-1)
    mla_out = causal_block_attention(q_a, k_a, v_a, (MLA_NOPE + MLA_ROPE) ** -0.5)
    mla_out = mla_out.reshape(B, S, MLA_HEADS * MLA_V)
    dil = cols[..., o3:].reshape(B, S, DIL_GROUPS, 3, DIL_HEADS, DIL_HD)
    dq = apply_rope(rms_norm(dil[:, :, :, 0], dil_q_g), cos64[:, :, None, None], sin64[:, :, None, None])
    dk = apply_rope(rms_norm(dil[:, :, :, 1], dil_k_g), cos64[:, :, None, None], sin64[:, :, None, None])
    dv = dil[:, :, :, 2]
    outs, lses = [], []
    for g, (window, dilation) in enumerate(DIL_PATTERNS):
        o_g, lse_g = dilated_group_attention(dq[:, :, g], dk[:, :, g], dv[:, :, g], dilation, window // dilation)
        outs.append(o_g)
        lses.append(lse_g)
    wts = jax.nn.softmax(jnp.stack(lses, axis=0), axis=0)
    dil_out = jnp.sum(wts[..., None] * jnp.stack(outs, axis=0).astype(jnp.float32), axis=0).astype(h.dtype)
    dil_out = dil_out.reshape(B, S, DIL_HEADS * DIL_HD)
    return jnp.concatenate([mla_out, dil_out], axis=-1) @ w_out

def sparse_mixer(h, w_in, q_g, k_g, w_out, cos64, sin64):
    B, S, _ = h.shape
    cols = h @ w_in
    o1 = SPA_HEADS * SPA_HD
    o2 = o1 + SPA_HD
    o3 = o2 + SPA_HD
    o4 = o3 + IDX_HEADS * IDX_HD
    o5 = o4 + IDX_HD
    q = apply_rope(rms_norm(cols[..., :o1].reshape(B, S, SPA_HEADS, SPA_HD), q_g), cos64[:, :, None], sin64[:, :, None])
    k = apply_rope(rms_norm(cols[..., o1:o2], k_g), cos64, sin64)
    v = cols[..., o2:o3]
    qi = apply_rope(cols[..., o3:o4].reshape(B, S, IDX_HEADS, IDX_HD), cos64[:, :, None], sin64[:, :, None])
    ki = apply_rope(cols[..., o4:o5], cos64, sin64)
    wi = cols[..., o5:] * (IDX_HEADS ** -0.5)
    n_keep = min(TOPK_MAX, S // 4)
    nb = S // Q_BLOCK
    kpos = jnp.arange(S)

    def to_blocks(a):
        return a.reshape((B, nb, Q_BLOCK) + a.shape[2:]).swapaxes(0, 1)

    def attend(args):
        qb, qib, wib, i = args
        qpos = i * Q_BLOCK + jnp.arange(Q_BLOCK)
        logits = jnp.einsum('bqhe,bse->bqhs', qib, ki).astype(jnp.float32) * (IDX_HD ** -0.5)
        score = jnp.einsum('bqh,bqhs->bqs', wib.astype(jnp.float32), jax.nn.relu(logits))
        score = jnp.where(kpos[None, None, :] <= qpos[None, :, None], score, -jnp.inf)
        _, idx = lax.top_k(score, n_keep)
        valid = idx <= qpos[None, :, None]
        kg = jax.vmap(lambda a, ix: a[ix])(k, idx)
        vg = jax.vmap(lambda a, ix: a[ix])(v, idx)
        s = jnp.einsum('bqhe,bqke->bqhk', qb, kg).astype(jnp.float32) * (SPA_HD ** -0.5)
        s = jnp.where(valid[:, :, None, :], s, -jnp.inf)
        p = jax.nn.softmax(s, axis=-1).astype(vg.dtype)
        return jnp.einsum('bqhk,bqke->bqhe', p, vg)

    out = lax.map(attend, (to_blocks(q), to_blocks(qi), to_blocks(wi), jnp.arange(nb)))
    out = out.swapaxes(0, 1).reshape(B, S, ODD_MIX)
    return out @ w_out

def memory_cross_attention(h, mem_n, wq, wkv, q_g, k_g, wo):
    B, S, _ = h.shape
    M = mem_n.shape[1]
    q = rms_norm((h @ wq).reshape(B, S, X_HEADS, X_HD), q_g)
    kv = (mem_n @ wkv).reshape(B, M, 2, X_HEADS, X_HD)
    k = rms_norm(kv[:, :, 0], k_g)
    v = kv[:, :, 1]
    s = jnp.einsum('bshd,bmhd->bhsm', q, k).astype(jnp.float32) * (X_HD ** -0.5)
    p = jax.nn.softmax(s, axis=-1).astype(v.dtype)
    o = jnp.einsum('bhsm,bmhd->bshd', p, v).reshape(B, S, D_MODEL)
    return o @ wo

def setup_inputs(seed: int = 0) -> dict:
    key = jax.random.key(seed)
    ks = iter(jax.random.split(key, 40))

    def w(shape, fan_in):
        return jax.random.normal(next(ks), shape, jnp.float32) * (fan_in ** -0.5)

    def gain(shape):
        return 1.0 + 0.02 * jax.random.normal(next(ks), shape, jnp.float32)

    x = jax.random.normal(next(ks), (BATCH, SEQ, D_MODEL), jnp.float32)
    mem = jax.random.normal(next(ks), (BATCH, MEM_LEN, D_MODEL), jnp.float32)
    offsets = jax.random.randint(next(ks), (BATCH, 1), 0, 4096, dtype=jnp.int32)
    positions = (offsets + jnp.arange(SEQ, dtype=jnp.int32)[None, :]).astype(jnp.int32)
    return {
        'x': x, 'mem': mem, 'positions': positions,
        'ffn1_norm': gain((DEPTH, D_MODEL)),
        'ffn1_w13': w((DEPTH, D_MODEL, 2 * D_FF), D_MODEL),
        'ffn1_w2': w((DEPTH, D_FF, D_MODEL), D_FF),
        'mix_norm': gain((DEPTH, D_MODEL)),
        'xattn_norm': gain((DEPTH, D_MODEL)),
        'mem_norm': gain((DEPTH, D_MODEL)),
        'xattn_wq': w((DEPTH, D_MODEL, D_MODEL), D_MODEL),
        'xattn_wkv': w((DEPTH, D_MODEL, 2 * D_MODEL), D_MODEL),
        'xattn_q_gain': gain((DEPTH, X_HD)),
        'xattn_k_gain': gain((DEPTH, X_HD)),
        'xattn_wo': w((DEPTH, D_MODEL, D_MODEL), D_MODEL),
        'ffn2_norm': gain((DEPTH, D_MODEL)),
        'ffn2_w13': w((DEPTH, D_MODEL, 2 * D_FF), D_MODEL),
        'ffn2_w2': w((DEPTH, D_FF, D_MODEL), D_FF),
        'even_w_in': w((N_EVEN, D_MODEL, EVEN_IN), D_MODEL),
        'mla_q_lora_norm': gain((N_EVEN, MLA_Q_LORA)),
        'mla_kv_lora_norm': gain((N_EVEN, MLA_KV_LORA)),
        'mla_w_uq': w((N_EVEN, MLA_Q_LORA, MLA_HEADS * (MLA_NOPE + MLA_ROPE)), MLA_Q_LORA),
        'mla_w_ukv': w((N_EVEN, MLA_KV_LORA, MLA_HEADS * (MLA_NOPE + MLA_V)), MLA_KV_LORA),
        'mla_q_gain': gain((N_EVEN, MLA_NOPE + MLA_ROPE)),
        'mla_k_gain': gain((N_EVEN, MLA_NOPE + MLA_ROPE)),
        'dil_q_gain': gain((N_EVEN, DIL_HD)),
        'dil_k_gain': gain((N_EVEN, DIL_HD)),
        'even_w_out': w((N_EVEN, EVEN_MIX, D_MODEL), EVEN_MIX),
        'odd_w_in': w((N_ODD, D_MODEL, ODD_IN), D_MODEL),
        'sparse_q_gain': gain((N_ODD, SPA_HD)),
        'sparse_k_gain': gain((N_ODD, SPA_HD)),
        'odd_w_out': w((N_ODD, ODD_MIX, D_MODEL), ODD_MIX),
    }

def reference(x, mem, positions, ffn1_norm, ffn1_w13, ffn1_w2, mix_norm, xattn_norm, mem_norm,
              xattn_wq, xattn_wkv, xattn_q_gain, xattn_k_gain, xattn_wo, ffn2_norm, ffn2_w13, ffn2_w2,
              even_w_in, mla_q_lora_norm, mla_kv_lora_norm, mla_w_uq, mla_w_ukv, mla_q_gain, mla_k_gain,
              dil_q_gain, dil_k_gain, even_w_out, odd_w_in, sparse_q_gain, sparse_k_gain, odd_w_out):
    cos32, sin32 = rope_tables(positions, MLA_ROPE)
    cos64, sin64 = rope_tables(positions, FULL_ROPE_DIM)
    for i in range(DEPTH):
        j = i // 2
        x = x + 0.5 * swiglu(rms_norm(x, ffn1_norm[i]), ffn1_w13[i], ffn1_w2[i])
        h = rms_norm(x, mix_norm[i])
        if i % 2 == 0:
            mix = even_mixer(h, even_w_in[j], mla_q_lora_norm[j], mla_kv_lora_norm[j], mla_w_uq[j], mla_w_ukv[j],
                             mla_q_gain[j], mla_k_gain[j], dil_q_gain[j], dil_k_gain[j], even_w_out[j],
                             cos32, sin32, cos64, sin64)
        else:
            mix = sparse_mixer(h, odd_w_in[j], sparse_q_gain[j], sparse_k_gain[j], odd_w_out[j], cos64, sin64)
        x = x + mix
        x = x + memory_cross_attention(rms_norm(x, xattn_norm[i]), rms_norm(mem, mem_norm[i]), xattn_wq[i],
                                       xattn_wkv[i], xattn_q_gain[i], xattn_k_gain[i], xattn_wo[i])
        x = x + 0.5 * swiglu(rms_norm(x, ffn2_norm[i]), ffn2_w13[i], ffn2_w2[i])
    return x


_drawn_inputs = setup_inputs


def setup_inputs(seed=0):
    import zlib

    import numpy as np

    out = dict(_drawn_inputs(seed))
    spreads = {}
    factors = {'ffn1_norm': 2.792,
     'xattn_norm': 6.904,
     'mem_norm': 5.018,
     'xattn_q_gain': 6.478,
     'xattn_k_gain': 7.314,
     'ffn2_norm': 3.241,
     'mla_q_lora_norm': 5.368,
     'mla_kv_lora_norm': 5.404,
     'mla_q_gain': 6.857,
     'mla_k_gain': 5.816,
     'dil_q_gain': 8.0,
     'dil_k_gain': 8.0,
     'sparse_q_gain': 8.0,
     'sparse_k_gain': 8.0}
    for name, (base, spread) in spreads.items():
        noise = np.random.default_rng([zlib.crc32(name.encode()), seed]).standard_normal(out[name].shape)
        drawn = base * np.exp(spread * noise) if base else spread * noise
        out[name] = __import__('jax').numpy.asarray(drawn.astype(out[name].dtype))
    for name, factor in factors.items():
        out[name] = (out[name] * factor).astype(out[name].dtype)
    return out
```

```python
import math
from contextlib import ExitStack

import numpy as np

import concourse.bass as bass
from concourse import mybir

F32 = mybir.dt.float32
F32R = mybir.dt.float32r
BF16 = mybir.dt.bfloat16
I32 = mybir.dt.int32
ALU = mybir.AluOpType
ACT = mybir.ActivationFunctionType
AX = mybir.AxisListType.X

P = 128
D = 1024
SEQ = 256
NT = SEQ // P
KD = D // P
FF = 2816
CH = 256
NCH = FF // CH
EPS = 1e-6
NEG = -1e30
TAKEN = -3e38
HD = 64
Q_LORA, KV_LORA, ROPE = 256, 128, 32
MLA_H, MLA_QK = 8, 96
DIL0 = Q_LORA + KV_LORA + ROPE
EVEN_IN = DIL0 + 2304
SPA_H, IDX_H = 16, 8
ODD_IN = 1736
TOPK = 64
X_H, X_HD = 4, 256
RAW, SPLIT = 6, 6
LOOPS = 4
C1 = 6.28125
C2 = float(np.float32(np.float32((2 * math.pi - C1) * 2 ** 20).astype(np.int64) // 2 ** 6 * 2 ** 6 / 2 ** 20))
C3 = float(np.float32(2 * math.pi - C1 - C2))
ROUND = 12582912.0


class Projection:

    def __init__(self, name, rows, groups, wide=False):
        self.name, self.kt, self.groups, self.wide = name, rows // P, groups, wide
        self.starts = [sum(groups[:g]) for g in range(len(groups))]
        self.upg = 1 if wide else (self.kt + 1) // 2
        self.units = 1 if wide else self.upg * len(groups)

    def end(self, g):
        return self.unit0 + (1 if self.wide else self.upg * (g + 1))


def plan_stream():
    order = ["ffn0",
             Projection("even_in", D, [DIL0, 512, 512, 512, 512, 256]),
             Projection("uq", Q_LORA, [512, 256]),
             Projection("ukv", KV_LORA, [512, 512], wide=True),
             Projection("memkv0", D, [512] * 4),
             Projection("even_out", 768, [512] * 2),
             Projection("xq0", D, [512] * 2), Projection("xo0", D, [512] * 2),
             "ffn1", "ffn2",
             Projection("odd_in", D, [512, 512, 512, 200]),
             Projection("memkv1", D, [512] * 4),
             Projection("odd_out", D, [512] * 2),
             Projection("xq1", D, [512] * 2), Projection("xo1", D, [512] * 2),
             "ffn3"]
    unit = group = 0
    places = {}
    for it in order:
        if isinstance(it, str):
            places[it] = unit
            unit += 6 * NCH
        else:
            it.unit0, it.group0 = unit, group
            unit += it.units
            group += len(it.groups)
            places[it.name] = it
    return order, places, unit


def plan_rms():
    widths = []
    def both(name, w):
        for t in range(NT):
            widths.append((f"{name}{t}", w))
    for layer in range(2):
        both(f"norm_ffn1_{layer}_", 1)
        both(f"norm_mix_{layer}_", 1)
        if layer == 0:
            for t in range(NT):
                widths += [(f"lora_q{t}", 1), (f"lora_kv{t}", 1)]
        both(f"norm_mem_{layer}_", 1)
        if layer == 0:
            for t in range(NT):
                widths += [(f"mla_q{t}", 8), (f"mla_qr{t}", 8), (f"mla_k{t}", 8), (f"mla_kr{t}", 1)]
            for t in range(NT):
                widths += [(f"dil{g}_{t}", 8) for g in range(3)]
        else:
            for t in range(NT):
                widths += [(f"spa_q0_{t}", 8), (f"spa_q1_{t}", 8), (f"spa_k{t}", 1)]
        both(f"memk{layer}_", X_H)
        both(f"norm_x_{layer}_", 1)
        both(f"xq{layer}_", X_H)
        both(f"norm_ffn2_{layer}_", 1)
    out, col = {}, 0
    for i, (name, w) in enumerate(widths):
        out[name] = (i, col, w)
        col += w
    return out, col


def half_first(r):
    return 2 * (r % 4) + r // 4


class Tile:

    def __init__(self, kind, qt, rows, segs, keys, first, out, scale):
        self.kind, self.qt, self.rows, self.segs, self.keys = kind, qt, rows, segs, keys
        self.first, self.out, self.scale = first, out, scale
        self.width = segs * keys
        self.blocks = rows * self.width // P
        self.pitch = 1024 if kind == "dil" else self.width

    def head(self, r):
        return half_first(r) + self.first if self.kind == "spa" else self.first + r


def even_tiles():
    mla = [Tile("mla", qt, MLA_H, 1, P * (qt + 1), 0, HD, MLA_QK ** -0.5) for qt in range(NT)]
    dil = [Tile("dil", qt, 2, 3, P * (qt + 1), h, HD, HD ** -0.5) for qt in range(NT) for h in (0, 2)]
    return mla, dil


def odd_tiles():
    return [Tile("spa", qt, 8, 1, P * (qt + 1), h, HD, HD ** -0.5) for qt in range(NT) for h in (0, 8)]


def x_tiles():
    return [Tile("x", qt, X_H, 1, SEQ, 0, X_HD, X_HD ** -0.5) for qt in range(NT)]


def build(nc, x_in, mem_in, positions, ffn_norms, ffn_w13, ffn_w2, mix_norm, xattn_norm, mem_norm,
          xattn_wq, xattn_wkv, xattn_q_gain, xattn_k_gain, xattn_wo, even_w_in, q_lora_norm, kv_lora_norm,
          w_uq, w_ukv, mla_q_gain, mla_k_gain, dil_q_gain, dil_k_gain, even_w_out, odd_w_in,
          sparse_q_gain, sparse_k_gain, odd_w_out, rope_freq, y_out):
    order, place, UNITS = plan_stream()
    rms, RMS_COLS = plan_rms()
    MLA_TILES, DIL_TILES = even_tiles()
    SPA_TILES, X_TILES = odd_tiles(), x_tiles()
    weights = {"even_in": even_w_in[0], "uq": w_uq[0], "ukv": w_ukv[0], "even_out": even_w_out[0],
               "odd_in": odd_w_in[0], "odd_out": odd_w_out[0]}
    for l in range(2):
        weights[f"memkv{l}"], weights[f"xq{l}"], weights[f"xo{l}"] = xattn_wkv[l], xattn_wq[l], xattn_wo[l]

    ctx = ExitStack()
    with ctx:
        def sb(name, shape, dt=F32):
            return ctx.enter_context(nc.sbuf_tensor(name, shape, dt))

        def sem(name):
            return ctx.enter_context(nc.semaphore(name))

        raw = sb("raw", [P, RAW, 1024])
        w_hi = sb("w_hi", [P, SPLIT, 1024], F32R)
        w_lo = sb("w_lo", [P, SPLIT, 1024], F32R)
        act_hi = sb("act_hi", [P, KD, SEQ], F32R)
        act_lo = sb("act_lo", [P, KD, SEQ], F32R)
        x = sb("x", [P, NT, D])
        tm = sb("tm", [P, NT, D])
        kvb = sb("kvb", [P, NT, 2 * D])
        cols = sb("cols", [P, NT, EVEN_IN])
        v_mla = sb("v_mla", [P, NT, MLA_H * HD])
        qkT = sb("qkT", [P, 4096])
        scb = sb("scb", [P, 2048])
        pTb = sb("pTb", [P, 2048])
        gain = sb("gain", [P, D])
        causal = sb("causal", [P, SEQ])
        dil_mask = sb("dil_mask", [P, 3, SEQ])
        lora_gain = sb("lora_gain", [P, Q_LORA + KV_LORA])
        nope_gain = sb("nope_gain", [P, 2, HD])
        x_gain = sb("x_gain", [P, 2, X_HD])
        freq = sb("freq", [P, 48])
        pos_i = sb("pos_i", [P, NT], I32)
        pos_f = sb("pos_f", [P, NT])
        rc64 = sb("rc64", [P, NT, HD])
        rs64 = sb("rs64", [P, NT, HD])
        gc64 = sb("gc64", [P, NT, 4, HD])
        gs64 = sb("gs64", [P, NT, 4, HD])
        head_gain = sb("head_gain", [P, 2 * ROPE + 4 * HD])
        gc32 = sb("gc32", [P, NT, 2, ROPE])
        gs32 = sb("gs32", [P, NT, 2, ROPE])
        scr_a = sb("scr_a", [P, 512])
        scr_b = sb("scr_b", [P, 512])
        sumsq = sb("sumsq", [P, RMS_COLS])
        meansq = sumsq
        rstd = sb("rstd", [P, RMS_COLS])
        minus_half = sb("minus_half", [P, 8])
        rowmax = sb("rowmax", [P, 8])
        negmax = sb("negmax", [P, 2, 8])
        den = sb("den", [P, 2, 8])
        rden = sb("rden", [P, 8])
        w_idx = sb("w_idx", [P, NT, IDX_H])
        top8 = sb("top8", [P, 8])
        ident = sb("ident", [P, P])
        zeros = sb("zeros", [P, P], BF16)

        silu_g = cols[:, 0, 0:512].rearrange("p (t f) -> p t f", t=NT)
        gated = cols[:, 0, 512:1024].rearrange("p (t f) -> p t f", t=NT)
        gT_hi = sb("gT_hi", [P, 2, SEQ], F32R)
        gT_lo = sb("gT_lo", [P, 2, SEQ], F32R)
        q_mla = scb[:, 0:1536].rearrange("p (t c) -> p t c", t=NT)
        k_mla = pTb[:, 0:1536].rearrange("p (t c) -> p t c", t=NT)
        mla_qT = qkT[:, 0:2048].rearrange("p (h s) -> p h s", h=8)
        mla_kT = qkT[:, 2048:4096].rearrange("p (h s) -> p h s", h=8)
        dil_qT = qkT[:, 0:1536].rearrange("p (b s) -> p b s", b=6)
        dil_kT = qkT[:, 1536:3072].rearrange("p (b s) -> p b s", b=6)
        spa_qT = qkT[:, 0:2048].rearrange("p (b s) -> p b s", b=8)
        idx_qT = qkT[:, 2048:3072].rearrange("p (b s) -> p b s", b=4)
        spa_kT = qkT[:, 3072:3328]
        idx_kT = qkT[:, 3328:3584]
        x_qT = qkT[:, 0:2048].rearrange("p (b s) -> p b s", b=8)
        x_kT = qkT[:, 2048:4096].rearrange("p (b s) -> p b s", b=8)
        angle = scb[:, 0:192].rearrange("p (j t f) -> p j t f", j=2, t=NT)
        sines = scb[:, 192:384].rearrange("p (j t f) -> p j t f", j=2, t=NT)
        sel_bias = dil_mask[:, 0:NT, :]
        twin = cols[:, :, ODD_IN:ODD_IN + 256]
        score = cols[:, :, ODD_IN + 256:ODD_IN + 512]
        left = cols[:, :, ODD_IN + 512:ODD_IN + 768]

        low = ctx.enter_context(nc.psum_tensor("low", [P, 2048], F32))
        SC = [low[:, i * 512:(i + 1) * 512] for i in range(4)]
        high = ctx.enter_context(nc.psum_tensor("high", [P, 2048], F32))
        CK = [high[:, 0:512], high[:, 512:1024]]
        OB = high[:, 1024:2048]

        def acc(t, n):
            return high[:, (2 * n + t) * 512:(2 * n + t + 1) * 512]

        const_loaded = sem("const_loaded")
        x_loaded = [sem(f"x_loaded{t}") for t in range(NT)]
        gain_loaded = sem("gain_loaded")
        mem_loaded = [sem(f"mem_loaded{t}") for t in range(NT)]
        xgain_loaded = sem("xgain_loaded")
        unit_loaded = [sem(f"unit_loaded{i}") for i in range(RAW)]
        loader_turn = sem("loader_turn")
        hi_done = sem("hi_done")
        lo_done = sem("lo_done")
        unit_used = sem("unit_used")
        silu_done = sem("silu_done")
        gated_done = sem("gated_done")
        gT_psum = sem("gT_psum")
        gT_hi_done = sem("gT_hi_done")
        gT_split = sem("gT_split")
        ffn_sum = sem("ffn_sum")
        x_updated = sem("x_updated")
        sumsq_done = sem("sumsq_done")
        meansq_done = sem("meansq_done")
        rstd_done = sem("rstd_done")
        rows_ready = sem("rows_ready")
        T_psum = sem("T_psum")
        T_hi = sem("T_hi")
        T_split = sem("T_split")
        group_out = [sem(f"group_out{t}") for t in range(NT)]
        heads_ready = sem("heads_ready")
        chunk_psum = sem("chunk_psum")
        chunk_out = [sem("chunk_out_dve"), sem("chunk_out_act")]
        scores_ready = sem("scores_ready")
        scores_read = sem("scores_read")
        max_ready = sem("max_ready")
        probs_ready = sem("probs_ready")
        out_ready = sem("out_ready")
        out_read = sem("out_read")
        logits_ready = sem("logits_ready")
        relu_done = sem("relu_done")
        score_done = sem("score_done")
        pool_step = sem("pool_step")
        consts_made = sem("consts_made")
        angle_ready = sem("angle_ready")
        sin_ready = sem("sin_ready")
        dve_step = sem("dve_step")
        stored = sem("stored")

        NORMS = []
        for l in range(2):
            NORMS += [ffn_norms[0][l:l + 1, :], mix_norm[l:l + 1, :], mem_norm[l:l + 1, :],
                      xattn_norm[l:l + 1, :], ffn_norms[1][l:l + 1, :]]
        X_UPDATES = 4 * NT
        N_SMALL = 13

        def val(base, per_turn, i):
            return base if i is None else i * per_turn + base

        T_KT = [8, 8, 3, 8, 6, 8, 8, 8, 8, 8, 8, 8, 8, 8, 8]
        ROWS = [nm for nm in ("ffn0", "even_in", "lora", "memkv0", "xq0", "ffn1", "ffn2", "odd_in", "memkv1",
                              "xq1", "ffn3")]
        T_NAMES = ["ffn0", "even_in", "lora", "memkv0", "even_out", "xq0", "xo0", "ffn1", "ffn2", "odd_in",
                   "memkv1", "odd_out", "xq1", "xo1", "ffn3"]
        T_first = {}
        n = 0
        for name, kt in zip(T_NAMES, T_KT):
            T_first[name] = (n, kt, T_NAMES.index(name))
            n += NT * (2 if kt > 4 else 1)

        def T_parts(name):
            c, kt, _ = T_first[name]
            for t in range(NT):
                for h in range(2 if kt > 4 else 1):
                    yield c, t, 4 * h, min(4, kt - 4 * h)
                    c += 1

        def T_done(name):
            c, kt, _ = T_first[name]
            return c + NT * (2 if kt > 4 else 1)

        TILE0 = {"mla": 0, "dil": len(MLA_TILES), "x0": len(MLA_TILES) + len(DIL_TILES)}
        TILE0["spa"] = TILE0["x0"] + len(X_TILES)
        TILE0["x1"] = TILE0["spa"] + len(SPA_TILES)

        def mla_chunks():
            for t in range(NT):
                for src, dst in ((q_mla, mla_qT), (k_mla, mla_kT)):
                    for g in (0, 4):
                        yield ([src[:, t, h * MLA_QK:(h + 1) * MLA_QK] for h in range(g, g + 4)],
                               dst[0:MLA_QK, g:g + 4, t * P:(t + 1) * P])

        def dil_cols(t):
            return cols[:, t, DIL0:EVEN_IN].rearrange("p (g h e) -> p g h e", g=3, h=12)

        def dil_chunks():
            for t in range(NT):
                for first, dst in ((0, dil_qT), (256, dil_kT)):
                    for b, n in ((0, 4), (4, 2)):
                        yield ([cols[:, t, DIL0 + (bb // 2) * 768 + first + (bb % 2) * P:][:, 0:P]
                                for bb in range(b, b + n)],
                               dst[:, b:b + n, t * P:(t + 1) * P])

        def idx_chunks():
            for t in range(NT):
                yield ([cols[:, t, 1152 + b * P:1152 + (b + 1) * P] for b in range(4)],
                       idx_qT[:, :, t * P:(t + 1) * P])
            for t in range(NT):
                yield ([twin[:, t, P:2 * P]], idx_kT[:, t * P:(t + 1) * P].unsqueeze(1))

        def spa_chunks():
            for t in range(NT):
                for b in (0, 4):
                    yield ([cols[:, t, bb * P:(bb + 1) * P] for bb in range(b, b + 4)],
                           spa_qT[:, b:b + 4, t * P:(t + 1) * P])
            for t in range(NT):
                yield ([twin[:, t, 0:P]], spa_kT[:, t * P:(t + 1) * P].unsqueeze(1))

        def x_chunks():
            for src, dst in ((kvb, x_kT), (cols, x_qT)):
                for t in range(NT):
                    for b in (0, 4):
                        yield ([src[:, t, bb * P:(bb + 1) * P] for bb in range(b, b + 4)],
                               dst[:, b:b + 4, t * P:(t + 1) * P])

        def prob_chunks(tl):
            for j in range(0, tl.blocks, 4):
                n = min(4, tl.blocks - j)
                yield ([scb[:, b * P:(b + 1) * P] for b in range(j, j + n)],
                       pTb[:, j * P:(j + n) * P].rearrange("p (b s) -> p b s", b=n))

        def cols_pairs(pr, t, g):
            w = pr.groups[g]
            return [(cols[:, t, pr.starts[g]:pr.starts[g] + w], acc(t, (pr.group0 + g) % 2)[:, 0:w])]

        def uq_pairs(t, g):
            pr = place["uq"]
            w = pr.groups[g]
            return [(q_mla[:, t, pr.starts[g]:pr.starts[g] + w], acc(t, (pr.group0 + g) % 2)[:, 0:w])]

        def ukv_pairs(t, g):
            src = acc(t, (place["ukv"].group0 + g) % 2).rearrange("p (h c) -> p h c", h=4)
            k = k_mla[:, t, :].rearrange("p (h c) -> p h c", h=MLA_H)[:, 4 * g:4 * g + 4, 0:HD]
            v = v_mla[:, t, 256 * g:256 * (g + 1)].rearrange("p (h c) -> p h c", h=4)
            return [(k, src[:, :, 0:HD]), (v, src[:, :, HD:])]

        def memkv_pairs(pr, t, g):
            return [(kvb[:, t, g * 512:(g + 1) * 512], acc(t, (pr.group0 + g) % 2))]

        HEADS = {name: i + 1 for i, name in enumerate(("mla", "dil", "x0", "idx", "spa", "x1"))}

        block = ctx.enter_context(nc.Block())

        @block.sync
        def _(sp):
            def slot_free(n, i=None):
                if n >= RAW or i is not None:
                    sp.wait_ge(lo_done, val(max(1, n - RAW + 1), 12, i))
                    if i is not None:
                        sp.sem_inc(loader_turn, 1)

            def load_w13(l, n, c, g, i=None):
                src = ffn_w13[l].rearrange("(k p) (u f) -> p k u f", p=P, u=2)[:, 2 * g:2 * g + 2, :, :]
                col = val(c * CH, 2 * CH, i)
                dst = raw[:, n % RAW, :].rearrange("p (k u f) -> p k u f", k=2, u=2)
                slot_free(n, i)
                for u in range(2):
                    sp.dma_start(dst[:, :, u, :], src[:, :, u, bass.ds(col, CH)]).then_inc(unit_loaded[n % RAW], 16)

            def load_w2(l, n, c, b, i=None):
                slot_free(n, i)
                row = val(c * CH + b * P, 2 * CH, i)
                for h in range(2):
                    at = slice(h * 512, (h + 1) * 512)
                    sp.dma_start(raw[:, n % RAW, at], ffn_w2[l][bass.ds(row, P), at])\
                        .then_inc(unit_loaded[n % RAW], 16)

            def load_step(l, n, c, i=None):
                for g in range(4):
                    load_w13(l, n + g, c, g, i)
                for b in range(2):
                    load_w2(l, n + 4 + b, c - 1, b, i)

            def load_ffn(f):
                n = place[f"ffn{f}"]
                for g in range(4):
                    load_w13(f, n + g, 0, g)
                n += 4
                with sp.Fori(0, LOOPS) as i:
                    load_step(f, n, 1, i)
                    load_step(f, n + 6, 2, i)
                for c in range(1 + 2 * LOOPS, NCH):
                    load_step(f, n + 6 * (c - 1), c)
                for b in range(2):
                    load_w2(f, n + 6 * (NCH - 1) + b, NCH - 1, b)

            def load_projection(pr):
                w = weights[pr.name].rearrange("(k p) n -> p k n", p=P)
                n = pr.unit0
                if pr.wide:
                    slot_free(n)
                    for h in range(2):
                        at = slice(h * 512, (h + 1) * 512)
                        sp.dma_start(raw[:, n % RAW, at], w[:, 0, at]).then_inc(unit_loaded[n % RAW], 16)
                    return
                for g, width in enumerate(pr.groups):
                    for u in range(pr.upg):
                        slot_free(n)
                        for k in range(2):
                            sp.dma_start(raw[:, n % RAW, k * 512:k * 512 + width],
                                         w[:, 2 * u + k, pr.starts[g]:pr.starts[g] + width])\
                                .then_inc(unit_loaded[n % RAW], 16)
                        n += 1

            for it in order:
                if isinstance(it, str):
                    load_ffn(int(it[3:]))
                else:
                    load_projection(it)
            for t in range(NT):
                sp.wait_ge(x_updated, X_UPDATES - NT + t + 1)
                sp.dma_start(y_out[t * P:(t + 1) * P, :], x[:, t, :]).then_inc(stored, 16)
            sp.wait_ge(stored, 16 * NT)

        @block.gpsimd
        def _(pool):
            for t in range(NT):
                pool.dma_start(x[:, t, :], x_in[t * P:(t + 1) * P, :]).then_inc(x_loaded[t], 16)
            pool.dma_start(gain[:, :], NORMS[0].to_broadcast([P, D])).then_inc(gain_loaded, 16)
            nc.gpsimd.memset(minus_half[:, :], -0.5).then_inc(pool_step, 1)
            nc.gpsimd.memset(ident[:, :], 0.0).then_inc(pool_step, 1)
            nc.gpsimd.memset(causal[:, :], 0.0).then_inc(pool_step, 1)
            pool.wait_ge(pool_step, 3)
            nc.gpsimd.affine_select(out=ident[:, :], in_=ident[:, :], compare_op=ALU.not_equal, fill=1.0,
                                    base=0, pattern=[[-1, P]], channel_multiplier=1).then_inc(consts_made, 1)
            nc.gpsimd.memset(zeros[:, :], 0.0).then_inc(consts_made, 1)
            nc.gpsimd.affine_select(out=causal[:, :], in_=causal[:, :], compare_op=ALU.is_ge, fill=NEG,
                                    base=P, pattern=[[-1, SEQ]], channel_multiplier=1).then_inc(consts_made, 1)
            nc.gpsimd.iota(pTb[:, 0:SEQ].bitcast(I32), pattern=[[-1, SEQ]], base=SEQ,
                           channel_multiplier=1).then_inc(consts_made, 1)
            pool.wait_ge(consts_made, 4)
            nc.gpsimd.affine_select(out=dil_mask[:, 0, :], in_=causal[:, :], compare_op=ALU.is_ge, fill=NEG,
                                    base=0, pattern=[[1, SEQ]], channel_multiplier=-1).then_inc(consts_made, 1)
            small = [(pos_i[:, t:t + 1], positions[0:1, t * P:(t + 1) * P].rearrange("o p -> p o"))
                     for t in range(NT)]
            small += [(freq[:, :], rope_freq[0:1, :].to_broadcast([P, 48])),
                      (lora_gain[:, 0:Q_LORA], q_lora_norm.to_broadcast([P, Q_LORA])),
                      (lora_gain[:, Q_LORA:], kv_lora_norm.to_broadcast([P, KV_LORA])),
                      (nope_gain[:, 0, :], mla_q_gain[:, 0:HD].to_broadcast([P, HD])),
                      (nope_gain[:, 1, :], mla_k_gain[:, 0:HD].to_broadcast([P, HD])),
                      (head_gain[:, 0:ROPE], mla_q_gain[:, HD:].to_broadcast([P, ROPE])),
                      (head_gain[:, ROPE:2 * ROPE], mla_k_gain[:, HD:].to_broadcast([P, ROPE]))]
            small += [(head_gain[:, 64 + i * HD:64 + (i + 1) * HD], g.to_broadcast([P, HD]))
                      for i, g in enumerate((dil_q_gain, dil_k_gain, sparse_q_gain, sparse_k_gain))]
            assert len(small) == N_SMALL
            for dst, src in small:
                pool.dma_start(dst, src).then_inc(const_loaded, 16)

            def serve(*names):
                for name in names:
                    i, c, w = rms[name]
                    pool.wait_ge(meansq_done, i + 1)
                    nc.gpsimd.tensor_tensor(rstd[:, c:c + w], meansq[:, c:c + w], minus_half[:, 0:w],
                                            ALU.pow).then_inc(rstd_done, 1)

            def both(name):
                return [f"{name}{t}" for t in range(NT)]

            def next_gain(n, name):
                pool.wait_ge(rows_ready, NT * (ROWS.index(name) + 1))
                pool.dma_start(gain[:, :], NORMS[n].to_broadcast([P, D])).then_inc(gain_loaded, 16)

            for l in range(2):
                if l:
                    pool.wait_ge(out_read, TILE0["x0"] + len(X_TILES))
                for t in range(NT):
                    pool.dma_start(kvb[:, t, 0:D], mem_in[t * P:(t + 1) * P, :]).then_inc(mem_loaded[t], 16)
                pool.dma_start(x_gain[:, 0, :], xattn_q_gain[l:l + 1, :].to_broadcast([P, X_HD]))\
                    .then_inc(xgain_loaded, 16)
                pool.dma_start(x_gain[:, 1, :], xattn_k_gain[l:l + 1, :].to_broadcast([P, X_HD]))\
                    .then_inc(xgain_loaded, 16)
                serve(*both(f"norm_ffn1_{l}_"))
                next_gain(5 * l + 1, f"ffn{2 * l}")
                serve(*both(f"norm_mix_{l}_"))
                next_gain(5 * l + 2, ("even_in", "odd_in")[l])
                if l == 0:
                    for t in range(NT):
                        serve(f"lora_q{t}", f"lora_kv{t}")
                serve(*both(f"norm_mem_{l}_"))
                next_gain(5 * l + 3, f"memkv{l}")
                for t in range(NT):
                    if l == 0:
                        serve(f"mla_q{t}", f"mla_qr{t}", f"mla_k{t}", f"mla_kr{t}")
                    else:
                        serve(f"spa_q0_{t}", f"spa_q1_{t}", f"spa_k{t}")
                if l == 0:
                    for t in range(NT):
                        serve(*[f"dil{g}_{t}" for g in range(3)])
                serve(*both(f"memk{l}_"))
                serve(*both(f"norm_x_{l}_"))
                next_gain(5 * l + 4, f"xq{l}")
                serve(*both(f"xq{l}_"))
                serve(*both(f"norm_ffn2_{l}_"))
                if l == 0:
                    next_gain(5, "ffn1")

        @block.scalar
        def _(act):
            done = [0]
            chunk = [0]
            tile = [0]

            def hi(n, i=None):
                act.wait_ge(unit_loaded[n % RAW], val(32 * (n // RAW + 1), 32 * 12 // RAW, i))
                if n >= SPLIT:
                    act.wait_ge(unit_used, val(n - SPLIT + 1, 12, i))
                nc.scalar.copy(w_hi[:, n % SPLIT, :], raw[:, n % RAW, :]).then_inc(hi_done, 1)

            def hi_until(n):
                while done[0] < min(n, UNITS):
                    hi(done[0])
                    done[0] += 1

            def square_rows(name, t, src, junk, sem_, count):
                act.wait_ge(sem_, count)
                c = rms[name][1]
                nc.scalar.activation(junk, src, ACT.Square, accum_out=sumsq[:, c:c + 1]).then_inc(sumsq_done, 1)

            def squares(name, wait):
                for t in range(NT):
                    square_rows(f"{name}{t}", t, x[:, t, :], tm[:, t, :], *wait(t))

            def T_hi_part(c, t, b, nb):
                act.wait_ge(T_psum, c + 1)
                nc.scalar.copy(act_hi[:, b:b + nb, t * P:(t + 1) * P],
                               SC[2 * t + b // 4][:, 0:nb * P].rearrange("p (b s) -> p b s", b=nb))\
                    .then_inc(T_hi, 1)

            def T_event(name):
                for part in T_parts(name):
                    T_hi_part(*part)

            def silu(f, c, used, i=None):
                act.wait_ge(unit_used, val(used, 12, i))
                for t in range(NT):
                    nc.scalar.activation(silu_g[:, t, :], SC[t][:, 0:CH], ACT.Silu).then_inc(silu_done, 1)

            def gT_hi_step(f, c, i=None):
                act.wait_ge(gT_psum, val(NCH * f + c + 1, 2, i))
                nc.scalar.copy(gT_hi[:, :, :], SC[2].rearrange("p (b s) -> p b s", b=2)).then_inc(gT_hi_done, 1)

            def ffn_step(f, n, c, i=None):
                gT_hi_step(f, c - 1, i)
                for u in range(6, 10):
                    if n + u < UNITS:
                        hi(n + u, i)
                silu(f, c, n + 4, i)
                for u in range(10, 12):
                    if n + u < UNITS:
                        hi(n + u, i)

            def ffn(f):
                n = place[f"ffn{f}"]
                hi_until(n + 10)
                silu(f, 0, n + 4)
                n += 4
                with act.Fori(0, LOOPS) as i:
                    ffn_step(f, n, 1, i)
                    ffn_step(f, n + 6, 2, i)
                for c in range(1 + 2 * LOOPS, NCH):
                    ffn_step(f, n + 6 * (c - 1), c)
                gT_hi_step(f, NCH - 1)
                done[0] = min(UNITS, n + 6 * NCH)

            def project(pr, dst=None):
                for g in range(len(pr.groups)):
                    hi_until(pr.end(g) + 2)
                    if dst is not None:
                        act.wait_ge(unit_used, pr.end(g))
                        pairs = dst(0, g)
                        for o, i_ in pairs:
                            last = nc.scalar.copy(o, i_)
                        last.then_inc(group_out[0], 1)
                hi_until(pr.unit0 + pr.units + SPLIT)

            def move_chunks(chunks):
                for srcs, dst in chunks:
                    if chunk[0] % 2:
                        act.wait_ge(chunk_psum, chunk[0] + 1)
                        n = len(srcs)
                        rows = srcs[0].shape[1]
                        nc.scalar.copy(dst, CK[1][0:rows, 0:n * P].rearrange("p (b s) -> p b s", b=n))\
                            .then_inc(chunk_out[1], 1)
                    chunk[0] += 1

            def attend(tiles):
                for tl in tiles:
                    a = tile[0]
                    act.wait_ge(max_ready, a + 1)
                    for r in range(tl.rows):
                        w = scb[:, r * tl.width:(r + 1) * tl.width]
                        last = nc.scalar.activation(w, w, ACT.Exp, bias=negmax[:, a % 2, r:r + 1], scale=tl.scale,
                                                    accum_out=den[:, a % 2, r:r + 1])
                    last.then_inc(probs_ready, 1)
                    move_chunks(prob_chunks(tl))
                    tile[0] += 1

            def update_wait(pr):
                return lambda t: (group_out[t], pr.group0 + len(pr.groups))

            squares("norm_ffn1_0_", lambda t: (x_loaded[t], 16))
            hi_until(4)
            T_event("ffn0")
            hi_until(6)
            act.wait_ge(angle_ready, 1)
            nc.scalar.activation(sines[:, :, :, :], angle[:, :, :, :], ACT.Sin).then_inc(sin_ready, 1)
            for l in range(2):
                if l:
                    squares(f"norm_ffn1_{l}_", lambda t: (x_updated, (2 * l - 1) * NT + t + 1))
                    T_event("ffn2")
                ffn(2 * l)
                squares(f"norm_mix_{l}_", lambda t: (x_updated, 2 * l * NT + t + 1))
                mixer_in = place[("even_in", "odd_in")[l]]
                memkv, xq, xo = place[f"memkv{l}"], place[f"xq{l}"], place[f"xo{l}"]
                T_event(mixer_in.name)
                project(mixer_in, lambda t, g, pr=mixer_in: cols_pairs(pr, t, g))
                for t in range(NT):
                    square_rows(f"norm_mem_{l}_{t}", t, kvb[:, t, 0:D], kvb[:, t, D:2 * D], mem_loaded[t], 16 * (l + 1))
                if l == 0:
                    T_event("lora")
                    project(place["uq"], uq_pairs)
                    project(place["ukv"], ukv_pairs)
                T_event(memkv.name)
                project(memkv, lambda t, g, pr=memkv: memkv_pairs(pr, t, g))
                if l == 0:
                    move_chunks(mla_chunks())
                    attend(MLA_TILES)
                    move_chunks(dil_chunks())
                    attend(DIL_TILES)
                else:
                    move_chunks(idx_chunks())
                    for qt in range(NT):
                        keys = P * (qt + 1)
                        act.wait_ge(logits_ready, qt + 1)
                        if qt:
                            act.wait_ge(score_done, qt)
                        nc.scalar.activation(scb[:, 0:IDX_H * keys], low[:, 0:IDX_H * keys], ACT.Relu,
                                             scale=HD ** -0.5).then_inc(relu_done, 1)
                    move_chunks(spa_chunks())
                    attend(SPA_TILES)
                mixer_out = place[("even_out", "odd_out")[l]]
                T_event(mixer_out.name)
                project(mixer_out)
                squares(f"norm_x_{l}_", update_wait(mixer_out))
                T_event(xq.name)
                project(xq, lambda t, g, pr=xq: cols_pairs(pr, t, g))
                move_chunks(x_chunks())
                attend(X_TILES)
                T_event(xo.name)
                project(xo)
                squares(f"norm_ffn2_{l}_", update_wait(xo))
                T_event(f"ffn{2 * l + 1}")
                ffn(2 * l + 1)

        @block.vector
        def _(dve):
            done = [0]
            chunk = [0]
            tile = [0]
            steps = [0]
            row_events = [0]
            rms_events = [0]
            square_events = [0]

            def link(ins):
                steps[0] += 1
                ins.then_inc(dve_step, 1)
                dve.wait_ge(dve_step, steps[0])

            def lo(n, i=None):
                dve.wait_ge(hi_done, val(n + 1, 12, i))
                nc.vector.tensor_tensor(w_lo[:, n % SPLIT, :], raw[:, n % RAW, :],
                                        w_hi[:, n % SPLIT, :].bitcast(F32), ALU.subtract).then_inc(lo_done, 1)

            def lo_until(n):
                while done[0] < min(n, UNITS):
                    lo(done[0])
                    done[0] += 1

            def mean_square(name, width):
                i, c, w = rms[name]
                assert i == rms_events[0], name
                rms_events[0] += 1
                nc.vector.tensor_scalar(meansq[:, c:c + w], sumsq[:, c:c + w], 1.0 / width, EPS, ALU.mult,
                                        ALU.add).then_inc(meansq_done, 1)

            def rstd_of(name):
                i, c, w = rms[name]
                dve.wait_ge(rstd_done, i + 1)
                return rstd[:, c:c + w]

            def norm_rows(name, rows, gains, src, dst):
                for t in range(NT):
                    square_events[0] += 1
                    dve.wait_ge(sumsq_done, square_events[0])
                    mean_square(f"{name}{t}", D)
                dve.wait_ge(gain_loaded, 16 * gains)
                for t in range(NT):
                    nc.vector.scalar_tensor_tensor(out=dst[:, t, 0:D], in0=src[:, t, 0:D], scalar=rstd_of(f"{name}{t}"),
                                                   in1=gain[:, :], op0=ALU.mult, op1=ALU.mult)\
                        .then_inc(rows_ready, 1)

            def T_event(name):
                for c, t, b, nb in T_parts(name):
                    dve.wait_ge(T_hi, c + 1)
                    h = act_hi[:, b:b + nb, t * P:(t + 1) * P]
                    nc.vector.tensor_tensor(act_lo[:, b:b + nb, t * P:(t + 1) * P],
                                            SC[2 * t + b // 4][:, 0:nb * P].rearrange("p (b s) -> p b s", b=nb),
                                            h.bitcast(F32), ALU.subtract).then_inc(T_split, 1)

            def gate(f, c, i=None):
                for t in range(NT):
                    dve.wait_ge(silu_done, val(NT * (NCH * f + c) + t + 1, 2 * NT, i))
                    nc.vector.tensor_tensor(gated[:, t, :], silu_g[:, t, :], SC[t][:, CH:2 * CH], ALU.mult)\
                        .then_inc(gated_done, 1)

            def gT_lo_step(f, c, i=None):
                dve.wait_ge(gT_hi_done, val(NCH * f + c + 1, 2, i))
                nc.vector.tensor_tensor(gT_lo[:, :, :], SC[2].rearrange("p (b s) -> p b s", b=2),
                                        gT_hi[:, :, :].bitcast(F32), ALU.subtract).then_inc(gT_split, 1)

            def ffn_step(f, n, c, i=None):
                gT_lo_step(f, c - 1, i)
                for u in range(6, 10):
                    if n + u < UNITS:
                        lo(n + u, i)
                gate(f, c, i)
                for u in range(10, 12):
                    if n + u < UNITS:
                        lo(n + u, i)

            def ffn(f):
                n = place[f"ffn{f}"]
                lo_until(n + 10)
                gate(f, 0)
                n += 4
                with dve.Fori(0, LOOPS) as i:
                    ffn_step(f, n, 1, i)
                    ffn_step(f, n + 6, 2, i)
                for c in range(1 + 2 * LOOPS, NCH):
                    ffn_step(f, n + 6 * (c - 1), c)
                gT_lo_step(f, NCH - 1)
                done[0] = min(UNITS, n + 6 * NCH)
                for t in range(NT):
                    if t == 0:
                        dve.wait_ge(ffn_sum, f + 1)
                    else:
                        dve.wait_ge(unit_used, place[f"ffn{f}"] + 6 * NCH)
                    for h in range(2):
                        xs = x[:, t, h * 512:(h + 1) * 512]
                        last = nc.vector.scalar_tensor_tensor(out=xs, in0=acc(t, h), scalar=0.5, in1=xs,
                                                              op0=ALU.mult, op1=ALU.add)
                    last.then_inc(x_updated, 1)

            def project(pr, dst):
                for g in range(len(pr.groups)):
                    while done[0] < min(pr.end(g) + 2, UNITS):
                        lo_until(done[0] + 1)
                        yield
                    dve.wait_ge(unit_used, pr.end(g))
                    for o, i_ in dst(1, g):
                        last = nc.vector.tensor_copy(o, i_)
                    last.then_inc(group_out[1], 1)
                    yield
                while done[0] < min(pr.unit0 + pr.units + SPLIT, UNITS):
                    lo_until(done[0] + 1)
                    yield

            def run(steps_):
                for _ in steps_:
                    pass

            def project_update(pr):
                for g in range(len(pr.groups)):
                    lo_until(pr.end(g) + 2)
                    dve.wait_ge(unit_used, pr.end(g))
                    for t in range(NT):
                        xs = x[:, t, g * 512:(g + 1) * 512]
                        nc.vector.tensor_tensor(xs, acc(t, (pr.group0 + g) % 2), xs, ALU.add)\
                            .then_inc(group_out[t], 1)

            def head_squares(name, src, width):
                h = src.shape[1]
                sq = scr_a[:, 0:h * width].rearrange("p (h e) -> p h e", h=h)
                i, c, w = rms[name]
                link(nc.vector.tensor_tensor(sq, src, src, ALU.mult))
                link(nc.vector.tensor_reduce(sumsq[:, c:c + w], sq, AX, ALU.add))
                mean_square(name, width)

            def scale_heads(name, v):
                r = rstd_of(name)
                return nc.vector.tensor_tensor(v, v, r.unsqueeze(2).to_broadcast(list(v.shape)), ALU.mult)

            def rotate(v, c, s):
                shape = list(v.shape)
                e = shape[-1]
                size = int(np.prod(shape[1:]))
                names = {3: "p (a e) -> p a e", 4: "p (a b e) -> p a b e"}[len(shape)]
                kw = {3: dict(a=shape[1]), 4: dict(a=shape[1], b=shape[2] if len(shape) > 3 else 1)}[len(shape)]
                va = scr_a[:, 0:size].rearrange(names, **kw)
                vb = scr_b[:, 0:size].rearrange(names, **kw)
                nc.vector.tensor_tensor(va, v, c, ALU.mult)
                nc.vector.tensor_tensor(vb[..., 0:e // 2], v[..., e // 2:], s[..., 0:e // 2], ALU.mult)
                link(nc.vector.tensor_tensor(vb[..., e // 2:], v[..., 0:e // 2], s[..., e // 2:], ALU.mult))
                link(nc.vector.tensor_tensor(v, va, vb, ALU.add))

            def over_heads(table, h):
                return table.unsqueeze(1).to_broadcast([P, h, table.shape[-1]])

            def move_chunks(chunks):
                for srcs, dst in chunks:
                    if chunk[0] % 2 == 0:
                        dve.wait_ge(chunk_psum, chunk[0] + 1)
                        n = len(srcs)
                        rows = srcs[0].shape[1]
                        nc.vector.tensor_copy(dst, CK[0][0:rows, 0:n * P].rearrange("p (b s) -> p b s", b=n))\
                            .then_inc(chunk_out[0], 1)
                    chunk[0] += 1

            def mask_and_max(tl, a, chunks_before):
                dve.wait_ge(scores_ready, a + 1)
                if chunks_before:
                    dve.wait_ge(chunk_psum, chunks_before)
                n = tl.rows * tl.width
                s = low[:, 0:tl.rows * tl.pitch].rearrange("p (r w) -> p r w", r=tl.rows)[:, :, 0:tl.width]
                o = scb[:, 0:n]
                if tl.kind == "x":
                    nc.vector.tensor_copy(o.rearrange("p (r w) -> p r w", r=tl.rows), s).then_inc(scores_read, 1)
                else:
                    form = dict(r=tl.rows, g=tl.segs)
                    m = {"mla": lambda: causal[:, SEQ - tl.keys:].unsqueeze(1),
                         "dil": lambda: dil_mask[:, :, SEQ - tl.keys:],
                         "spa": lambda: sel_bias[:, tl.qt, 0:tl.keys].unsqueeze(1)}[tl.kind]()
                    m = m.unsqueeze(1).to_broadcast([P, tl.rows, tl.segs, tl.keys])
                    nc.vector.tensor_tensor(o.rearrange("p (r g k) -> p r g k", **form),
                                            s.rearrange("p r (g k) -> p r g k", g=tl.segs), m, ALU.add)\
                        .then_inc(scores_read, 1)
                dve.wait_ge(scores_read, a + 1)
                link(nc.vector.tensor_reduce(rowmax[:, 0:tl.rows], o.rearrange("p (r w) -> p r w", r=tl.rows),
                                             AX, ALU.max))
                nc.vector.tensor_scalar(negmax[:, a % 2, 0:tl.rows], rowmax[:, 0:tl.rows], -tl.scale, None,
                                        ALU.mult).then_inc(max_ready, 1)

            def attend(tiles):
                for tl in tiles:
                    a = tile[0]
                    mask_and_max(tl, a, chunk[0])
                    move_chunks(prob_chunks(tl))
                    dve.wait_ge(probs_ready, a + 1)
                    link(nc.vector.reciprocal(rden[:, 0:tl.rows], den[:, a % 2, 0:tl.rows]))
                    dve.wait_ge(out_ready, a + 1)
                    n = tl.rows * tl.out
                    at = {"mla": 0, "dil": MLA_H * HD + tl.first * HD, "spa": tl.first * HD, "x": 0}[tl.kind]
                    j = 2 if tl.kind == "spa" else 1
                    form = dict(j=j, q=tl.rows // j)
                    r = rden[:, 0:tl.rows].rearrange("p (j q) -> p q j", **form).unsqueeze(3)
                    nc.vector.tensor_tensor(
                        tm[:, tl.qt, at:at + n].rearrange("p (q j e) -> p q j e", **form),
                        OB[:, 0:n].rearrange("p (q j e) -> p q j e", **form),
                        r.to_broadcast([P, tl.rows // j, j, tl.out]), ALU.mult).then_inc(out_read, 1)
                    tile[0] += 1

            def tables():
                dve.wait_ge(consts_made, 5)
                off = pTb[:, 0:SEQ].bitcast(I32)
                for g, dilation in ((1, 4), (2, 16)):
                    rest = scr_a[:, 0:SEQ].bitcast(I32)
                    link(nc.vector.tensor_scalar(rest, off, dilation - 1, None, ALU.bitwise_and))
                    link(nc.vector.tensor_scalar(scr_b[:, 0:SEQ], rest, 0.0, NEG, ALU.is_gt, ALU.mult))
                    link(nc.vector.tensor_tensor(dil_mask[:, g, :], scr_b[:, 0:SEQ], causal[:, :], ALU.add))
                dve.wait_ge(const_loaded, 16 * N_SMALL)
                link(nc.vector.tensor_copy(pos_f[:, :], pos_i[:, :]))
                product = scr_a[:, 0:48 * NT].rearrange("p (t f) -> p t f", t=NT)
                turns = scr_b[:, 0:48 * NT].rearrange("p (t f) -> p t f", t=NT)
                for t in range(NT):
                    ins = nc.vector.tensor_scalar(product[:, t, :], freq[:, :], pos_f[:, t:t + 1], None, ALU.mult)
                link(ins)
                for j, quarter in ((0, 0.25), (1, 0.0)):
                    a = angle[:, j, :, :]
                    link(nc.vector.tensor_scalar(turns, product, 1 / (2 * math.pi), quarter, ALU.mult, ALU.add))
                    link(nc.vector.tensor_scalar(turns, turns, ROUND, None, ALU.add))
                    link(nc.vector.tensor_scalar(turns, turns, ROUND, None, ALU.subtract))
                    link(nc.vector.scalar_tensor_tensor(out=a, in0=turns, scalar=-C1, in1=product,
                                                        op0=ALU.mult, op1=ALU.add))
                    link(nc.vector.scalar_tensor_tensor(out=a, in0=turns, scalar=-C2, in1=a,
                                                        op0=ALU.mult, op1=ALU.add))
                    link(nc.vector.scalar_tensor_tensor(out=a, in0=turns, scalar=-C3, in1=a,
                                                        op0=ALU.mult, op1=ALU.add))
                    if quarter:
                        link(nc.vector.tensor_scalar(a, a, math.pi / 2, None, ALU.add))
                    last = nc.vector.tensor_scalar(a, a, 3.1415925, -3.1415925, ALU.min, ALU.max)
                    if quarter:
                        link(last)
                last.then_inc(angle_ready, 1)
                dve.wait_ge(sin_ready, 1)
                for t in range(NT):
                    cos, sin = sines[:, 0, t, :], sines[:, 1, t, :]
                    for h in range(2):
                        nc.vector.tensor_copy(rc64[:, t, h * 32:(h + 1) * 32], cos[:, 0:32])
                        nc.vector.tensor_scalar(rs64[:, t, h * 32:(h + 1) * 32], sin[:, 0:32], 2.0 * h - 1, None,
                                                ALU.mult)
                        nc.vector.tensor_copy(scr_a[:, h * 16:(h + 1) * 16], cos[:, 32:48])
                        last = nc.vector.tensor_scalar(scr_b[:, h * 16:(h + 1) * 16], sin[:, 32:48], 2.0 * h - 1,
                                                       None, ALU.mult)
                    link(last)
                    for j in range(2):
                        g = head_gain[:, j * ROPE:(j + 1) * ROPE]
                        nc.vector.tensor_tensor(gc32[:, t, j, :], scr_a[:, 0:32], g, ALU.mult)
                        nc.vector.tensor_tensor(gs32[:, t, j, 0:16], scr_b[:, 0:16], g[:, 16:], ALU.mult)
                        nc.vector.tensor_tensor(gs32[:, t, j, 16:], scr_b[:, 16:32], g[:, 0:16], ALU.mult)
                    for j in range(4):
                        g = head_gain[:, 64 + j * HD:64 + (j + 1) * HD]
                        nc.vector.tensor_tensor(gc64[:, t, j, :], rc64[:, t, :], g, ALU.mult)
                        nc.vector.tensor_tensor(gs64[:, t, j, 0:32], rs64[:, t, 0:32], g[:, 32:], ALU.mult)
                        last = nc.vector.tensor_tensor(gs64[:, t, j, 32:], rs64[:, t, 32:], g[:, 0:32], ALU.mult)
                    link(last)

            def heads(v, h):
                return v.rearrange("p (h e) -> p h e", h=h)

            def lora_rows():
                for t in range(NT):
                    for name, at, w in (("lora_q", 0, Q_LORA), ("lora_kv", Q_LORA, KV_LORA)):
                        head_squares(f"{name}{t}", cols[:, t, at:at + w].unsqueeze(1), w)
                for t in range(NT):
                    for name, at, w in (("lora_q", 0, Q_LORA), ("lora_kv", Q_LORA, KV_LORA)):
                        last = nc.vector.scalar_tensor_tensor(out=tm[:, t, at:at + w], in0=cols[:, t, at:at + w],
                                                              scalar=rstd_of(f"{name}{t}"),
                                                              in1=lora_gain[:, at:at + w], op0=ALU.mult, op1=ALU.mult)
                    last.then_inc(rows_ready, 1)

            def mla_heads(pump):
                for t in range(NT):
                    q = heads(q_mla[:, t, :], MLA_H)
                    k = heads(k_mla[:, t, :], MLA_H)
                    kr = cols[:, t, Q_LORA + KV_LORA:DIL0].unsqueeze(1)
                    for name, v, w in ((f"mla_q{t}", q[:, :, 0:HD], HD), (f"mla_qr{t}", q[:, :, HD:], ROPE),
                                       (f"mla_k{t}", k[:, :, 0:HD], HD), (f"mla_kr{t}", kr, ROPE)):
                        head_squares(name, v, w)
                        next(pump, None)
                    rotate(q[:, :, HD:], over_heads(gc32[:, t, 0, :], MLA_H), over_heads(gs32[:, t, 0, :], MLA_H))
                    next(pump, None)
                    rotate(kr, over_heads(gc32[:, t, 1, :], 1), over_heads(gs32[:, t, 1, :], 1))
                    scale_heads(f"mla_q{t}", q[:, :, 0:HD])
                    scale_heads(f"mla_qr{t}", q[:, :, HD:])
                    scale_heads(f"mla_k{t}", k[:, :, 0:HD])
                    link(scale_heads(f"mla_kr{t}", kr))
                    next(pump, None)
                    nc.vector.tensor_tensor(q[:, :, 0:HD], q[:, :, 0:HD], over_heads(nope_gain[:, 0, :], MLA_H),
                                            ALU.mult)
                    nc.vector.tensor_tensor(k[:, :, 0:HD], k[:, :, 0:HD], over_heads(nope_gain[:, 1, :], MLA_H),
                                            ALU.mult)
                    last = nc.vector.tensor_copy(k[:, :, HD:], kr.to_broadcast([P, MLA_H, ROPE]))
                    next(pump, None)
                last.then_inc(heads_ready, 1)

            def dil_heads(pump):
                for t in range(NT):
                    for g in range(3):
                        v = dil_cols(t)[:, g, 0:8, :]
                        name = f"dil{g}_{t}"
                        head_squares(name, v, HD)
                        next(pump, None)
                        v4 = v.rearrange("p (j h) e -> p j h e", j=2)
                        rotate(v4, gc64[:, t, 0:2, :].unsqueeze(2).to_broadcast([P, 2, 4, HD]),
                               gs64[:, t, 0:2, :].unsqueeze(2).to_broadcast([P, 2, 4, HD]))
                        last = scale_heads(name, v)
                        next(pump, None)
                last.then_inc(heads_ready, 1)

            def idx_heads():
                for t in range(NT):
                    qi = heads(cols[:, t, 1152:1664], IDX_H)
                    ki = cols[:, t, 1664:1728].unsqueeze(1)
                    rotate(qi, over_heads(rc64[:, t, :], IDX_H), over_heads(rs64[:, t, :], IDX_H))
                    rotate(ki, over_heads(rc64[:, t, :], 1), over_heads(rs64[:, t, :], 1))
                    nc.vector.tensor_copy(twin[:, t, P:2 * P].rearrange("p (j e) -> p j e", j=2),
                                          ki.to_broadcast([P, 2, HD]))
                    last = nc.vector.tensor_scalar(w_idx[:, t, :], cols[:, t, 1728:1736], IDX_H ** -0.5, None,
                                                   ALU.mult)
                last.then_inc(heads_ready, 1)

            def spa_heads(pump):
                for t in range(NT):
                    for j in range(2):
                        q = heads(cols[:, t, j * 512:(j + 1) * 512], 8)
                        head_squares(f"spa_q{j}_{t}", q, HD)
                        next(pump, None)
                        rotate(q, over_heads(gc64[:, t, 2, :], 8), over_heads(gs64[:, t, 2, :], 8))
                        scale_heads(f"spa_q{j}_{t}", q)
                        next(pump, None)
                    k = cols[:, t, 1024:1088].unsqueeze(1)
                    head_squares(f"spa_k{t}", k, HD)
                    rotate(k, over_heads(gc64[:, t, 3, :], 1), over_heads(gs64[:, t, 3, :], 1))
                    link(scale_heads(f"spa_k{t}", k))
                    last = nc.vector.tensor_copy(twin[:, t, 0:P].rearrange("p (j e) -> p j e", j=2),
                                                 k.to_broadcast([P, 2, HD]))
                    next(pump, None)
                last.then_inc(heads_ready, 1)

            def wide_heads(name, src, j):
                for t in range(NT):
                    v = heads(src[:, t, 0:D], X_H)
                    i, c, w = rms[f"{name}{t}"]
                    for h in range(0, X_H, 2):
                        sq = scr_a[:, :].rearrange("p (h e) -> p h e", h=2)
                        link(nc.vector.tensor_tensor(sq, v[:, h:h + 2, :], v[:, h:h + 2, :], ALU.mult))
                        link(nc.vector.tensor_reduce(sumsq[:, c + h:c + h + 2], sq, AX, ALU.add))
                    mean_square(f"{name}{t}", X_HD)
                for t in range(NT):
                    v = heads(src[:, t, 0:D], X_H)
                    link(scale_heads(f"{name}{t}", v))
                    last = nc.vector.tensor_tensor(v, v, over_heads(x_gain[:, j, :], X_H), ALU.mult)
                return last

            def select_keys():
                for t in range(NT):
                    keys = P * (t + 1)
                    s, l_ = score[:, t, 0:keys], left[:, t, 0:keys]
                    dve.wait_ge(relu_done, t + 1)
                    link(nc.vector.tensor_scalar(s, scb[:, 0:keys], w_idx[:, t, 0:1], 0.0, ALU.mult, ALU.add))
                    for r in range(1, IDX_H):
                        h = half_first(r)
                        ins = nc.vector.scalar_tensor_tensor(out=s, in0=scb[:, r * keys:(r + 1) * keys],
                                                             scalar=w_idx[:, t, h:h + 1], in1=s,
                                                             op0=ALU.mult, op1=ALU.add)
                        if r < IDX_H - 1:
                            link(ins)
                    ins.then_inc(score_done, 1)
                    dve.wait_ge(score_done, t + 1)
                    link(nc.vector.tensor_tensor(s, s, causal[:, SEQ - keys:], ALU.add))
                    for n in range(TOPK // 8):
                        have = s if n == 0 else l_
                        link(nc.vector.max(top8[:, :], have))
                        link(nc.vector.match_replace(l_, top8[:, :], have, TAKEN))
                    link(nc.vector.tensor_scalar(l_, l_, -1e38, NEG, ALU.is_gt, ALU.mult))
                    link(nc.vector.tensor_tensor(sel_bias[:, t, 0:keys], l_, causal[:, SEQ - keys:], ALU.add))

            lo_first = 4
            norm_rows("norm_ffn1_0_", "ffn0", 1, x, tm)
            lo_until(lo_first)
            T_event("ffn0")
            lo_until(6)
            tables()
            for l in range(2):
                if l:
                    norm_rows(f"norm_ffn1_{l}_", "ffn2", 5 * l + 1, x, tm)
                    T_event("ffn2")
                ffn(2 * l)
                dve.wait_ge(x_updated, (2 * l + 1) * NT)
                mixer_in = place[("even_in", "odd_in")[l]]
                mixer_out = place[("even_out", "odd_out")[l]]
                memkv, xq, xo = place[f"memkv{l}"], place[f"xq{l}"], place[f"xo{l}"]
                norm_rows(f"norm_mix_{l}_", mixer_in.name, 5 * l + 2, x, tm)
                T_event(mixer_in.name)
                run(project(mixer_in, lambda t, g: cols_pairs(mixer_in, t, g)))
                dve.wait_ge(group_out[1], mixer_in.group0 + len(mixer_in.groups))
                dve.wait_ge(group_out[0], mixer_in.group0 + len(mixer_in.groups))
                if l == 0:
                    lora_rows()
                    T_event("lora")
                norm_rows(f"norm_mem_{l}_", memkv.name, 5 * l + 3, kvb, kvb)
                if l == 0:
                    run(project(place["uq"], uq_pairs))
                    run(project(place["ukv"], ukv_pairs))
                    dve.wait_ge(group_out[1], place["ukv"].group0 + 2)
                    dve.wait_ge(group_out[0], place["ukv"].group0 + 2)
                T_event(memkv.name)
                pump = project(memkv, lambda t, g, pr=memkv: memkv_pairs(pr, t, g))
                if l == 0:
                    mla_heads(pump)
                    dil_heads(pump)
                else:
                    idx_heads()
                    spa_heads(pump)
                run(pump)
                dve.wait_ge(group_out[0], memkv.group0 + 4)
                dve.wait_ge(group_out[1], memkv.group0 + 4)
                dve.wait_ge(xgain_loaded, 32 * (l + 1))
                link(wide_heads(f"memk{l}_", kvb, 1))
                if l == 0:
                    move_chunks(mla_chunks())
                    attend(MLA_TILES)
                    move_chunks(dil_chunks())
                    attend(DIL_TILES)
                else:
                    move_chunks(idx_chunks())
                    select_keys()
                    move_chunks(spa_chunks())
                    attend(SPA_TILES)
                T_event(mixer_out.name)
                project_update(mixer_out)
                for t in range(NT):
                    dve.wait_ge(group_out[t], mixer_out.group0 + 2)
                norm_rows(f"norm_x_{l}_", xq.name, 5 * l + 4, x, tm)
                T_event(xq.name)
                run(project(xq, lambda t, g: cols_pairs(xq, t, g)))
                for t in range(NT):
                    dve.wait_ge(group_out[t], xq.group0 + 2)
                wide_heads(f"xq{l}_", cols, 0).then_inc(heads_ready, 1)
                move_chunks(x_chunks())
                attend(X_TILES)
                T_event(xo.name)
                project_update(xo)
                for t in range(NT):
                    dve.wait_ge(group_out[t], xo.group0 + 2)
                norm_rows(f"norm_ffn2_{l}_", f"ffn{2 * l + 1}", 5 * l + 5, x, tm)
                T_event(f"ffn{2 * l + 1}")
                ffn(2 * l + 1)
                dve.wait_ge(x_updated, (2 * l + 2) * NT)

        @block.tensor
        def _(pe):
            chunk = [0]
            tile = [0]

            def product(out, lh, ll, rh, rl, start, stop):
                nc.tensor.matmul(out, lh, rh, start=start, stop=False)
                nc.tensor.matmul(out, lh, rl, start=False, stop=False)
                return nc.tensor.matmul(out, ll, rh, start=False, stop=stop)

            def weight_block(n, k, width, pitch=512):
                at = slice(k * pitch, k * pitch + width)
                return w_hi[:, n % SPLIT, at], w_lo[:, n % SPLIT, at]

            def act_block(k, t):
                at = slice(t * P, (t + 1) * P)
                return act_hi[:, k, at], act_lo[:, k, at]

            def T_event(name, src, ready):
                for c, t, b, nb in T_parts(name):
                    if b == 0:
                        pe.wait_ge(*ready(t))
                    for j in range(nb):
                        last = nc.tensor.transpose(SC[2 * t + b // 4][:, j * P:(j + 1) * P],
                                                   src[:, t, (b + j) * P:(b + j + 1) * P], ident[:, :])
                    last.then_inc(T_psum, 1)

            def rows(name):
                return lambda t: (rows_ready, NT * ROWS.index(name) + t + 1)

            def up(f, n, c, i=None):
                if NCH * f + c > 0:
                    pe.wait_ge(gated_done, val(NT * (NCH * f + c), 2 * NT, i))
                for g in range(4):
                    pe.wait_ge(lo_done, val(n + g + 1, 12, i))
                    for k in range(2):
                        for t in range(NT):
                            last = product(SC[t], *act_block(2 * g + k, t), *weight_block(n + g, k, 512),
                                           g + k == 0, g == 3 and k == 1)
                    last.then_inc(unit_used, 1)

            def gate_transposes(f, c, i=None):
                for t in range(NT):
                    pe.wait_ge(gated_done, val(NT * (NCH * f + c) + t + 1, 2 * NT, i))
                    for b in range(2):
                        last = nc.tensor.transpose(SC[2][:, b * SEQ + t * P:b * SEQ + (t + 1) * P],
                                                   gated[:, t, b * P:(b + 1) * P], ident[:, :])
                last.then_inc(gT_psum, 1)

            def down(f, n, c, i=None):
                pe.wait_ge(gT_split, val(NCH * f + c + 1, 2, i))
                for b in range(2):
                    pe.wait_ge(lo_done, val(n + b + 1, 12, i))
                    for t in range(NT):
                        at = slice(t * P, (t + 1) * P)
                        for h in range(2):
                            last = product(acc(t, h), gT_hi[:, b, at], gT_lo[:, b, at],
                                           *weight_block(n + b, h, 512), False, False)
                    last.then_inc(unit_used, 1)

            def down_last(f, n, c):
                pe.wait_ge(gT_split, NCH * f + c + 1)
                pe.wait_ge(lo_done, n + 2)
                for t in range(NT):
                    at = slice(t * P, (t + 1) * P)
                    for b in range(2):
                        for h in range(2):
                            last = product(acc(t, h), gT_hi[:, b, at], gT_lo[:, b, at],
                                           *weight_block(n + b, h, 512), False, b == 1)
                        if t == 1:
                            last.then_inc(unit_used, 1)
                    if t == 0:
                        last.then_inc(ffn_sum, 1)

            def ffn_step(f, n, c, i=None):
                up(f, n, c, i)
                down(f, n + 4, c - 1, i)
                gate_transposes(f, c, i)

            def ffn(f):
                n = place[f"ffn{f}"]
                T_event(f"ffn{f}", tm, rows(f"ffn{f}"))
                for t in range(NT):
                    for h in range(2):
                        for b in range(2):
                            nc.tensor.matmul(acc(t, h)[:, b * SEQ:(b + 1) * SEQ], zeros[:, :],
                                             ident[:, :].bitcast(BF16), start=b == 0, stop=False)
                pe.wait_ge(T_split, T_done(f"ffn{f}"))
                up(f, n, 0)
                gate_transposes(f, 0)
                n += 4
                with pe.Fori(0, LOOPS) as i:
                    ffn_step(f, n, 1, i)
                    ffn_step(f, n + 6, 2, i)
                for c in range(1 + 2 * LOOPS, NCH):
                    ffn_step(f, n + 6 * (c - 1), c)
                down_last(f, n + 6 * (NCH - 1), NCH - 1)

            def project(pr, event, k0=0):
                pe.wait_ge(T_split, T_done(event))
                for g, width in enumerate(pr.groups):
                    G = pr.group0 + g
                    for t in range(NT):
                        if G >= 2:
                            pe.wait_ge(group_out[t], G - 1)
                    if pr.wide:
                        pe.wait_ge(lo_done, pr.unit0 + 1)
                        for t in range(NT):
                            last = product(acc(t, G % 2), *act_block(k0, t), *weight_block(pr.unit0, g, width),
                                           True, True)
                        if g == len(pr.groups) - 1:
                            last.then_inc(unit_used, 1)
                        continue
                    for u in range(pr.upg):
                        n = pr.unit0 + pr.upg * g + u
                        pe.wait_ge(lo_done, n + 1)
                        for k in range(2 * u, 2 * u + 2):
                            for t in range(NT):
                                last = product(acc(t, G % 2)[:, 0:width], *act_block(k0 + k, t),
                                               *weight_block(n, k % 2, width), k == 0, k == pr.kt - 1)
                        last.then_inc(unit_used, 1)

            def transpose_chunks(chunks):
                for srcs, dst in chunks:
                    c = chunk[0]
                    if c >= 2:
                        pe.wait_ge(chunk_out[c % 2], c // 2)
                    for j, s in enumerate(srcs):
                        last = nc.tensor.transpose(CK[c % 2][0:s.shape[1], j * P:(j + 1) * P], s, ident[:, :])
                    last.then_inc(chunk_psum, 1)
                    chunk[0] += 1

            def moved():
                c = chunk[0]
                pe.wait_ge(chunk_out[0], (c + 1) // 2)
                pe.wait_ge(chunk_out[1], c // 2)

            def operands(tl, r, s):
                q = slice(tl.qt * P, (tl.qt + 1) * P)
                h = tl.head(r)
                if tl.kind == "mla":
                    return [(mla_qT[0:MLA_QK, h, q], mla_kT[0:MLA_QK, h, 0:tl.keys])]
                half = slice((h % 2) * HD, (h % 2 + 1) * HD)
                if tl.kind == "dil":
                    return [(dil_qT[half, 2 * s + h // 2, q], dil_kT[half, 2 * s + h // 2, 0:tl.keys])]
                if tl.kind == "spa":
                    return [(spa_qT[half, h // 2, q], spa_kT[half, 0:tl.keys])]
                return [(x_qT[:, 2 * h + j, q], x_kT[:, 2 * h + j, 0:tl.keys]) for j in range(2)]

            def values(tl, r, s, kt):
                h = tl.head(r)
                return {"mla": lambda: v_mla[:, kt, h * HD:(h + 1) * HD],
                        "dil": lambda: dil_cols(kt)[:, s, 8 + h, :],
                        "spa": lambda: cols[:, kt, 1088:1152],
                        "x": lambda: kvb[:, kt, D + h * X_HD:D + (h + 1) * X_HD]}[tl.kind]()

            def scores(tl, a):
                if a:
                    pe.wait_ge(scores_read, a)
                for r in range(tl.rows):
                    for s in range(tl.segs):
                        at = r * tl.pitch + s * tl.keys
                        parts = operands(tl, r, s)
                        for j, (q, k) in enumerate(parts):
                            last = nc.tensor.matmul(low[:, at:at + tl.keys], q, k, start=j == 0,
                                                    stop=j == len(parts) - 1)
                last.then_inc(scores_ready, 1)

            def outputs(tl, a):
                if a:
                    pe.wait_ge(out_read, a)
                moved()
                per = tl.width // P
                for r in range(tl.rows):
                    for j in range(per):
                        b = r * per + j
                        o = (tl.head(r) - tl.first) * tl.out
                        last = nc.tensor.matmul(OB[:, o:o + tl.out], pTb[:, b * P:(b + 1) * P],
                                                values(tl, r, j // (tl.keys // P), j % (tl.keys // P)),
                                                start=j == 0, stop=j == per - 1)
                last.then_inc(out_ready, 1)

            def attend(tiles):
                first = tile[0]
                scores(tiles[0], first)
                for j, tl in enumerate(tiles):
                    if j + 1 < len(tiles):
                        scores(tiles[j + 1], first + j + 1)
                    pe.wait_ge(probs_ready, first + j + 1)
                    transpose_chunks(prob_chunks(tl))
                    outputs(tl, first + j)
                tile[0] = first + len(tiles)

            def groups_read(pr):
                for t in range(NT):
                    pe.wait_ge(group_out[t], pr.group0 + len(pr.groups))

            pe.wait_ge(consts_made, 2)
            for l in range(2):
                ffn(2 * l)
                mixer_in = place[("even_in", "odd_in")[l]]
                mixer_out = place[("even_out", "odd_out")[l]]
                memkv, xq, xo = place[f"memkv{l}"], place[f"xq{l}"], place[f"xo{l}"]
                T_event(mixer_in.name, tm, rows(mixer_in.name))
                project(mixer_in, mixer_in.name)
                if l == 0:
                    T_event("lora", tm, rows("lora"))
                    project(place["uq"], "lora")
                    project(place["ukv"], "lora", 2)
                T_event(memkv.name, kvb, rows(memkv.name))
                project(memkv, memkv.name)
                groups_read(memkv)
                if l == 0:
                    pe.wait_ge(heads_ready, HEADS["mla"])
                    transpose_chunks(mla_chunks())
                    moved()
                    attend(MLA_TILES)
                    pe.wait_ge(heads_ready, HEADS["dil"])
                    transpose_chunks(dil_chunks())
                    moved()
                    attend(DIL_TILES)
                    n_tiles = TILE0["x0"]
                    out_count = [len(MLA_TILES) + 2, len(MLA_TILES) + 4]
                else:
                    pe.wait_ge(heads_ready, HEADS["idx"])
                    transpose_chunks(idx_chunks())
                    moved()
                    for qt in range(NT):
                        keys = P * (qt + 1)
                        if qt:
                            pe.wait_ge(relu_done, qt)
                        for r in range(IDX_H):
                            h = half_first(r)
                            half = slice((h % 2) * HD, (h % 2 + 1) * HD)
                            last = nc.tensor.matmul(low[:, r * keys:(r + 1) * keys],
                                                    idx_qT[half, h // 2, qt * P:(qt + 1) * P], idx_kT[half, 0:keys],
                                                    start=True, stop=True)
                        last.then_inc(logits_ready, 1)
                    pe.wait_ge(heads_ready, HEADS["spa"])
                    transpose_chunks(spa_chunks())
                    moved()
                    pe.wait_ge(relu_done, NT)
                    attend(SPA_TILES)
                    out_count = [TILE0["spa"] + 2, TILE0["spa"] + 4]
                T_event(mixer_out.name, tm, lambda t: (out_read, out_count[t]))
                project(mixer_out, mixer_out.name)
                T_event(xq.name, tm, rows(xq.name))
                project(xq, xq.name)
                groups_read(xq)
                pe.wait_ge(heads_ready, HEADS[f"x{l}"])
                transpose_chunks(x_chunks())
                moved()
                attend(X_TILES)
                T_event(xo.name, tm, lambda t: (out_read, TILE0[f"x{l}"] + t + 1))
                project(xo, xo.name)
                ffn(2 * l + 1)


_F32 = ["mix_norm", "xattn_norm", "mem_norm", "xattn_wq", "xattn_wkv", "xattn_q_gain", "xattn_k_gain", "xattn_wo",
        "even_w_in", "mla_q_lora_norm", "mla_kv_lora_norm", "mla_w_uq", "mla_w_ukv", "mla_q_gain", "mla_k_gain",
        "dil_q_gain", "dil_k_gain", "even_w_out", "odd_w_in", "sparse_q_gain", "sparse_k_gain", "odd_w_out"]


def kernel(**inputs):
    import concourse.bacc as _bacc
    from concourse.bass_utils import run_bass_kernel_spmd as _run

    nc = _bacc.Bacc("TRN2", target_bir_lowering=False, num_devices=1)
    arrays = {}

    def give(name, a):
        a = np.ascontiguousarray(a)
        arrays["in_" + name] = a
        return nc.dram_tensor("in_" + name, a.shape, mybir.dt.from_np(a.dtype), kind="ExternalInput").ap()

    x_in = give("x", np.asarray(inputs["x"])[0])
    mem_in = give("mem", np.asarray(inputs["mem"])[0])
    positions = give("positions", inputs["positions"])
    norms = [give("ffn1_norm", inputs["ffn1_norm"]), give("ffn2_norm", inputs["ffn2_norm"])]
    w13 = [give("ffn1_w13", inputs["ffn1_w13"]), give("ffn2_w13", inputs["ffn2_w13"])]
    w2 = [give("ffn1_w2", inputs["ffn1_w2"]), give("ffn2_w2", inputs["ffn2_w2"])]
    all_w13 = [w13[f % 2][f // 2] for f in range(4)]
    all_w2 = [w2[f % 2][f // 2] for f in range(4)]
    rest = [give(name, inputs[name]) for name in _F32]
    inv = [np.exp(np.float32(-math.log(10000.0)) * np.arange(0, dim, 2, dtype=np.float32) / np.float32(dim))
           for dim in (HD, ROPE)]
    freq = give("rope_frequencies", np.concatenate(inv)[None].astype(np.float32))
    out = nc.dram_tensor("out", (SEQ, D), F32, kind="ExternalOutput").ap()
    build(nc, x_in, mem_in, positions, norms, all_w13, all_w2, *rest, freq, out)
    r = _run(nc, [arrays], core_ids=[0])
    return r.results[0]["out"].reshape(1, SEQ, D)
```

```python
import math
from contextlib import ExitStack

import numpy as np

import concourse.bass as bass
from concourse import mybir

F32 = mybir.dt.float32
F32R = mybir.dt.float32r
BF16 = mybir.dt.bfloat16
I32 = mybir.dt.int32
ALU = mybir.AluOpType
ACT = mybir.ActivationFunctionType
AX = mybir.AxisListType.X

P = 128
D = 1024
SEQ = 256
NT = SEQ // P
KD = D // P
FF = 2816
CH = 256
NCH = FF // CH
EPS = 1e-6
NEG = -1e30
TAKEN = -3e38
HD = 64
Q_LORA, KV_LORA, ROPE = 256, 128, 32
MLA_H, MLA_QK = 8, 96
DIL0 = Q_LORA + KV_LORA + ROPE
EVEN_IN = DIL0 + 2304
SPA_H, IDX_H = 16, 8
ODD_IN = 1736
TOPK = 64
X_H, X_HD = 4, 256
RAW, SPLIT = 6, 6
LOOPS = 4
C1 = 6.28125
C2 = float(np.float32(np.float32((2 * math.pi - C1) * 2 ** 20).astype(np.int64) // 2 ** 6 * 2 ** 6 / 2 ** 20))
C3 = float(np.float32(2 * math.pi - C1 - C2))
ROUND = 12582912.0


class Projection:

    def __init__(self, name, rows, groups, wide=False, tiled=()):
        self.name, self.kt, self.wide, self.tiled = name, rows // P, wide, tiled
        self.groups = [g if len(g) == 4 else (*g, 1, 0) for g in groups]
        self.upg = 1 if wide else (self.kt + 1) // 2
        self.units = 1 if wide else self.upg * len(groups)

    def end(self, g):
        return self.unit0 + (1 if self.wide else self.upg * (g + 1))


def plan_stream():
    def halves(name, rows):
        return Projection(name, rows, [(0, 512), (512, 512)], tiled=(0, 1))

    def memory(name):
        return Projection(name, D, [(512 * g, 512) for g in range(4)], tiled=(0,))

    even_in = [(0, DIL0)] + [(DIL0 + 768 * g, 512) for g in range(3)]
    even_in += [(DIL0 + 512, 512, 2, 768), (DIL0 + 768 * 2 + 512, 256)]
    odd_in = [(1024, 512), (1536, 200), (0, 512), (512, 512)]
    order = ["ffn0",
             Projection("even_in", D, even_in, tiled=(0,)),
             Projection("uq", Q_LORA, [(0, 512), (512, 256)], tiled=(0,)),
             Projection("ukv", KV_LORA, [(0, 512), (512, 512)], wide=True),
             memory("memkv0"), halves("even_out", 768), halves("xq0", D), halves("xo0", D),
             "ffn1", "ffn2",
             Projection("odd_in", D, odd_in, tiled=(0,)),
             memory("memkv1"), halves("odd_out", D), halves("xq1", D), halves("xo1", D),
             "ffn3"]
    unit = group = early = 0
    places, first = {}, {}
    for it in order:
        if isinstance(it, str):
            places[it] = unit
            unit += 6 * NCH
            first[it, 0], first[it, NCH - 1] = early + 1, early + 2
            early += 2
        else:
            for g in it.tiled:
                early += 1
                first[it.name, g] = early
            it.unit0, it.group0 = unit, group
            unit += it.units
            group += len(it.groups)
            places[it.name] = it
    return order, places, unit, first


def plan_rms():
    widths = []
    def both(name, w):
        for t in range(NT):
            widths.append((f"{name}{t}", w))
    for layer in range(2):
        both(f"norm_ffn1_{layer}_", 1)
        both(f"norm_mem_{layer}_", 1)
        both(f"norm_mix_{layer}_", 1)
        if layer == 0:
            for t in range(NT):
                widths += [(f"lora_q{t}", 1), (f"lora_kv{t}", 1)]
            for g in range(3):
                both(f"dil{g}_", 8)
            for t in range(NT):
                widths += [(f"mla_q{t}", 8), (f"mla_qr{t}", 8), (f"mla_k{t}", 8), (f"mla_kr{t}", 1)]
        else:
            both("spa_k", 1)
            both("spa_q0_", 8)
            both("spa_q1_", 8)
        both(f"memk{layer}_", X_H)
        both(f"norm_x_{layer}_", 1)
        both(f"xq{layer}_", X_H)
        both(f"norm_ffn2_{layer}_", 1)
    out, col = {}, 0
    for i, (name, w) in enumerate(widths):
        out[name] = (i, col, w)
        col += w
    return out, col


def half_first(r, n=8):
    return 2 * (r % (n // 2)) + r // (n // 2)


class Tile:

    def __init__(self, kind, qt, rows, segs, keys, first, out, scale):
        self.kind, self.qt, self.rows, self.segs, self.keys = kind, qt, rows, segs, keys
        self.first, self.out, self.scale = first, out, scale
        self.width = segs * keys
        self.blocks = rows * self.width // P
        self.pitch = 512 if kind == "dil" and rows == 2 else self.width

    def head(self, r):
        return self.first + (half_first(r, self.rows) if self.kind == "spa" else r)


def mla_tiles():
    return [Tile("mla", 0, 8, 1, P, 0, HD, MLA_QK ** -0.5)] + \
           [Tile("mla", 1, 4, 1, SEQ, h, HD, MLA_QK ** -0.5) for h in (0, 4)]


def dil_tiles():
    return [Tile("dil", 0, 2, 3, P, h, HD, HD ** -0.5) for h in (0, 2)] + \
           [Tile("dil", 1, 1, 3, SEQ, h, HD, HD ** -0.5) for h in range(4)]


def spa_tiles():
    return [Tile("spa", 0, 8, 1, P, h, HD, HD ** -0.5) for h in (0, 8)] + \
           [Tile("spa", 1, 4, 1, SEQ, h, HD, HD ** -0.5) for h in range(0, SPA_H, 4)]


def x_tiles():
    return [Tile("x", qt, 2, 1, SEQ, h, X_HD, X_HD ** -0.5) for qt in range(NT) for h in (0, 2)]


def build(nc, x_in, mem_in, positions, ffn_norms, ffn_w13, ffn_w2, mix_norm, xattn_norm, mem_norm,
          xattn_wq, xattn_wkv, xattn_q_gain, xattn_k_gain, xattn_wo, even_w_in, q_lora_norm, kv_lora_norm,
          w_uq, w_ukv, mla_q_gain, mla_k_gain, dil_q_gain, dil_k_gain, even_w_out, odd_w_in,
          sparse_q_gain, sparse_k_gain, odd_w_out, rope_freq, y_out):
    order, place, UNITS, FIRST = plan_stream()
    rms, RMS_COLS = plan_rms()
    MLA_TILES, DIL_TILES, SPA_TILES, X_TILES = mla_tiles(), dil_tiles(), spa_tiles(), x_tiles()
    weights = {"even_in": even_w_in[0], "uq": w_uq[0], "ukv": w_ukv[0], "even_out": even_w_out[0],
               "odd_in": odd_w_in[0], "odd_out": odd_w_out[0]}
    for l in range(2):
        weights[f"memkv{l}"], weights[f"xq{l}"], weights[f"xo{l}"] = xattn_wkv[l], xattn_wq[l], xattn_wo[l]

    ctx = ExitStack()
    with ctx:
        def sb(name, shape, dt=F32):
            return ctx.enter_context(nc.sbuf_tensor(name, shape, dt))

        def sem(name):
            return ctx.enter_context(nc.semaphore(name))

        raw = sb("raw", [P, RAW, 1024])
        w_hi = sb("w_hi", [P, SPLIT, 1024], F32R)
        w_lo = sb("w_lo", [P, SPLIT, 1024], F32R)
        act_hi = sb("act_hi", [P, KD, SEQ], F32R)
        act_lo = sb("act_lo", [P, KD, SEQ], F32R)
        x = sb("x", [P, NT, D])
        tm = sb("tm", [P, NT, D])
        kvb = sb("kvb", [P, NT, 2 * D])
        cols = sb("cols", [P, NT, EVEN_IN])
        v_mla = sb("v_mla", [P, NT, MLA_H * HD])
        qkT = sb("qkT", [P, 4096])
        scb = sb("scb", [P, 2048])
        pTb = sb("pTb", [P, 2048])
        gain = sb("gain", [P, D])
        causal = sb("causal", [P, SEQ], BF16)
        dil_mask = sb("dil_mask", [P, 3, SEQ], BF16)
        sel_mask = dil_mask[:, 0:NT, :]
        lora_gain = sb("lora_gain", [P, Q_LORA + KV_LORA])
        nope_gain = sb("nope_gain", [P, 2, HD])
        x_gain = sb("x_gain", [P, 2, X_HD])
        freq = sb("freq", [P, 48])
        pos_i = sb("pos_i", [P, NT], I32)
        pos_f = sb("pos_f", [P, NT])
        rc64 = sb("rc64", [P, NT, HD])
        rs64 = sb("rs64", [P, NT, HD])
        gc64 = sb("gc64", [P, NT, 4, HD])
        gs64 = sb("gs64", [P, NT, 4, HD])
        head_gain = sb("head_gain", [P, 2 * ROPE + 4 * HD])
        gc32 = sb("gc32", [P, NT, 2, ROPE])
        gs32 = sb("gs32", [P, NT, 2, ROPE])
        scr_a = sb("scr_a", [P, 512])
        scr_b = sb("scr_b", [P, 512])
        sumsq = sb("sumsq", [P, RMS_COLS])
        meansq = sumsq
        rstd = sb("rstd", [P, RMS_COLS])
        minus_half = sb("minus_half", [P, 8])
        rowmax = sb("rowmax", [P, 2, 8])
        negmax = sb("negmax", [P, 4, 8])
        den = sb("den", [P, 4, 8])
        rden = sb("rden", [P, 2, 8])
        w_idx = sb("w_idx", [P, NT, IDX_H])
        top8 = sb("top8", [P, 8])
        ident = sb("ident", [P, P])
        ident_b = sb("ident_b", [P, P], BF16)
        zeros = sb("zeros", [P, P], BF16)

        silu_g = cols[:, 0, 0:512].rearrange("p (t f) -> p t f", t=NT)
        gated = cols[:, 0, 512:1024].rearrange("p (t f) -> p t f", t=NT)
        gT_hi = sb("gT_hi", [P, 3, SEQ], F32R)
        gT_lo = sb("gT_lo", [P, 3, SEQ], F32R)
        q_mla = scb[:, 0:1536].rearrange("p (t c) -> p t c", t=NT)
        k_mla = pTb[:, 0:1536].rearrange("p (t c) -> p t c", t=NT)
        mla_qT = qkT[:, 0:2048].rearrange("p (h s) -> p h s", h=8)
        mla_kT = qkT[:, 2048:4096].rearrange("p (h s) -> p h s", h=8)
        dil_qT = qkT[:, 0:1536].rearrange("p (b s) -> p b s", b=6)
        dil_kT = qkT[:, 1536:3072].rearrange("p (b s) -> p b s", b=6)
        spa_qT = qkT[:, 0:2048].rearrange("p (b s) -> p b s", b=8)
        idx_qT = qkT[:, 2048:3072].rearrange("p (b s) -> p b s", b=4)
        spa_kT = qkT[:, 3072:3328]
        idx_kT = qkT[:, 3328:3584]
        x_qT = qkT[:, 0:2048].rearrange("p (b s) -> p b s", b=8)
        x_kT = qkT[:, 2048:4096].rearrange("p (b s) -> p b s", b=8)
        angle = scb[:, 0:192].rearrange("p (j t f) -> p j t f", j=2, t=NT)
        sines = scb[:, 192:384].rearrange("p (j t f) -> p j t f", j=2, t=NT)
        twin = cols[:, :, ODD_IN:ODD_IN + 256]
        score = cols[:, :, ODD_IN + 256:ODD_IN + 512]
        left = cols[:, :, ODD_IN + 512:ODD_IN + 768]

        def relu_of(qt):
            return scb if qt else pTb

        low = ctx.enter_context(nc.psum_tensor("low", [P, 2048], F32))
        SC = [low[:, i * 512:(i + 1) * 512] for i in range(4)]
        high = ctx.enter_context(nc.psum_tensor("high", [P, 2048], F32))
        CK = [high[:, 0:512], high[:, 512:1024]]
        OB = [high[:, 1024:1536], high[:, 1536:2048]]

        def acc(t, n):
            return high[:, (2 * n + t) * 512:(2 * n + t + 1) * 512]

        const_loaded = sem("const_loaded")
        rope_loaded = sem("rope_loaded")
        x_loaded = [sem(f"x_loaded{t}") for t in range(NT)]
        first_gain_loaded = sem("first_gain_loaded")
        gain_loaded = sem("gain_loaded")
        mem_loaded = [sem(f"mem_loaded{t}") for t in range(NT)]
        xgain_loaded = sem("xgain_loaded")
        unit_loaded = [sem(f"unit_loaded{i}") for i in range(RAW)]
        loader_turn = sem("loader_turn")
        hi_done = sem("hi_done")
        lo_done = sem("lo_done")
        unit_used = sem("unit_used")
        silu_done = sem("silu_done")
        gated_done = sem("gated_done")
        gT_psum = sem("gT_psum")
        gT_hi_done = sem("gT_hi_done")
        gT_split = sem("gT_split")
        tile0_done = sem("tile0_done")
        ffn_sum = sem("ffn_sum")
        x_updated = sem("x_updated")
        sumsq_done = sem("sumsq_done")
        meansq_done = sem("meansq_done")
        rstd_done = sem("rstd_done")
        rows_ready = sem("rows_ready")
        T_psum = sem("T_psum")
        T_hi = sem("T_hi")
        T_split = sem("T_split")
        group_out = [sem(f"group_out{t}") for t in range(NT)]
        heads_ready = sem("heads_ready")
        chunk_psum = sem("chunk_psum")
        chunk_out = [sem("chunk_out_dve"), sem("chunk_out_act")]
        scores_ready = sem("scores_ready")
        max_ready = sem("max_ready")
        probs_ready = sem("probs_ready")
        out_ready = sem("out_ready")
        out_read = sem("out_read")
        logits_ready = sem("logits_ready")
        relu_done = sem("relu_done")
        selected = sem("selected")
        pool_step = sem("pool_step")
        consts_made = sem("consts_made")
        angle_ready = sem("angle_ready")
        sin_ready = sem("sin_ready")
        dve_step = sem("dve_step")
        stored = sem("stored")

        NORMS = []
        for l in range(2):
            NORMS += [ffn_norms[0][l:l + 1, :], mem_norm[l:l + 1, :], mix_norm[l:l + 1, :],
                      xattn_norm[l:l + 1, :], ffn_norms[1][l:l + 1, :]]
        X_UPDATES = 4 * NT
        GT_COUNT = NCH + 1
        N_SMALL = 10

        def val(base, per_turn, i):
            return base if i is None else i * per_turn + base

        T_KT = [8, 8, 3, 8, 6, 8, 8, 8, 8, 8, 8, 8, 8, 8, 8]
        ROWS = ["ffn0", "memkv0", "even_in", "lora", "xq0", "ffn1", "ffn2", "memkv1", "odd_in", "xq1", "ffn3"]
        T_NAMES = ["ffn0", "even_in", "lora", "memkv0", "even_out", "xq0", "xo0", "ffn1", "ffn2", "odd_in",
                   "memkv1", "odd_out", "xq1", "xo1", "ffn3"]
        T_first = {}
        n = 0
        for name, kt in zip(T_NAMES, T_KT):
            T_first[name] = (n, kt, T_NAMES.index(name))
            n += NT * (2 if kt > 4 else 1)

        def T_parts(name):
            c, kt, _ = T_first[name]
            for t in range(NT):
                for h in range(2 if kt > 4 else 1):
                    yield c, t, 4 * h, min(4, kt - 4 * h)
                    c += 1

        def T_done(name):
            c, kt, _ = T_first[name]
            return c + NT * (2 if kt > 4 else 1)

        def T_tile(name, t):
            return [part for part in T_parts(name) if part[1] == t]

        def first_group(name):
            return place[name] + 4 if name.startswith("ffn") else place[name].end(0)

        def T_dest(name):
            return (gT_hi, gT_lo) if name == "lora" else (act_hi, act_lo)

        TILE0 = {"mla": 0, "dil": len(MLA_TILES), "x0": len(MLA_TILES) + len(DIL_TILES)}
        TILE0["spa"] = TILE0["x0"] + len(X_TILES)
        TILE0["x1"] = TILE0["spa"] + len(SPA_TILES)

        def mla_chunks():
            for t in range(NT):
                for src, dst in ((q_mla, mla_qT), (k_mla, mla_kT)):
                    for g in (0, 4):
                        yield ([src[:, t, h * MLA_QK:(h + 1) * MLA_QK] for h in range(g, g + 4)],
                               dst[0:MLA_QK, g:g + 4, t * P:(t + 1) * P])

        def dil_cols(t):
            return cols[:, t, DIL0:EVEN_IN].rearrange("p (g h e) -> p g h e", g=3, h=12)

        def dil_chunks():
            for t in range(NT):
                for first, dst in ((0, dil_qT), (256, dil_kT)):
                    for b, n in ((0, 4), (4, 2)):
                        yield ([cols[:, t, DIL0 + (bb // 2) * 768 + first + (bb % 2) * P:][:, 0:P]
                                for bb in range(b, b + n)],
                               dst[:, b:b + n, t * P:(t + 1) * P])

        def idx_chunks():
            for t in range(NT):
                yield ([cols[:, t, 1152 + b * P:1152 + (b + 1) * P] for b in range(4)],
                       idx_qT[:, :, t * P:(t + 1) * P])
            for t in range(NT):
                yield ([twin[:, t, P:2 * P]], idx_kT[:, t * P:(t + 1) * P].unsqueeze(1))

        def spa_chunks():
            for t in range(NT):
                for b in (0, 4):
                    yield ([cols[:, t, bb * P:(bb + 1) * P] for bb in range(b, b + 4)],
                           spa_qT[:, b:b + 4, t * P:(t + 1) * P])
            for t in range(NT):
                yield ([twin[:, t, 0:P]], spa_kT[:, t * P:(t + 1) * P].unsqueeze(1))

        def x_chunks(which):
            src, dst = {"k": (kvb, x_kT), "q": (cols, x_qT)}[which]
            for t in range(NT):
                for b in (0, 4):
                    yield ([src[:, t, bb * P:(bb + 1) * P] for bb in range(b, b + 4)],
                           dst[:, b:b + 4, t * P:(t + 1) * P])

        def prob_chunks(tl, a):
            at = 1024 * (a % 2)
            for j in range(0, tl.blocks, 4):
                n = min(4, tl.blocks - j)
                yield ([scb[:, at + b * P:at + (b + 1) * P] for b in range(j, j + n)],
                       pTb[:, at + j * P:at + (j + n) * P].rearrange("p (b s) -> p b s", b=n))

        def plan_chunks():
            kinds = []

            def heads(chunks):
                kinds.extend(i % 2 for i, _ in enumerate(chunks))

            def probs(tiles):
                for tl in tiles:
                    kinds.extend(0 for _ in prob_chunks(tl, 0))

            heads(mla_chunks()), probs(MLA_TILES), heads(dil_chunks()), probs(DIL_TILES)
            heads(x_chunks("k")), heads(x_chunks("q")), probs(X_TILES)
            heads(idx_chunks()), heads(spa_chunks()), probs(SPA_TILES)
            heads(x_chunks("k")), heads(x_chunks("q")), probs(X_TILES)
            return [(k, kinds[:i + 1].count(k)) for i, k in enumerate(kinds)]

        def sums(pr, t, g):
            return acc(t, (pr.group0 + g) % 2)[:, 0:pr.groups[g][1]]

        def cols_pairs(pr, t, g):
            at, w, pieces, pitch = pr.groups[g]
            if pieces == 1:
                return [(cols[:, t, at:at + w], sums(pr, t, g))]
            w //= pieces
            return [(cols[:, t, at + i * pitch:at + i * pitch + w], sums(pr, t, g)[:, i * w:(i + 1) * w])
                    for i in range(pieces)]

        def uq_pairs(pr, t, g):
            at, w = pr.groups[g][0:2]
            return [(q_mla[:, t, at:at + w], sums(pr, t, g))]

        def ukv_pairs(pr, t, g):
            src = sums(pr, t, g).rearrange("p (h c) -> p h c", h=4)
            k = k_mla[:, t, :].rearrange("p (h c) -> p h c", h=MLA_H)[:, 4 * g:4 * g + 4, 0:HD]
            v = v_mla[:, t, 256 * g:256 * (g + 1)].rearrange("p (h c) -> p h c", h=4)
            return [(k, src[:, :, 0:HD]), (v, src[:, :, HD:])]

        def memkv_pairs(pr, t, g):
            return [(kvb[:, t, g * 512:(g + 1) * 512], sums(pr, t, g))]

        HEADS = {name: i + 1 for i, name in enumerate(("dil", "mla", "xk0", "xq0", "idx", "spa", "xk1", "xq1"))}
        CHUNKS = plan_chunks()

        block = ctx.enter_context(nc.Block())

        @block.sync
        def _(sp):
            def slot_free(n, i=None):
                if n >= RAW or i is not None:
                    sp.wait_ge(lo_done, val(max(1, n - RAW + 1), 12, i))
                    if i is not None:
                        sp.sem_inc(loader_turn, 1)

            def load_w13(l, n, c, g, i=None):
                src = ffn_w13[l].rearrange("(k p) (u f) -> p k u f", p=P, u=2)[:, 2 * g:2 * g + 2, :, :]
                col = val(c * CH, 2 * CH, i)
                dst = raw[:, n % RAW, :].rearrange("p (k u f) -> p k u f", k=2, u=2)
                slot_free(n, i)
                for u in range(2):
                    sp.dma_start(dst[:, :, u, :], src[:, :, u, bass.ds(col, CH)]).then_inc(unit_loaded[n % RAW], 16)

            def load_w2(l, n, c, b, i=None):
                slot_free(n, i)
                row = val(c * CH + b * P, 2 * CH, i)
                for h in range(2):
                    at = slice(h * 512, (h + 1) * 512)
                    sp.dma_start(raw[:, n % RAW, at], ffn_w2[l][bass.ds(row, P), at])\
                        .then_inc(unit_loaded[n % RAW], 16)

            def load_step(l, n, c, i=None):
                for g in range(4):
                    load_w13(l, n + g, c, g, i)
                for b in range(2):
                    load_w2(l, n + 4 + b, c - 1, b, i)

            def load_ffn(f):
                n = place[f"ffn{f}"]
                for g in range(4):
                    load_w13(f, n + g, 0, g)
                n += 4
                with sp.Fori(0, LOOPS) as i:
                    load_step(f, n, 1, i)
                    load_step(f, n + 6, 2, i)
                for c in range(1 + 2 * LOOPS, NCH):
                    load_step(f, n + 6 * (c - 1), c)
                for b in range(2):
                    load_w2(f, n + 6 * (NCH - 1) + b, NCH - 1, b)

            def load_projection(pr):
                w = weights[pr.name].rearrange("(k p) n -> p k n", p=P)
                n = pr.unit0
                if pr.wide:
                    slot_free(n)
                    for h in range(2):
                        at = slice(h * 512, (h + 1) * 512)
                        sp.dma_start(raw[:, n % RAW, at], w[:, 0, at]).then_inc(unit_loaded[n % RAW], 16)
                    return
                for at, width, pieces, pitch in pr.groups:
                    for u in range(pr.upg):
                        slot_free(n)
                        for k in range(2):
                            dst = raw[:, n % RAW, k * 512:k * 512 + width]
                            src = w[:, 2 * u + k, at:at + width]
                            if pieces > 1:
                                dst = dst.rearrange("p (i c) -> p i c", i=pieces)
                                src = w[:, 2 * u + k, at:at + pitch * pieces]\
                                    .rearrange("p (i c) -> p i c", i=pieces)[:, :, 0:width // pieces]
                            sp.dma_start(dst, src).then_inc(unit_loaded[n % RAW], 16)
                        n += 1

            for it in order:
                if isinstance(it, str):
                    load_ffn(int(it[3:]))
                else:
                    load_projection(it)
            for t in range(NT):
                sp.wait_ge(x_updated, X_UPDATES - NT + t + 1)
                sp.dma_start(y_out[t * P:(t + 1) * P, :], x[:, t, :]).then_inc(stored, 16)
            sp.wait_ge(stored, 16 * NT)

        @block.gpsimd
        def _(pool):
            nc.gpsimd.memset(minus_half[:, :], -0.5).then_inc(pool_step, 1)
            nc.gpsimd.memset(ident[:, :], 0.0).then_inc(pool_step, 1)
            nc.gpsimd.memset(causal[:, :], 0.0).then_inc(pool_step, 1)
            pool.wait_ge(pool_step, 3)
            nc.gpsimd.affine_select(out=ident[:, :], in_=ident[:, :], compare_op=ALU.not_equal, fill=1.0,
                                    base=0, pattern=[[-1, P]], channel_multiplier=1).then_inc(consts_made, 1)
            nc.gpsimd.memset(zeros[:, :], 0.0).then_inc(consts_made, 1)
            nc.gpsimd.memset(ident_b[:, :], 0.0).then_inc(pool_step, 1)
            nc.gpsimd.affine_select(out=causal[:, :], in_=causal[:, :], compare_op=ALU.is_ge, fill=NEG,
                                    base=P, pattern=[[-1, SEQ]], channel_multiplier=1).then_inc(consts_made, 1)
            nc.gpsimd.iota(pTb[:, 0:SEQ].bitcast(I32), pattern=[[-1, SEQ]], base=SEQ,
                           channel_multiplier=1).then_inc(consts_made, 1)
            pool.wait_ge(pool_step, 4)
            nc.gpsimd.affine_select(out=ident_b[:, :], in_=ident_b[:, :], compare_op=ALU.not_equal, fill=1.0,
                                    base=0, pattern=[[-1, P]], channel_multiplier=1).then_inc(pool_step, 1)
            pool.wait_ge(consts_made, 4)
            nc.gpsimd.affine_select(out=dil_mask[:, 0, :], in_=causal[:, :], compare_op=ALU.is_ge, fill=NEG,
                                    base=0, pattern=[[1, SEQ]], channel_multiplier=-1).then_inc(consts_made, 1)
            def serve(*names):
                for name in names:
                    i, c, w = rms[name]
                    pool.wait_ge(meansq_done, i + 1)
                    nc.gpsimd.tensor_tensor(rstd[:, c:c + w], meansq[:, c:c + w], minus_half[:, 0:w],
                                            ALU.pow).then_inc(rstd_done, 1)

            def both(name):
                return [f"{name}{t}" for t in range(NT)]

            def next_gain(n, name):
                pool.wait_ge(rows_ready, NT * (ROWS.index(name) + 1))
                pool.dma_start(gain[:, :], NORMS[n].to_broadcast([P, D])).then_inc(gain_loaded, 16)

            serve(*both("norm_ffn1_0_"))
            small = [(lora_gain[:, 0:Q_LORA], q_lora_norm.to_broadcast([P, Q_LORA])),
                      (lora_gain[:, Q_LORA:], kv_lora_norm.to_broadcast([P, KV_LORA])),
                      (nope_gain[:, 0, :], mla_q_gain[:, 0:HD].to_broadcast([P, HD])),
                      (nope_gain[:, 1, :], mla_k_gain[:, 0:HD].to_broadcast([P, HD])),
                      (head_gain[:, 0:ROPE], mla_q_gain[:, HD:].to_broadcast([P, ROPE])),
                      (head_gain[:, ROPE:2 * ROPE], mla_k_gain[:, HD:].to_broadcast([P, ROPE]))]
            small += [(head_gain[:, 64 + i * HD:64 + (i + 1) * HD], g.to_broadcast([P, HD]))
                      for i, g in enumerate((dil_q_gain, dil_k_gain, sparse_q_gain, sparse_k_gain))]
            assert len(small) == N_SMALL
            for dst, src in small:
                pool.dma_start(dst, src).then_inc(const_loaded, 16)

            for l in range(2):
                if l:
                    pool.wait_ge(out_read, TILE0["x0"] + len(X_TILES))
                for t in range(NT):
                    pool.dma_start(kvb[:, t, 0:D], mem_in[t * P:(t + 1) * P, :]).then_inc(mem_loaded[t], 16)
                pool.dma_start(x_gain[:, 0, :], xattn_q_gain[l:l + 1, :].to_broadcast([P, X_HD]))\
                    .then_inc(xgain_loaded, 16)
                pool.dma_start(x_gain[:, 1, :], xattn_k_gain[l:l + 1, :].to_broadcast([P, X_HD]))\
                    .then_inc(xgain_loaded, 16)
                if l:
                    serve(*both(f"norm_ffn1_{l}_"))
                next_gain(5 * l + 1, f"ffn{2 * l}")
                serve(*both(f"norm_mem_{l}_"))
                next_gain(5 * l + 2, f"memkv{l}")
                serve(*both(f"norm_mix_{l}_"))
                next_gain(5 * l + 3, ("even_in", "odd_in")[l])
                if l == 0:
                    for t in range(NT):
                        serve(f"lora_q{t}", f"lora_kv{t}")
                    serve(*[f"dil{g}_{t}" for g in range(3) for t in range(NT)])
                    for t in range(NT):
                        serve(f"mla_q{t}", f"mla_qr{t}", f"mla_k{t}", f"mla_kr{t}")
                else:
                    serve(*both("spa_k"), *both("spa_q0_"), *both("spa_q1_"))
                serve(*both(f"memk{l}_"))
                serve(*both(f"norm_x_{l}_"))
                next_gain(5 * l + 4, f"xq{l}")
                serve(*both(f"xq{l}_"))
                serve(*both(f"norm_ffn2_{l}_"))
                if l == 0:
                    next_gain(5, "ffn1")

        @block.scalar
        def _(act):
            done = [0]
            chunk = [0]
            tile = [0]
            ends = [0, 0]

            def hi(n, i=None):
                act.wait_ge(unit_loaded[n % RAW], val(32 * (n // RAW + 1), 32 * 12 // RAW, i))
                if n >= SPLIT:
                    act.wait_ge(unit_used, val(n - SPLIT + 1, 12, i))
                nc.scalar.copy(w_hi[:, n % SPLIT, :], raw[:, n % RAW, :]).then_inc(hi_done, 1)

            def hi_until(n):
                while done[0] < min(n, UNITS):
                    hi(done[0])
                    done[0] += 1

            def square(name, src, junk, sem_, count):
                act.wait_ge(sem_, count)
                c = rms[name][1]
                nc.scalar.activation(junk, src, ACT.Square, accum_out=sumsq[:, c:c + 1]).then_inc(sumsq_done, 1)

            def square_heads(name, t, src, heads_, first):
                c = rms[f"{name}{t}"][1] + first
                for h in range(heads_):
                    last = nc.scalar.activation(tm[:, t, (first + h) * X_HD:(first + h + 1) * X_HD], src[:, h * X_HD:(h + 1) * X_HD], ACT.Square,
                                                accum_out=sumsq[:, c + h:c + h + 1])
                last.then_inc(sumsq_done, 1)

            def T_hi_tile(name, t):
                hi_, _ = T_dest(name)
                for c, t, b, nb in T_tile(name, t):
                    act.wait_ge(T_psum, c + 1)
                    nc.scalar.copy(hi_[:, b:b + nb, t * P:(t + 1) * P],
                                   SC[2 * t + b // 4][:, 0:nb * P].rearrange("p (b s) -> p b s", b=nb))\
                        .then_inc(T_hi, 1)

            def T_event(name):
                for t in range(NT):
                    T_hi_tile(name, t)

            def norm(rms_name, name, wait):
                for t in range(NT):
                    square(f"{rms_name}{t}", x[:, t, :], tm[:, t, :], *wait(t))
                    T_hi_tile(name, t)
                    if t == 0:
                        hi_until(first_group(name))

            def silu(f, c, used, i=None):
                for t in range(NT):
                    if t == 0 and i is None and (f"ffn{f}", c) in FIRST:
                        act.wait_ge(tile0_done, FIRST[f"ffn{f}", c])
                    else:
                        act.wait_ge(unit_used, val(used, 12, i))
                    nc.scalar.activation(silu_g[:, t, :], SC[t][:, 0:CH], ACT.Silu).then_inc(silu_done, 1)

            def gT_hi_step(f, c, i=None):
                act.wait_ge(gT_psum, val(GT_COUNT * f + c + 1, 2, i))
                nc.scalar.copy(gT_hi[:, 0:2, :], SC[2].rearrange("p (b s) -> p b s", b=2)).then_inc(gT_hi_done, 1)

            def gT_hi_last(f):
                for t in range(NT):
                    act.wait_ge(gT_psum, GT_COUNT * f + NCH + t)
                    nc.scalar.copy(act_hi[:, 0:2, t * P:(t + 1) * P],
                                   SC[2 + t][:, 0:2 * P].rearrange("p (b s) -> p b s", b=2)).then_inc(gT_hi_done, 1)

            def ffn_step(f, n, c, i=None):
                gT_hi_step(f, c - 1, i)
                for u in range(6, 10):
                    if n + u < UNITS:
                        hi(n + u, i)
                silu(f, c, n + 4, i)
                if c == NCH - 1:
                    gT_hi_last(f)
                for u in range(10, 12):
                    if n + u < UNITS:
                        hi(n + u, i)

            def ffn(f):
                n = place[f"ffn{f}"]
                hi_until(n + 6)
                silu_first = FIRST[f"ffn{f}", 0]
                act.wait_ge(tile0_done, silu_first)
                hi_until(n + 10)
                silu(f, 0, n + 4)
                if f % 2 == 0:
                    for t in range(NT):
                        square(f"norm_mem_{f // 2}_{t}", kvb[:, t, 0:D], kvb[:, t, D:2 * D], mem_loaded[t],
                               16 * (f // 2 + 1))
                n += 4
                with act.Fori(0, LOOPS) as i:
                    ffn_step(f, n, 1, i)
                    ffn_step(f, n + 6, 2, i)
                for c in range(1 + 2 * LOOPS, NCH):
                    ffn_step(f, n + 6 * (c - 1), c)
                done[0] = min(UNITS, n + 6 * NCH)

            def project(pr, dst=None, after=None):
                for g in range(len(pr.groups)):
                    hi_until(pr.end(g) + 2)
                    for t in range(NT):
                        if dst is None:
                            continue
                        if t == 0 and g in pr.tiled:
                            act.wait_ge(tile0_done, FIRST[pr.name, g])
                        else:
                            act.wait_ge(unit_used, pr.end(g))
                        for o, i_ in dst(pr, t, g):
                            last = nc.scalar.copy(o, i_)
                        last.then_inc(group_out[t], 1)
                        if after is not None:
                            act.wait_ge(group_out[t], pr.group0 + g + 1)
                            after(g, t)
                hi_until(pr.end(len(pr.groups) - 1) + SPLIT - (pr.upg if dst is None else 0))

            def move_chunks(chunks):
                for srcs, dst in chunks:
                    c = chunk[0]
                    if CHUNKS[c][0] == 1:
                        act.wait_ge(chunk_psum, c + 1)
                        n, rows = len(srcs), srcs[0].shape[1]
                        nc.scalar.copy(dst, CK[c % 2][0:rows, 0:n * P].rearrange("p (b s) -> p b s", b=n))\
                            .then_inc(chunk_out[1], 1)
                    chunk[0] += 1

            def attend(tiles):
                for tl in tiles:
                    a = tile[0]
                    act.wait_ge(max_ready, a + 1)
                    if ends[0]:
                        act.wait_ge(chunk_psum, ends[0])
                    ends[0], ends[1] = ends[1], chunk[0] + sum(1 for _ in prob_chunks(tl, a))
                    for r in range(tl.rows):
                        at = 1024 * (a % 2) + r * tl.width
                        s = 1024 * (a % 2) + r * tl.pitch
                        last = nc.scalar.activation(scb[:, at:at + tl.width], low[:, s:s + tl.width], ACT.Exp,
                                                    bias=negmax[:, a % 4, r:r + 1], scale=tl.scale,
                                                    accum_out=den[:, a % 4, r:r + 1])
                    last.then_inc(probs_ready, 1)
                    move_chunks(prob_chunks(tl, a))
                    tile[0] += 1

            def update_wait(pr):
                return lambda t: (group_out[t], pr.group0 + len(pr.groups))

            for t in range(NT):
                act.dma_start(x[:, t, :], x_in[t * P:(t + 1) * P, :]).then_inc(x_loaded[t], 16)
            act.dma_start(gain[:, :], NORMS[0].to_broadcast([P, D])).then_inc(first_gain_loaded, 16)
            for t in range(NT):
                act.dma_start(pos_i[:, t:t + 1], positions[0:1, t * P:(t + 1) * P].rearrange("o p -> p o"))\
                    .then_inc(rope_loaded, 16)
            act.dma_start(freq[:, :], rope_freq[0:1, :].to_broadcast([P, 48])).then_inc(rope_loaded, 16)
            for t in range(NT):
                square(f"norm_ffn1_0_{t}", x[:, t, :], tm[:, t, :], x_loaded[t], 16)
            hi_until(4)
            T_event("ffn0")
            act.wait_ge(angle_ready, 1)
            nc.scalar.activation(sines[:, :, :, :], angle[:, :, :, :], ACT.Sin).then_inc(sin_ready, 1)
            for l in range(2):
                if l:
                    norm(f"norm_ffn1_{l}_", "ffn2", lambda t: (x_updated, (2 * l - 1) * NT + t + 1))
                ffn(2 * l)
                mixer_in = place[("even_in", "odd_in")[l]]
                mixer_out = place[("even_out", "odd_out")[l]]
                memkv, xq, xo = place[f"memkv{l}"], place[f"xq{l}"], place[f"xo{l}"]
                norm(f"norm_mix_{l}_", mixer_in.name, lambda t: (x_updated, 2 * l * NT + t + 1))
                project(mixer_in, cols_pairs)
                if l == 0:
                    T_event("lora")
                    project(place["uq"], uq_pairs)
                    project(place["ukv"], ukv_pairs)
                else:
                    move_chunks(idx_chunks())
                    for qt in range(NT):
                        keys = P * (qt + 1)
                        act.wait_ge(logits_ready, qt + 1)
                        nc.scalar.activation(relu_of(qt)[:, 0:IDX_H * keys], low[:, 0:IDX_H * keys], ACT.Relu,
                                             scale=HD ** -0.5).then_inc(relu_done, 1)
                T_event(memkv.name)
                project(memkv, memkv_pairs)
                for t in range(NT):
                    act.wait_ge(group_out[t], memkv.group0 + 4)
                    square_heads(f"memk{l}_", t, kvb[:, t, 0:D], X_H, 0)
                if l == 0:
                    move_chunks(mla_chunks())
                    attend(MLA_TILES)
                    move_chunks(dil_chunks())
                    attend(DIL_TILES)
                else:
                    move_chunks(spa_chunks())
                    attend(SPA_TILES)
                T_event(mixer_out.name)
                project(mixer_out)
                norm(f"norm_x_{l}_", xq.name, update_wait(mixer_out))
                project(xq, cols_pairs, after=lambda g, t: square_heads(
                    f"xq{l}_", t, cols[:, t, g * 512:(g + 1) * 512], 2, 2 * g))
                move_chunks(x_chunks("k"))
                move_chunks(x_chunks("q"))
                attend(X_TILES)
                T_event(xo.name)
                project(xo)
                norm(f"norm_ffn2_{l}_", f"ffn{2 * l + 1}", update_wait(xo))
                ffn(2 * l + 1)

        @block.vector
        def _(dve):
            done = [0]
            chunk = [0]
            tile = [0]
            steps = [0]
            row_events = [0]
            rms_events = [0]
            square_events = [0]

            def link(ins):
                steps[0] += 1
                ins.then_inc(dve_step, 1)
                dve.wait_ge(dve_step, steps[0])

            def lo(n, i=None):
                dve.wait_ge(hi_done, val(n + 1, 12, i))
                nc.vector.tensor_tensor(w_lo[:, n % SPLIT, :], raw[:, n % RAW, :],
                                        w_hi[:, n % SPLIT, :].bitcast(F32), ALU.subtract).then_inc(lo_done, 1)

            def lo_until(n):
                while done[0] < min(n, UNITS):
                    lo(done[0])
                    done[0] += 1

            def mean_square(name, width):
                i, c, w = rms[name]
                assert i == rms_events[0], name
                rms_events[0] += 1
                nc.vector.tensor_scalar(meansq[:, c:c + w], sumsq[:, c:c + w], 1.0 / width, EPS, ALU.mult,
                                        ALU.add).then_inc(meansq_done, 1)

            def rstd_of(name):
                i, c, w = rms[name]
                dve.wait_ge(rstd_done, i + 1)
                return rstd[:, c:c + w]

            def row_mean(name, t):
                square_events[0] += 1
                dve.wait_ge(sumsq_done, square_events[0])
                mean_square(f"{name}{t}", D)

            def norm_row(name, t, gains, src, dst):
                if gains == 1:
                    dve.wait_ge(first_gain_loaded, 16)
                else:
                    dve.wait_ge(gain_loaded, 16 * (gains - 1))
                nc.vector.scalar_tensor_tensor(out=dst[:, t, 0:D], in0=src[:, t, 0:D], scalar=rstd_of(f"{name}{t}"),
                                               in1=gain[:, :], op0=ALU.mult, op1=ALU.mult).then_inc(rows_ready, 1)

            def T_lo_tile(name, t):
                hi_, lo_ = T_dest(name)
                for c, t, b, nb in T_tile(name, t):
                    dve.wait_ge(T_hi, c + 1)
                    at = slice(t * P, (t + 1) * P)
                    nc.vector.tensor_tensor(lo_[:, b:b + nb, at],
                                            SC[2 * t + b // 4][:, 0:nb * P].rearrange("p (b s) -> p b s", b=nb),
                                            hi_[:, b:b + nb, at].bitcast(F32), ALU.subtract).then_inc(T_split, 1)

            def T_event(name):
                for t in range(NT):
                    T_lo_tile(name, t)

            def norm(rms_name, name, gains, update, updated):
                update(0)
                row_mean(rms_name, 0)
                dve.wait_ge(*updated(0))
                norm_row(rms_name, 0, gains, x, tm)
                update(1)
                T_lo_tile(name, 0)
                lo_until(first_group(name))
                row_mean(rms_name, 1)
                dve.wait_ge(*updated(1))
                norm_row(rms_name, 1, gains, x, tm)
                T_lo_tile(name, 1)

            def gate(f, c, i=None):
                for t in range(NT):
                    dve.wait_ge(silu_done, val(NT * (NCH * f + c) + t + 1, 2 * NT, i))
                    nc.vector.tensor_tensor(gated[:, t, :], silu_g[:, t, :], SC[t][:, CH:2 * CH], ALU.mult)\
                        .then_inc(gated_done, 1)

            def gT_lo_step(f, c, i=None):
                dve.wait_ge(gT_hi_done, val(GT_COUNT * f + c + 1, 2, i))
                nc.vector.tensor_tensor(gT_lo[:, 0:2, :], SC[2].rearrange("p (b s) -> p b s", b=2),
                                        gT_hi[:, 0:2, :].bitcast(F32), ALU.subtract).then_inc(gT_split, 1)

            def gT_lo_last(f):
                for t in range(NT):
                    dve.wait_ge(gT_hi_done, GT_COUNT * f + NCH + t)
                    at = slice(t * P, (t + 1) * P)
                    nc.vector.tensor_tensor(act_lo[:, 0:2, at],
                                            SC[2 + t][:, 0:2 * P].rearrange("p (b s) -> p b s", b=2),
                                            act_hi[:, 0:2, at].bitcast(F32), ALU.subtract).then_inc(gT_split, 1)

            def ffn_step(f, n, c, i=None):
                gT_lo_step(f, c - 1, i)
                for u in range(6, 10):
                    if n + u < UNITS:
                        lo(n + u, i)
                gate(f, c, i)
                if c == NCH - 1:
                    gT_lo_last(f)
                for u in range(10, 12):
                    if n + u < UNITS:
                        lo(n + u, i)

            def ffn(f):
                n = place[f"ffn{f}"]
                lo_until(n + 10)
                gate(f, 0)
                if f % 2 == 0:
                    for t in range(NT):
                        row_mean(f"norm_mem_{f // 2}_", t)
                    for t in range(NT):
                        norm_row(f"norm_mem_{f // 2}_", t, 5 * (f // 2) + 2, kvb, kvb)
                n += 4
                with dve.Fori(0, LOOPS) as i:
                    ffn_step(f, n, 1, i)
                    ffn_step(f, n + 6, 2, i)
                for c in range(1 + 2 * LOOPS, NCH):
                    ffn_step(f, n + 6 * (c - 1), c)
                    if f == 0 and c == NCH - 2:
                        rope_tables()
                done[0] = min(UNITS, n + 6 * NCH)

            def ffn_update(f):
                def update(t):
                    if t == 0:
                        dve.wait_ge(ffn_sum, f + 1)
                    else:
                        dve.wait_ge(unit_used, place[f"ffn{f}"] + 6 * NCH)
                    for h in range(2):
                        xs = x[:, t, h * 512:(h + 1) * 512]
                        last = nc.vector.scalar_tensor_tensor(out=xs, in0=acc(t, h), scalar=0.5, in1=xs,
                                                              op0=ALU.mult, op1=ALU.add)
                    last.then_inc(x_updated, 1)
                return update

            def project_lo(limit):
                while done[0] < min(limit, UNITS):
                    lo_until(done[0] + 1)
                    yield

            def lo_of(pr):
                return project_lo(pr.end(len(pr.groups) - 1) + SPLIT)

            def run(steps_):
                for _ in steps_:
                    pass

            def half_update(pr, g, t):
                if t == 0:
                    dve.wait_ge(tile0_done, FIRST[pr.name, g])
                else:
                    dve.wait_ge(unit_used, pr.end(g))
                xs = x[:, t, g * 512:(g + 1) * 512]
                nc.vector.tensor_tensor(xs, sums(pr, t, g), xs, ALU.add).then_inc(group_out[t], 1)

            def project_update(pr):
                lo_until(pr.end(0) + 2)
                half_update(pr, 0, 0)
                lo_until(pr.end(0) + 3)
                half_update(pr, 0, 1)
                lo_until(pr.end(1))

                def update(t):
                    half_update(pr, 1, t)
                    if t == 0:
                        lo_until(pr.end(1) + 2)
                return update

            def update_wait(pr):
                return lambda t: (group_out[t], pr.group0 + len(pr.groups))

            def groups_out(pr, g):
                for t in range(NT):
                    dve.wait_ge(group_out[t], pr.group0 + g + 1)

            def head_squares(name, src, width):
                h = src.shape[1]
                sq = scr_a[:, 0:h * width].rearrange("p (h e) -> p h e", h=h)
                i, c, w = rms[name]
                link(nc.vector.tensor_tensor(sq, src, src, ALU.mult))
                link(nc.vector.tensor_reduce(sumsq[:, c:c + w], sq, AX, ALU.add))
                mean_square(name, width)

            def scale_heads(name, v):
                r = rstd_of(name)
                return nc.vector.tensor_tensor(v, v, r.unsqueeze(2).to_broadcast(list(v.shape)), ALU.mult)

            def rotate(v, c, s):
                shape = list(v.shape)
                e = shape[-1]
                size = int(np.prod(shape[1:]))
                names = {3: "p (a e) -> p a e", 4: "p (a b e) -> p a b e"}[len(shape)]
                kw = {3: dict(a=shape[1]), 4: dict(a=shape[1], b=shape[2] if len(shape) > 3 else 1)}[len(shape)]
                va = scr_a[:, 0:size].rearrange(names, **kw)
                vb = scr_b[:, 0:size].rearrange(names, **kw)
                nc.vector.tensor_tensor(va, v, c, ALU.mult)
                nc.vector.tensor_tensor(vb[..., 0:e // 2], v[..., e // 2:], s[..., 0:e // 2], ALU.mult)
                link(nc.vector.tensor_tensor(vb[..., e // 2:], v[..., 0:e // 2], s[..., e // 2:], ALU.mult))
                link(nc.vector.tensor_tensor(v, va, vb, ALU.add))

            def over_heads(table, h):
                return table.unsqueeze(1).to_broadcast([P, h, table.shape[-1]])

            def move_chunks(chunks):
                for srcs, dst in chunks:
                    c = chunk[0]
                    if CHUNKS[c][0] == 0:
                        dve.wait_ge(chunk_psum, c + 1)
                        n, rows = len(srcs), srcs[0].shape[1]
                        nc.vector.tensor_copy(dst, CK[c % 2][0:rows, 0:n * P].rearrange("p (b s) -> p b s", b=n))\
                            .then_inc(chunk_out[0], 1)
                    chunk[0] += 1

            def row_max(tl, a):
                dve.wait_ge(scores_ready, a + 1)
                s = low[:, 1024 * (a % 2):1024 * (a % 2) + tl.rows * tl.pitch]
                link(nc.vector.tensor_reduce(rowmax[:, a % 2, 0:tl.rows],
                                             s.rearrange("p (r w) -> p r w", r=tl.rows)[:, :, 0:tl.width],
                                             AX, ALU.max))
                nc.vector.tensor_scalar(negmax[:, a % 4, 0:tl.rows], rowmax[:, a % 2, 0:tl.rows], -tl.scale, None,
                                        ALU.mult).then_inc(max_ready, 1)

            def attend(tiles):
                first = tile[0]
                row_max(tiles[0], first)
                row_max(tiles[1], first + 1)
                for j, tl in enumerate(tiles):
                    a = first + j
                    move_chunks(prob_chunks(tl, a))
                    if j + 2 < len(tiles):
                        row_max(tiles[j + 2], a + 2)
                    dve.wait_ge(probs_ready, a + 1)
                    link(nc.vector.reciprocal(rden[:, a % 2, 0:tl.rows], den[:, a % 4, 0:tl.rows]))
                    dve.wait_ge(out_ready, a + 1)
                    n = tl.rows * tl.out
                    at = (MLA_H * HD if tl.kind == "dil" else 0) + tl.first * tl.out
                    two = 2 if tl.kind == "spa" else 1
                    form = dict(j=two, q=tl.rows // two)
                    r = rden[:, a % 2, 0:tl.rows].rearrange("p (j q) -> p q j", **form).unsqueeze(3)
                    nc.vector.tensor_tensor(
                        tm[:, tl.qt, at:at + n].rearrange("p (q j e) -> p q j e", **form),
                        OB[a % 2][:, 0:n].rearrange("p (q j e) -> p q j e", **form),
                        r.to_broadcast([P, tl.rows // two, two, tl.out]), ALU.mult).then_inc(out_read, 1)
                tile[0] = first + len(tiles)

            def dilated_masks():
                dve.wait_ge(consts_made, 5)
                off = pTb[:, 0:SEQ].bitcast(I32)
                for g, dilation in ((1, 4), (2, 16)):
                    rest = scr_a[:, 0:SEQ].bitcast(I32)
                    link(nc.vector.tensor_scalar(rest, off, dilation - 1, None, ALU.bitwise_and))
                    link(nc.vector.tensor_scalar(scr_b[:, 0:SEQ], rest, 0.0, NEG, ALU.is_gt, ALU.mult))
                    link(nc.vector.tensor_tensor(dil_mask[:, g, :], scr_b[:, 0:SEQ], causal[:, :], ALU.add))

            def angles():
                dve.wait_ge(rope_loaded, 16 * (NT + 1))
                link(nc.vector.tensor_copy(pos_f[:, :], pos_i[:, :]))
                product = scr_a[:, 0:48 * NT].rearrange("p (t f) -> p t f", t=NT)
                turns = scr_b[:, 0:48 * NT].rearrange("p (t f) -> p t f", t=NT)
                for t in range(NT):
                    ins = nc.vector.tensor_scalar(product[:, t, :], freq[:, :], pos_f[:, t:t + 1], None, ALU.mult)
                link(ins)
                for j, quarter in ((0, 0.25), (1, 0.0)):
                    a = angle[:, j, :, :]
                    link(nc.vector.tensor_scalar(turns, product, 1 / (2 * math.pi), quarter, ALU.mult, ALU.add))
                    link(nc.vector.tensor_scalar(turns, turns, ROUND, None, ALU.add))
                    link(nc.vector.tensor_scalar(turns, turns, ROUND, None, ALU.subtract))
                    link(nc.vector.scalar_tensor_tensor(out=a, in0=turns, scalar=-C1, in1=product,
                                                        op0=ALU.mult, op1=ALU.add))
                    link(nc.vector.scalar_tensor_tensor(out=a, in0=turns, scalar=-C2, in1=a,
                                                        op0=ALU.mult, op1=ALU.add))
                    link(nc.vector.scalar_tensor_tensor(out=a, in0=turns, scalar=-C3, in1=a,
                                                        op0=ALU.mult, op1=ALU.add))
                    if quarter:
                        link(nc.vector.tensor_scalar(a, a, math.pi / 2, None, ALU.add))
                    last = nc.vector.tensor_scalar(a, a, 3.1415925, -3.1415925, ALU.min, ALU.max)
                    if quarter:
                        link(last)
                last.then_inc(angle_ready, 1)

            def rope_tables():
                dve.wait_ge(sin_ready, 1)
                dve.wait_ge(const_loaded, 16 * N_SMALL)
                for t in range(NT):
                    cos, sin = sines[:, 0, t, :], sines[:, 1, t, :]
                    for h in range(2):
                        nc.vector.tensor_copy(rc64[:, t, h * 32:(h + 1) * 32], cos[:, 0:32])
                        nc.vector.tensor_scalar(rs64[:, t, h * 32:(h + 1) * 32], sin[:, 0:32], 2.0 * h - 1, None,
                                                ALU.mult)
                        nc.vector.tensor_copy(scr_a[:, h * 16:(h + 1) * 16], cos[:, 32:48])
                        last = nc.vector.tensor_scalar(scr_b[:, h * 16:(h + 1) * 16], sin[:, 32:48], 2.0 * h - 1,
                                                       None, ALU.mult)
                    link(last)
                    for j in range(2):
                        g = head_gain[:, j * ROPE:(j + 1) * ROPE]
                        nc.vector.tensor_tensor(gc32[:, t, j, :], scr_a[:, 0:32], g, ALU.mult)
                        nc.vector.tensor_tensor(gs32[:, t, j, 0:16], scr_b[:, 0:16], g[:, 16:], ALU.mult)
                        nc.vector.tensor_tensor(gs32[:, t, j, 16:], scr_b[:, 16:32], g[:, 0:16], ALU.mult)
                    for j in range(4):
                        g = head_gain[:, 64 + j * HD:64 + (j + 1) * HD]
                        nc.vector.tensor_tensor(gc64[:, t, j, :], rc64[:, t, :], g, ALU.mult)
                        nc.vector.tensor_tensor(gs64[:, t, j, 0:32], rs64[:, t, 0:32], g[:, 32:], ALU.mult)
                        last = nc.vector.tensor_tensor(gs64[:, t, j, 32:], rs64[:, t, 32:], g[:, 0:32], ALU.mult)
                    link(last)

            def heads(v, h):
                return v.rearrange("p (h e) -> p h e", h=h)

            def lora_rows():
                for t in range(NT):
                    for name, at, w in (("lora_q", 0, Q_LORA), ("lora_kv", Q_LORA, KV_LORA)):
                        head_squares(f"{name}{t}", cols[:, t, at:at + w].unsqueeze(1), w)
                for t in range(NT):
                    for name, at, w in (("lora_q", 0, Q_LORA), ("lora_kv", Q_LORA, KV_LORA)):
                        last = nc.vector.scalar_tensor_tensor(out=tm[:, t, at:at + w], in0=cols[:, t, at:at + w],
                                                              scalar=rstd_of(f"{name}{t}"),
                                                              in1=lora_gain[:, at:at + w], op0=ALU.mult, op1=ALU.mult)
                    last.then_inc(rows_ready, 1)

            def mla_heads(pump):
                for t in range(NT):
                    q = heads(q_mla[:, t, :], MLA_H)
                    k = heads(k_mla[:, t, :], MLA_H)
                    kr = cols[:, t, Q_LORA + KV_LORA:DIL0].unsqueeze(1)
                    for name, v, w in ((f"mla_q{t}", q[:, :, 0:HD], HD), (f"mla_qr{t}", q[:, :, HD:], ROPE),
                                       (f"mla_k{t}", k[:, :, 0:HD], HD), (f"mla_kr{t}", kr, ROPE)):
                        head_squares(name, v, w)
                        next(pump, None)
                    rotate(q[:, :, HD:], over_heads(gc32[:, t, 0, :], MLA_H), over_heads(gs32[:, t, 0, :], MLA_H))
                    next(pump, None)
                    rotate(kr, over_heads(gc32[:, t, 1, :], 1), over_heads(gs32[:, t, 1, :], 1))
                    scale_heads(f"mla_q{t}", q[:, :, 0:HD])
                    scale_heads(f"mla_qr{t}", q[:, :, HD:])
                    scale_heads(f"mla_k{t}", k[:, :, 0:HD])
                    link(scale_heads(f"mla_kr{t}", kr))
                    next(pump, None)
                    nc.vector.tensor_tensor(q[:, :, 0:HD], q[:, :, 0:HD], over_heads(nope_gain[:, 0, :], MLA_H),
                                            ALU.mult)
                    nc.vector.tensor_tensor(k[:, :, 0:HD], k[:, :, 0:HD], over_heads(nope_gain[:, 1, :], MLA_H),
                                            ALU.mult)
                    last = nc.vector.tensor_copy(k[:, :, HD:], kr.to_broadcast([P, MLA_H, ROPE]))
                    next(pump, None)
                last.then_inc(heads_ready, 1)

            def dil_heads(g, pump):
                for t in range(NT):
                    head_squares(f"dil{g}_{t}", dil_cols(t)[:, g, 0:8, :], HD)
                    next(pump, None)
                for t in range(NT):
                    v = dil_cols(t)[:, g, 0:8, :]
                    rotate(v.rearrange("p (j h) e -> p j h e", j=2),
                           gc64[:, t, 0:2, :].unsqueeze(2).to_broadcast([P, 2, 4, HD]),
                           gs64[:, t, 0:2, :].unsqueeze(2).to_broadcast([P, 2, 4, HD]))
                    last = scale_heads(f"dil{g}_{t}", v)
                    next(pump, None)
                if g == 2:
                    last.then_inc(heads_ready, 1)

            def idx_heads():
                for t in range(NT):
                    qi = heads(cols[:, t, 1152:1664], IDX_H)
                    ki = cols[:, t, 1664:1728].unsqueeze(1)
                    rotate(qi, over_heads(rc64[:, t, :], IDX_H), over_heads(rs64[:, t, :], IDX_H))
                    rotate(ki, over_heads(rc64[:, t, :], 1), over_heads(rs64[:, t, :], 1))
                    nc.vector.tensor_copy(twin[:, t, P:2 * P].rearrange("p (j e) -> p j e", j=2),
                                          ki.to_broadcast([P, 2, HD]))
                    last = nc.vector.tensor_scalar(w_idx[:, t, :], cols[:, t, 1728:1736], IDX_H ** -0.5, None,
                                                   ALU.mult)
                last.then_inc(heads_ready, 1)

            def spa_keys():
                for t in range(NT):
                    head_squares(f"spa_k{t}", cols[:, t, 1024:1088].unsqueeze(1), HD)
                for t in range(NT):
                    k = cols[:, t, 1024:1088].unsqueeze(1)
                    rotate(k, over_heads(gc64[:, t, 3, :], 1), over_heads(gs64[:, t, 3, :], 1))
                    link(scale_heads(f"spa_k{t}", k))
                    nc.vector.tensor_copy(twin[:, t, 0:P].rearrange("p (j e) -> p j e", j=2),
                                          k.to_broadcast([P, 2, HD]))

            def spa_queries(j, pump):
                for t in range(NT):
                    head_squares(f"spa_q{j}_{t}", heads(cols[:, t, j * 512:(j + 1) * 512], 8), HD)
                    next(pump, None)
                for t in range(NT):
                    q = heads(cols[:, t, j * 512:(j + 1) * 512], 8)
                    rotate(q, over_heads(gc64[:, t, 2, :], 8), over_heads(gs64[:, t, 2, :], 8))
                    last = scale_heads(f"spa_q{j}_{t}", q)
                    next(pump, None)
                if j == 1:
                    last.then_inc(heads_ready, 1)

            def wide_means(name, event):
                for t in range(NT):
                    dve.wait_ge(sumsq_done, square_events[0] + event(t))
                    mean_square(f"{name}{t}", X_HD)

            def wide_heads(name, src, j):
                for t in range(NT):
                    r = rstd_of(f"{name}{t}")
                    for h in range(X_H):
                        v = src[:, t, h * X_HD:(h + 1) * X_HD]
                        last = nc.vector.scalar_tensor_tensor(out=v, in0=v, scalar=r[:, h:h + 1],
                                                              in1=x_gain[:, j, :], op0=ALU.mult, op1=ALU.mult)
                last.then_inc(heads_ready, 1)

            def select_keys(pump):
                for t in range(NT):
                    keys = P * (t + 1)
                    s, l_ = score[:, t, 0:keys], left[:, t, 0:keys]
                    relu = relu_of(t)
                    dve.wait_ge(relu_done, t + 1)
                    link(nc.vector.tensor_scalar(s, relu[:, 0:keys], w_idx[:, t, 0:1], 0.0, ALU.mult, ALU.add))
                    for r in range(1, IDX_H):
                        h = half_first(r)
                        ins = nc.vector.scalar_tensor_tensor(out=s, in0=relu[:, r * keys:(r + 1) * keys],
                                                             scalar=w_idx[:, t, h:h + 1], in1=s,
                                                             op0=ALU.mult, op1=ALU.add)
                        link(ins)
                    link(nc.vector.tensor_tensor(s, s, causal[:, SEQ - keys:], ALU.add))
                    for n in range(TOPK // 8):
                        have = s if n == 0 else l_
                        link(nc.vector.max(top8[:, :], have))
                        link(nc.vector.match_replace(l_, top8[:, :], have, TAKEN))
                        if n % 3 == 2:
                            next(pump, None)
                    link(nc.vector.tensor_scalar(l_, l_, -1e38, NEG, ALU.is_gt, ALU.mult))
                    last = nc.vector.tensor_tensor(sel_mask[:, t, 0:keys], l_, causal[:, SEQ - keys:], ALU.add)
                    next(pump, None)
                last.then_inc(selected, 1)

            dilated_masks()
            for t in range(NT):
                row_mean("norm_ffn1_0_", t)
            for t in range(NT):
                norm_row("norm_ffn1_0_", t, 1, x, tm)
            lo_until(4)
            T_event("ffn0")
            angles()
            for l in range(2):
                if l:
                    norm(f"norm_ffn1_{l}_", "ffn2", 5 * l + 1, ffn_update(1), lambda t: (x_updated, NT + t + 1))
                ffn(2 * l)
                mixer_in = place[("even_in", "odd_in")[l]]
                mixer_out = place[("even_out", "odd_out")[l]]
                memkv, xq, xo = place[f"memkv{l}"], place[f"xq{l}"], place[f"xo{l}"]
                norm(f"norm_mix_{l}_", mixer_in.name, 5 * l + 3, ffn_update(2 * l),
                     lambda t: (x_updated, 2 * l * NT + t + 1))
                pump = lo_of(mixer_in)
                if l == 0:
                    run(project_lo(mixer_in.end(0) + 2))
                    groups_out(mixer_in, 0)
                    lora_rows()
                    for g in range(3):
                        run(project_lo(mixer_in.end(g + 1) + 1))
                        groups_out(mixer_in, g + 1)
                        dil_heads(g, pump)
                    run(pump)
                    T_event("lora")
                    run(lo_of(place["uq"]))
                    run(lo_of(place["ukv"]))
                    T_event(memkv.name)
                    groups_out(place["ukv"], 1)
                    pump = lo_of(memkv)
                    next(pump, None)
                    mla_heads(pump)
                else:
                    run(project_lo(mixer_in.end(1) + 2))
                    groups_out(mixer_in, 1)
                    idx_heads()
                    next(pump, None)
                    next(pump, None)
                    spa_keys()
                    run(project_lo(mixer_in.end(2) + 2))
                    groups_out(mixer_in, 2)
                    spa_queries(0, pump)
                    run(pump)
                    move_chunks(idx_chunks())
                    T_event(memkv.name)
                    pump = lo_of(memkv)
                    select_keys(pump)
                    groups_out(mixer_in, 3)
                    spa_queries(1, pump)
                run(pump)
                dve.wait_ge(xgain_loaded, 32 * (l + 1))
                wide_means(f"memk{l}_", lambda t: t + 1)
                square_events[0] += NT
                wide_heads(f"memk{l}_", kvb, 1)
                if l == 0:
                    move_chunks(mla_chunks())
                    attend(MLA_TILES)
                    move_chunks(dil_chunks())
                    attend(DIL_TILES)
                else:
                    move_chunks(spa_chunks())
                    attend(SPA_TILES)
                T_event(mixer_out.name)
                norm(f"norm_x_{l}_", xq.name, 5 * l + 4, project_update(mixer_out), update_wait(mixer_out))
                run(lo_of(xq))
                move_chunks(x_chunks("k"))
                wide_means(f"xq{l}_", lambda t: NT + t + 1)
                square_events[0] += 2 * NT
                wide_heads(f"xq{l}_", cols, 0)
                move_chunks(x_chunks("q"))
                attend(X_TILES)
                T_event(xo.name)
                norm(f"norm_ffn2_{l}_", f"ffn{2 * l + 1}", 5 * l + 5, project_update(xo), update_wait(xo))
                ffn(2 * l + 1)
            update = ffn_update(3)
            for t in range(NT):
                update(t)

        @block.tensor
        def _(pe):
            chunk = [0]
            tile = [0]

            def product(out, lh, ll, rh, rl, start, stop):
                nc.tensor.matmul(out, lh, rh, start=start, stop=False)
                nc.tensor.matmul(out, lh, rl, start=False, stop=False)
                return nc.tensor.matmul(out, ll, rh, start=False, stop=stop)

            def weight_block(n, k, width, pitch=512):
                at = slice(k * pitch, k * pitch + width)
                return w_hi[:, n % SPLIT, at], w_lo[:, n % SPLIT, at]

            def act_block(k, t, arrays_=(act_hi, act_lo)):
                at = slice(t * P, (t + 1) * P)
                return arrays_[0][:, k, at], arrays_[1][:, k, at]

            def T_tile_psum(name, src, ready, t):
                pe.wait_ge(*ready(t))
                for c, t, b, nb in T_tile(name, t):
                    for j in range(nb):
                        last = nc.tensor.transpose(SC[2 * t + b // 4][:, j * P:(j + 1) * P],
                                                   src[:, t, (b + j) * P:(b + j + 1) * P], ident[:, :])
                    last.then_inc(T_psum, 1)

            def T_split_of(name, t, block):
                c, kt, _ = T_first[name]
                per = 2 if kt > 4 else 1
                pe.wait_ge(T_split, c + t * per + (block // 4) + 1)

            def rows(name):
                return lambda t: (rows_ready, NT * ROWS.index(name) + t + 1)

            def up(f, n, c, i=None):
                if NCH * f + c > 0:
                    pe.wait_ge(gated_done, val(NT * (NCH * f + c), 2 * NT, i))
                for g in range(4):
                    pe.wait_ge(lo_done, val(n + g + 1, 12, i))
                    for k in range(2):
                        for t in range(NT):
                            last = product(SC[t], *act_block(2 * g + k, t), *weight_block(n + g, k, 512),
                                           g + k == 0, g == 3 and k == 1)
                    last.then_inc(unit_used, 1)

            def up_tile(f, n, t, event=None):
                if f + (event is None):
                    pe.wait_ge(gated_done, NT * NCH * f + (0 if event else NT * (NCH - 1)))
                for g in range(4):
                    if event:
                        T_split_of(event, t, 2 * g + 1)
                    if t == 0:
                        pe.wait_ge(lo_done, n + g + 1)
                    for k in range(2):
                        last = product(SC[t], *act_block(2 * g + k, t), *weight_block(n + g, k, 512),
                                       g + k == 0, g == 3 and k == 1)
                    if t == 1:
                        last.then_inc(unit_used, 1)
                if t == 0:
                    last.then_inc(tile0_done, 1)

            def gate_transposes(f, c, i=None):
                for t in range(NT):
                    pe.wait_ge(gated_done, val(NT * (NCH * f + c) + t + 1, 2 * NT, i))
                    for b in range(2):
                        last = nc.tensor.transpose(SC[2][:, b * SEQ + t * P:b * SEQ + (t + 1) * P],
                                                   gated[:, t, b * P:(b + 1) * P], ident[:, :])
                last.then_inc(gT_psum, 1)

            def gate_transposes_last(f, t):
                pe.wait_ge(gated_done, NT * (NCH * f + NCH - 1) + t + 1)
                for b in range(2):
                    last = nc.tensor.transpose(SC[2 + t][:, b * P:(b + 1) * P], gated[:, t, b * P:(b + 1) * P],
                                               ident[:, :])
                last.then_inc(gT_psum, 1)

            def down(f, n, c, i=None):
                pe.wait_ge(gT_split, val(GT_COUNT * f + c + 1, 2, i))
                for b in range(2):
                    pe.wait_ge(lo_done, val(n + b + 1, 12, i))
                    for t in range(NT):
                        at = slice(t * P, (t + 1) * P)
                        for h in range(2):
                            last = product(acc(t, h), gT_hi[:, b, at], gT_lo[:, b, at],
                                           *weight_block(n + b, h, 512), False, False)
                    last.then_inc(unit_used, 1)

            def down_tile(n, t, hi_, lo_, stop):
                at = slice(t * P, (t + 1) * P)
                for b in range(2):
                    for h in range(2):
                        last = product(acc(t, h), hi_[:, b, at], lo_[:, b, at], *weight_block(n + b, h, 512),
                                       False, stop and b == 1)
                    if t == 1:
                        last.then_inc(unit_used, 1)
                return last

            def last_chunk(f, n):
                for t in range(NT):
                    up_tile(f, n, t)
                base = GT_COUNT * f + NCH
                pe.wait_ge(gT_split, base - 1)
                gate_transposes_last(f, 0)
                pe.wait_ge(lo_done, n + 6)
                down_tile(n + 4, 0, gT_hi, gT_lo, False)
                gate_transposes_last(f, 1)
                pe.wait_ge(gT_split, base)
                pe.wait_ge(lo_done, n + 8)
                down_tile(n + 6, 0, act_hi, act_lo, True).then_inc(ffn_sum, 1)
                down_tile(n + 4, 1, gT_hi, gT_lo, False)
                pe.wait_ge(gT_split, base + 1)
                down_tile(n + 6, 1, act_hi, act_lo, True)

            def ffn_step(f, n, c, i=None):
                up(f, n, c, i)
                down(f, n + 4, c - 1, i)
                gate_transposes(f, c, i)

            def ffn(f):
                n = place[f"ffn{f}"]
                name = f"ffn{f}"
                for t in range(NT):
                    T_tile_psum(name, tm, rows(name), t)
                    up_tile(f, n, t, name)
                for t in range(NT):
                    for h in range(2):
                        for b in range(2):
                            nc.tensor.matmul(acc(t, h)[:, b * SEQ:(b + 1) * SEQ], zeros[:, :],
                                             ident[:, :].bitcast(BF16), start=b == 0, stop=False)
                gate_transposes(f, 0)
                n += 4
                with pe.Fori(0, LOOPS) as i:
                    ffn_step(f, n, 1, i)
                    ffn_step(f, n + 6, 2, i)
                for c in range(1 + 2 * LOOPS, NCH - 1):
                    ffn_step(f, n + 6 * (c - 1), c)
                last_chunk(f, n + 6 * (NCH - 2))

            def project(pr, event, src=None, ready=None, k0=0):
                arrays_ = T_dest(event)
                for g, (_, width, _, _) in enumerate(pr.groups):
                    G = pr.group0 + g
                    if g in pr.tiled:
                        for t in range(NT):
                            if g == 0 and src is not None:
                                T_tile_psum(event, src, ready, t)
                            if G >= 2:
                                pe.wait_ge(group_out[t], G - 1)
                            for u in range(pr.upg):
                                n = pr.unit0 + pr.upg * g + u
                                T_split_of(event, t, 2 * u + 1)
                                if t == 0:
                                    pe.wait_ge(lo_done, n + 1)
                                for k in range(2 * u, 2 * u + 2):
                                    last = product(sums(pr, t, g), *act_block(k0 + k, t, arrays_),
                                                   *weight_block(n, k % 2, width), k == 0, k == pr.kt - 1)
                                if t == 1:
                                    last.then_inc(unit_used, 1)
                            if t == 0:
                                last.then_inc(tile0_done, 1)
                        continue
                    pe.wait_ge(T_split, T_done(event))
                    for t in range(NT):
                        if G >= 2:
                            pe.wait_ge(group_out[t], G - 1)
                    if pr.wide:
                        pe.wait_ge(lo_done, pr.unit0 + 1)
                        for t in range(NT):
                            last = product(sums(pr, t, g), *act_block(k0, t, arrays_),
                                           *weight_block(pr.unit0, g, width), True, True)
                        if g == len(pr.groups) - 1:
                            last.then_inc(unit_used, 1)
                        continue
                    for u in range(pr.upg):
                        n = pr.unit0 + pr.upg * g + u
                        pe.wait_ge(lo_done, n + 1)
                        for k in range(2 * u, 2 * u + 2):
                            for t in range(NT):
                                last = product(sums(pr, t, g), *act_block(k0 + k, t, arrays_),
                                               *weight_block(n, k % 2, width), k == 0, k == pr.kt - 1)
                        last.then_inc(unit_used, 1)

            def transpose_chunks(chunks):
                for srcs, dst in chunks:
                    c = chunk[0]
                    if c >= 2:
                        who, count = CHUNKS[c - 2]
                        pe.wait_ge(chunk_out[who], count)
                    for j, s in enumerate(srcs):
                        last = nc.tensor.transpose(CK[c % 2][0:s.shape[1], j * P:(j + 1) * P], s, ident[:, :])
                    last.then_inc(chunk_psum, 1)
                    chunk[0] += 1

            def moved():
                for who in range(2):
                    count = sum(1 for w, _ in CHUNKS[:chunk[0]] if w == who)
                    if count:
                        pe.wait_ge(chunk_out[who], count)

            def operands(tl, r, s):
                q = slice(tl.qt * P, (tl.qt + 1) * P)
                h = tl.head(r)
                if tl.kind == "mla":
                    return [(mla_qT[0:MLA_QK, h, q], mla_kT[0:MLA_QK, h, 0:tl.keys])]
                half = slice((h % 2) * HD, (h % 2 + 1) * HD)
                if tl.kind == "dil":
                    return [(dil_qT[half, 2 * s + h // 2, q], dil_kT[half, 2 * s + h // 2, 0:tl.keys])]
                if tl.kind == "spa":
                    return [(spa_qT[half, h // 2, q], spa_kT[half, 0:tl.keys])]
                return [(x_qT[:, 2 * h + j, q], x_kT[:, 2 * h + j, 0:tl.keys]) for j in range(2)]

            def values(tl, r, s, kt):
                h = tl.head(r)
                return {"mla": lambda: v_mla[:, kt, h * HD:(h + 1) * HD],
                        "dil": lambda: dil_cols(kt)[:, s, 8 + h, :],
                        "spa": lambda: cols[:, kt, 1088:1152],
                        "x": lambda: kvb[:, kt, D + h * X_HD:D + (h + 1) * X_HD]}[tl.kind]()

            def mask_of(tl, r, s):
                if tl.kind == "mla":
                    return tl.keys - P, causal[:, P:SEQ]
                if tl.kind == "dil":
                    return 0, dil_mask[:, s, SEQ - tl.keys:]
                if tl.kind == "spa":
                    return 0, sel_mask[:, tl.qt, 0:tl.keys]
                return None

            def scores(tl, a):
                for r in range(tl.rows):
                    for s in range(tl.segs):
                        at = 1024 * (a % 2) + r * tl.pitch + s * tl.keys
                        parts = operands(tl, r, s)
                        for j, (q, k) in enumerate(parts):
                            last = nc.tensor.matmul(low[:, at:at + tl.keys], q, k, start=j == 0,
                                                    stop=mask_of(tl, r, s) is None and j == len(parts) - 1)
                        if mask_of(tl, r, s) is not None:
                            first, m = mask_of(tl, r, s)
                            last = nc.tensor.matmul(low[:, at + first:at + tl.keys], ident_b[:, :], m,
                                                    start=False, stop=True)
                last.then_inc(scores_ready, 1)

            def outputs(tl, a):
                if a >= 2:
                    pe.wait_ge(out_read, a - 1)
                moved()
                per = tl.width // P
                for r in range(tl.rows):
                    for j in range(per):
                        b = 1024 * (a % 2) + (r * per + j) * P
                        o = (tl.head(r) - tl.first) * tl.out
                        last = nc.tensor.matmul(OB[a % 2][:, o:o + tl.out], pTb[:, b:b + P],
                                                values(tl, r, j // (tl.keys // P), j % (tl.keys // P)),
                                                start=j == 0, stop=j == per - 1)
                last.then_inc(out_ready, 1)

            def attend(tiles):
                first = tile[0]
                scores(tiles[0], first)
                scores(tiles[1], first + 1)
                for j, tl in enumerate(tiles):
                    pe.wait_ge(probs_ready, first + j + 1)
                    transpose_chunks(prob_chunks(tl, first + j))
                    if j + 2 < len(tiles):
                        scores(tiles[j + 2], first + j + 2)
                    outputs(tl, first + j)
                tile[0] = first + len(tiles)

            def groups_read(pr):
                for t in range(NT):
                    pe.wait_ge(group_out[t], pr.group0 + len(pr.groups))

            pe.wait_ge(consts_made, 5)
            for l in range(2):
                ffn(2 * l)
                mixer_in = place[("even_in", "odd_in")[l]]
                mixer_out = place[("even_out", "odd_out")[l]]
                memkv, xq, xo = place[f"memkv{l}"], place[f"xq{l}"], place[f"xo{l}"]
                project(mixer_in, mixer_in.name, tm, rows(mixer_in.name))
                if l == 0:
                    project(place["uq"], "lora", tm, rows("lora"))
                    project(place["ukv"], "lora", k0=2)
                else:
                    groups_read(mixer_in)
                    pe.wait_ge(heads_ready, HEADS["idx"])
                    transpose_chunks(idx_chunks())
                    moved()
                    for qt in range(NT):
                        keys = P * (qt + 1)
                        if qt:
                            pe.wait_ge(relu_done, qt)
                        for r in range(IDX_H):
                            h = half_first(r)
                            half = slice((h % 2) * HD, (h % 2 + 1) * HD)
                            last = nc.tensor.matmul(low[:, r * keys:(r + 1) * keys],
                                                    idx_qT[half, h // 2, qt * P:(qt + 1) * P], idx_kT[half, 0:keys],
                                                    start=True, stop=True)
                        last.then_inc(logits_ready, 1)
                    pe.wait_ge(relu_done, NT)
                project(memkv, memkv.name, kvb, rows(memkv.name))
                groups_read(memkv)
                if l == 0:
                    pe.wait_ge(heads_ready, HEADS["mla"])
                    transpose_chunks(mla_chunks())
                    moved()
                    attend(MLA_TILES)
                    transpose_chunks(dil_chunks())
                    moved()
                    attend(DIL_TILES)
                    out_count = [TILE0["dil"] + 2, TILE0["dil"] + len(DIL_TILES)]
                else:
                    pe.wait_ge(heads_ready, HEADS["spa"])
                    transpose_chunks(spa_chunks())
                    moved()
                    pe.wait_ge(selected, 1)
                    attend(SPA_TILES)
                    out_count = [TILE0["spa"] + 2, TILE0["spa"] + len(SPA_TILES)]
                project(mixer_out, mixer_out.name, tm, lambda t: (out_read, out_count[t]))
                project(xq, xq.name, tm, rows(xq.name))
                groups_read(xq)
                pe.wait_ge(heads_ready, HEADS[f"xk{l}"])
                transpose_chunks(x_chunks("k"))
                pe.wait_ge(heads_ready, HEADS[f"xq{l}"])
                transpose_chunks(x_chunks("q"))
                moved()
                attend(X_TILES)
                project(xo, xo.name, tm, lambda t: (out_read, TILE0[f"x{l}"] + 2 * (t + 1)))
                ffn(2 * l + 1)


_F32 = ["mix_norm", "xattn_norm", "mem_norm", "xattn_wq", "xattn_wkv", "xattn_q_gain", "xattn_k_gain", "xattn_wo",
        "even_w_in", "mla_q_lora_norm", "mla_kv_lora_norm", "mla_w_uq", "mla_w_ukv", "mla_q_gain", "mla_k_gain",
        "dil_q_gain", "dil_k_gain", "even_w_out", "odd_w_in", "sparse_q_gain", "sparse_k_gain", "odd_w_out"]


def kernel(**inputs):
    import concourse.bacc as _bacc
    from concourse.bass_utils import run_bass_kernel_spmd as _run

    nc = _bacc.Bacc("TRN2", target_bir_lowering=False, num_devices=1)
    arrays = {}

    def give(name, a):
        a = np.ascontiguousarray(a)
        arrays["in_" + name] = a
        return nc.dram_tensor("in_" + name, a.shape, mybir.dt.from_np(a.dtype), kind="ExternalInput").ap()

    x_in = give("x", np.asarray(inputs["x"])[0])
    mem_in = give("mem", np.asarray(inputs["mem"])[0])
    positions = give("positions", inputs["positions"])
    norms = [give("ffn1_norm", inputs["ffn1_norm"]), give("ffn2_norm", inputs["ffn2_norm"])]
    w13 = [give("ffn1_w13", inputs["ffn1_w13"]), give("ffn2_w13", inputs["ffn2_w13"])]
    w2 = [give("ffn1_w2", inputs["ffn1_w2"]), give("ffn2_w2", inputs["ffn2_w2"])]
    all_w13 = [w13[f % 2][f // 2] for f in range(4)]
    all_w2 = [w2[f % 2][f // 2] for f in range(4)]
    rest = [give(name, inputs[name]) for name in _F32]
    inv = [np.exp(np.float32(-math.log(10000.0)) * np.arange(0, dim, 2, dtype=np.float32) / np.float32(dim))
           for dim in (HD, ROPE)]
    freq = give("rope_frequencies", np.concatenate(inv)[None].astype(np.float32))
    out = nc.dram_tensor("out", (SEQ, D), F32, kind="ExternalOutput").ap()
    build(nc, x_in, mem_in, positions, norms, all_w13, all_w2, *rest, freq, out)
    r = _run(nc, [arrays], core_ids=[0])
    return r.results[0]["out"].reshape(1, SEQ, D)
```

```python
import math
from contextlib import ExitStack

import numpy as np

import concourse.bass as bass
from concourse import mybir

F32 = mybir.dt.float32
F32R = mybir.dt.float32r
BF16 = mybir.dt.bfloat16
I32 = mybir.dt.int32
ALU = mybir.AluOpType
ACT = mybir.ActivationFunctionType
AX = mybir.AxisListType.X

P = 128
D = 1024
SEQ = 256
NT = SEQ // P
KD = D // P
FF = 2816
CH = 256
NCH = FF // CH
EPS = 1e-6
NEG = -1e30
TAKEN = -3e38
HD = 64
Q_LORA, KV_LORA, ROPE = 256, 128, 32
MLA_H, MLA_QK = 8, 96
DIL0 = Q_LORA + KV_LORA + ROPE
EVEN_IN = DIL0 + 2304
SPA_H, IDX_H = 16, 8
ODD_IN = 1736
TOPK = 64
X_H, X_HD = 4, 256
RAW, SPLIT = 6, 6
LOOPS = 4
C1 = 6.28125
C2 = float(np.float32(np.float32((2 * math.pi - C1) * 2 ** 20).astype(np.int64) // 2 ** 6 * 2 ** 6 / 2 ** 20))
C3 = float(np.float32(2 * math.pi - C1 - C2))
ROUND = 12582912.0


class Projection:

    def __init__(self, name, rows, groups, wide=False, tiled=()):
        self.name, self.kt, self.wide, self.tiled = name, rows // P, wide, tiled
        self.groups = [g if len(g) == 4 else (*g, 1, 0) for g in groups]
        self.upg = 1 if wide else (self.kt + 1) // 2
        self.units = 1 if wide else self.upg * len(groups)

    def end(self, g):
        return self.unit0 + (1 if self.wide else self.upg * (g + 1))


def plan_stream():
    def halves(name, rows):
        return Projection(name, rows, [(0, 512), (512, 512)], tiled=(0, 1))

    def memory(name):
        return Projection(name, D, [(512 * g, 512) for g in range(4)], tiled=(0,))

    even_in = [(0, DIL0)] + [(DIL0 + 768 * g, 512) for g in range(3)]
    even_in += [(DIL0 + 512, 512, 2, 768), (DIL0 + 768 * 2 + 512, 256)]
    odd_in = [(1024, 512), (1536, 200), (0, 512), (512, 512)]
    order = ["ffn0",
             Projection("even_in", D, even_in, tiled=(0,)),
             Projection("uq", Q_LORA, [(0, 512), (512, 256)], tiled=(0,)),
             Projection("ukv", KV_LORA, [(0, 512), (512, 512)], wide=True),
             memory("memkv0"), halves("even_out", 768), halves("xq0", D), halves("xo0", D),
             "ffn1", "ffn2",
             Projection("odd_in", D, odd_in, tiled=(0,)),
             memory("memkv1"), halves("odd_out", D), halves("xq1", D), halves("xo1", D),
             "ffn3"]
    unit = group = early = 0
    places, first = {}, {}
    for it in order:
        if isinstance(it, str):
            places[it] = unit
            unit += 6 * NCH
            first[it, 0], first[it, NCH - 1] = early + 1, early + 2
            early += 2
        else:
            for g in it.tiled:
                early += 1
                first[it.name, g] = early
            it.unit0, it.group0 = unit, group
            unit += it.units
            group += len(it.groups)
            places[it.name] = it
    return order, places, unit, first


def plan_rms():
    widths = []
    def both(name, w):
        for t in range(NT):
            widths.append((f"{name}{t}", w))
    for layer in range(2):
        both(f"norm_ffn1_{layer}_", 1)
        both(f"norm_mem_{layer}_", 1)
        both(f"norm_mix_{layer}_", 1)
        if layer == 0:
            for t in range(NT):
                widths += [(f"lora_q{t}", 1), (f"lora_kv{t}", 1)]
            for g in range(3):
                both(f"dil{g}_", 8)
            for t in range(NT):
                widths += [(f"mla_q{t}", 8), (f"mla_qr{t}", 8), (f"mla_k{t}", 8), (f"mla_kr{t}", 1)]
        else:
            both("spa_k", 1)
            both("spa_q0_", 8)
            both("spa_q1_", 8)
        both(f"memk{layer}_", X_H)
        both(f"norm_x_{layer}_", 1)
        both(f"xq{layer}_0", X_H // 2)
        both(f"xq{layer}_1", X_H // 2)
        both(f"norm_ffn2_{layer}_", 1)
    out, col = {}, 0
    for i, (name, w) in enumerate(widths):
        out[name] = (i, col, w)
        col += w
    return out, col


def half_first(r, n=8):
    return 2 * (r % (n // 2)) + r // (n // 2)


class Tile:

    def __init__(self, kind, qt, rows, segs, keys, first, out, scale):
        self.kind, self.qt, self.rows, self.segs, self.keys = kind, qt, rows, segs, keys
        self.first, self.out, self.scale = first, out, scale
        self.width = segs * keys
        self.blocks = rows * self.width // P
        self.pitch = 512 if kind == "dil" and rows == 2 else self.width

    def head(self, r):
        return self.first + (half_first(r, self.rows) if self.kind == "spa" else r)


def mla_tiles():
    return [Tile("mla", 0, 8, 1, P, 0, HD, MLA_QK ** -0.5)] + \
           [Tile("mla", 1, 4, 1, SEQ, h, HD, MLA_QK ** -0.5) for h in (0, 4)]


def dil_tiles():
    return [Tile("dil", 0, 2, 3, P, h, HD, HD ** -0.5) for h in (0, 2)] + \
           [Tile("dil", 1, 1, 3, SEQ, h, HD, HD ** -0.5) for h in range(4)]


def spa_tiles():
    return [Tile("spa", 0, 8, 1, P, h, HD, HD ** -0.5) for h in (0, 8)] + \
           [Tile("spa", 1, 4, 1, SEQ, h, HD, HD ** -0.5) for h in range(0, SPA_H, 4)]


def x_tiles():
    return [Tile("x", qt, 2, 1, SEQ, h, X_HD, X_HD ** -0.5) for qt in range(NT) for h in (0, 2)]


def build(nc, x_in, mem_in, positions, ffn_norms, ffn_w13, ffn_w2, mix_norm, xattn_norm, mem_norm,
          xattn_wq, xattn_wkv, xattn_q_gain, xattn_k_gain, xattn_wo, even_w_in, q_lora_norm, kv_lora_norm,
          w_uq, w_ukv, mla_q_gain, mla_k_gain, dil_q_gain, dil_k_gain, even_w_out, odd_w_in,
          sparse_q_gain, sparse_k_gain, odd_w_out, rope_freq, y_out):
    order, place, UNITS, FIRST = plan_stream()
    rms, RMS_COLS = plan_rms()
    MLA_TILES, DIL_TILES, SPA_TILES, X_TILES = mla_tiles(), dil_tiles(), spa_tiles(), x_tiles()
    weights = {"even_in": even_w_in[0], "uq": w_uq[0], "ukv": w_ukv[0], "even_out": even_w_out[0],
               "odd_in": odd_w_in[0], "odd_out": odd_w_out[0]}
    for l in range(2):
        weights[f"memkv{l}"], weights[f"xq{l}"], weights[f"xo{l}"] = xattn_wkv[l], xattn_wq[l], xattn_wo[l]

    ctx = ExitStack()
    with ctx:
        def sb(name, shape, dt=F32):
            return ctx.enter_context(nc.sbuf_tensor(name, shape, dt))

        def sem(name):
            return ctx.enter_context(nc.semaphore(name))

        raw = sb("raw", [P, RAW, 1024])
        w_hi = sb("w_hi", [P, SPLIT, 1024], F32R)
        w_lo = sb("w_lo", [P, SPLIT, 1024], F32R)
        act_hi = sb("act_hi", [P, KD, SEQ], F32R)
        act_lo = sb("act_lo", [P, KD, SEQ], F32R)
        x = sb("x", [P, NT, D])
        tm = sb("tm", [P, NT, D])
        kvb = sb("kvb", [P, NT, 2 * D])
        cols = sb("cols", [P, NT, EVEN_IN])
        v_mla = sb("v_mla", [P, NT, MLA_H * HD])
        qkT = sb("qkT", [P, 4096])
        scb = sb("scb", [P, 2048])
        pTb = sb("pTb", [P, 2048])
        gain = sb("gain", [P, D])
        causal = sb("causal", [P, SEQ], BF16)
        dil_mask = sb("dil_mask", [P, 3, SEQ], BF16)
        sel_mask = dil_mask[:, 0:NT, :]
        lora_gain = sb("lora_gain", [P, Q_LORA + KV_LORA])
        nope_gain = sb("nope_gain", [P, 2, HD])
        x_gain = sb("x_gain", [P, 2, X_HD])
        freq = sb("freq", [P, 48])
        pos_i = sb("pos_i", [P, NT], I32)
        pos_f = sb("pos_f", [P, NT])
        rc64 = sb("rc64", [P, NT, HD])
        rs64 = sb("rs64", [P, NT, HD])
        gc64 = sb("gc64", [P, NT, 4, HD])
        gs64 = sb("gs64", [P, NT, 4, HD])
        head_gain = sb("head_gain", [P, 2 * ROPE + 4 * HD])
        gc32 = sb("gc32", [P, NT, 2, ROPE])
        gs32 = sb("gs32", [P, NT, 2, ROPE])
        scr_a = sb("scr_a", [P, 512])
        scr_b = sb("scr_b", [P, 512])
        sumsq = sb("sumsq", [P, RMS_COLS])
        meansq = sumsq
        rstd = sb("rstd", [P, RMS_COLS])
        minus_half = sb("minus_half", [P, 8])
        warm = sb("warm", [P, 12])
        rowmax = sb("rowmax", [P, 2, 8])
        negmax = sb("negmax", [P, 4, 8])
        den = sb("den", [P, 4, 8])
        rden = sb("rden", [P, 2, 8])
        w_idx = sb("w_idx", [P, NT, IDX_H])
        top8 = sb("top8", [P, 8])
        ident = sb("ident", [P, P])
        ident_b = sb("ident_b", [P, P], BF16)
        zeros = sb("zeros", [P, P], BF16)

        silu_g = cols[:, 0, 0:512].rearrange("p (t f) -> p t f", t=NT)
        gated = cols[:, 0, 512:1024].rearrange("p (t f) -> p t f", t=NT)
        gT_hi = sb("gT_hi", [P, 3, SEQ], F32R)
        gT_lo = sb("gT_lo", [P, 3, SEQ], F32R)
        q_mla = scb[:, 0:1536].rearrange("p (t c) -> p t c", t=NT)
        k_mla = pTb[:, 0:1536].rearrange("p (t c) -> p t c", t=NT)
        mla_qT = qkT[:, 0:2048].rearrange("p (h s) -> p h s", h=8)
        mla_kT = qkT[:, 2048:4096].rearrange("p (h s) -> p h s", h=8)
        dil_qT = qkT[:, 0:1536].rearrange("p (b s) -> p b s", b=6)
        dil_kT = qkT[:, 1536:3072].rearrange("p (b s) -> p b s", b=6)
        spa_qT = qkT[:, 0:2048].rearrange("p (b s) -> p b s", b=8)
        idx_qT = qkT[:, 2048:3072].rearrange("p (b s) -> p b s", b=4)
        spa_kT = qkT[:, 3072:3328]
        idx_kT = qkT[:, 3328:3584]
        x_qT = qkT[:, 0:2048].rearrange("p (b s) -> p b s", b=8)
        x_kT = qkT[:, 2048:4096].rearrange("p (b s) -> p b s", b=8)
        angle = scb[:, 0:192].rearrange("p (j t f) -> p j t f", j=2, t=NT)
        sines = scb[:, 192:384].rearrange("p (j t f) -> p j t f", j=2, t=NT)
        twin = cols[:, :, ODD_IN:ODD_IN + 256]
        score = cols[:, :, ODD_IN + 256:ODD_IN + 512]
        left = cols[:, :, ODD_IN + 512:ODD_IN + 768]

        def relu_of(qt):
            return scb if qt else pTb

        low = ctx.enter_context(nc.psum_tensor("low", [P, 2048], F32))
        SC = [low[:, i * 512:(i + 1) * 512] for i in range(4)]
        high = ctx.enter_context(nc.psum_tensor("high", [P, 2048], F32))
        CK = [high[:, 0:512], high[:, 512:1024]]
        OB = [high[:, 1024:1536], high[:, 1536:2048]]

        mla_q_squares = qkT[:, 2048:3584].rearrange("p (t c) -> p t c", t=NT)
        mla_k_squares = qkT[:, 0:1024].rearrange("p (t c) -> p t c", t=NT)

        def square_place(g, t):
            at = 1024 * (g % 2) + 512 * t
            return qkT[:, at:at + 512]

        def logits_of(qt):
            return low[:, 0:IDX_H * SEQ] if qt else low[:, IDX_H * P:2 * IDX_H * P]

        def acc(t, n):
            return high[:, (2 * n + t) * 512:(2 * n + t + 1) * 512]

        const_loaded = sem("const_loaded")
        rope_loaded = sem("rope_loaded")
        x_loaded = [sem(f"x_loaded{t}") for t in range(NT)]
        first_gain_loaded = sem("first_gain_loaded")
        gain_loaded = sem("gain_loaded")
        mem_loaded = [sem(f"mem_loaded{t}") for t in range(NT)]
        xgain_loaded = sem("xgain_loaded")
        unit_loaded = [sem(f"unit_loaded{i}") for i in range(RAW)]
        loader_turn = sem("loader_turn")
        hi_done = sem("hi_done")
        lo_done = sem("lo_done")
        unit_used = sem("unit_used")
        silu_done = sem("silu_done")
        gated_done = sem("gated_done")
        gT_psum = sem("gT_psum")
        gT_hi_done = sem("gT_hi_done")
        gT_split = sem("gT_split")
        tile0_done = sem("tile0_done")
        ffn_sum = sem("ffn_sum")
        x_updated = sem("x_updated")
        sumsq_done = sem("sumsq_done")
        squares_ready = sem("squares_ready")
        meansq_done = sem("meansq_done")
        rstd_done = sem("rstd_done")
        rows_ready = sem("rows_ready")
        T_psum = sem("T_psum")
        T_hi = sem("T_hi")
        T_split = sem("T_split")
        group_out = [sem(f"group_out{t}") for t in range(NT)]
        heads_ready = sem("heads_ready")
        chunk_psum = sem("chunk_psum")
        chunk_out = [sem("chunk_out_dve"), sem("chunk_out_act")]
        scores_ready = sem("scores_ready")
        max_ready = sem("max_ready")
        probs_ready = sem("probs_ready")
        out_ready = sem("out_ready")
        out_read = sem("out_read")
        logits_ready = sem("logits_ready")
        relu_done = sem("relu_done")
        selected = sem("selected")
        pool_step = sem("pool_step")
        consts_made = sem("consts_made")
        angle_ready = sem("angle_ready")
        sin_ready = sem("sin_ready")
        dve_step = sem("dve_step")
        stored = sem("stored")

        NORMS = []
        for l in range(2):
            NORMS += [ffn_norms[0][l:l + 1, :], mem_norm[l:l + 1, :], mix_norm[l:l + 1, :],
                      xattn_norm[l:l + 1, :], ffn_norms[1][l:l + 1, :]]
        X_UPDATES = 4 * NT
        GT_COUNT = NCH + 1
        N_SMALL = 10
        LORA_AT = 4

        def val(base, per_turn, i):
            return base if i is None else i * per_turn + base

        T_KT = [8, 8, 3, 8, 6, 8, 8, 8, 8, 8, 8, 8, 8, 8, 8]
        ROWS = ["ffn0", "memkv0", "even_in", "lora", "xq0", "ffn1", "ffn2", "memkv1", "odd_in", "xq1", "ffn3"]
        T_NAMES = ["ffn0", "even_in", "lora", "memkv0", "even_out", "xq0", "xo0", "ffn1", "ffn2", "odd_in",
                   "memkv1", "odd_out", "xq1", "xo1", "ffn3"]
        T_first = {}
        n = 0
        for name, kt in zip(T_NAMES, T_KT):
            T_first[name] = (n, kt, T_NAMES.index(name))
            n += NT * (2 if kt > 4 else 1)

        def T_parts(name):
            c, kt, _ = T_first[name]
            for t in range(NT):
                for h in range(2 if kt > 4 else 1):
                    yield c, t, 4 * h, min(4, kt - 4 * h)
                    c += 1

        def T_done(name):
            c, kt, _ = T_first[name]
            return c + NT * (2 if kt > 4 else 1)

        def T_tile(name, t):
            return [part for part in T_parts(name) if part[1] == t]

        def first_group(name):
            return place[name] + 4 if name.startswith("ffn") else place[name].end(0)

        def T_dest(name):
            return (gT_hi, gT_lo) if name == "lora" else (act_hi, act_lo)

        TILE0 = {"mla": 0, "dil": len(MLA_TILES), "x0": len(MLA_TILES) + len(DIL_TILES)}
        TILE0["spa"] = TILE0["x0"] + len(X_TILES)
        TILE0["x1"] = TILE0["spa"] + len(SPA_TILES)

        def mla_chunks():
            for t in range(NT):
                for src, dst in ((q_mla, mla_qT), (k_mla, mla_kT)):
                    for g in (0, 4):
                        yield ([src[:, t, h * MLA_QK:(h + 1) * MLA_QK] for h in range(g, g + 4)],
                               dst[0:MLA_QK, g:g + 4, t * P:(t + 1) * P])

        def dil_cols(t):
            return cols[:, t, DIL0:EVEN_IN].rearrange("p (g h e) -> p g h e", g=3, h=12)

        def dil_chunks():
            for t in range(NT):
                for first, dst in ((0, dil_qT), (256, dil_kT)):
                    for b, n in ((0, 4), (4, 2)):
                        yield ([cols[:, t, DIL0 + (bb // 2) * 768 + first + (bb % 2) * P:][:, 0:P]
                                for bb in range(b, b + n)],
                               dst[:, b:b + n, t * P:(t + 1) * P])

        def idx_chunks():
            for t in range(NT):
                yield ([cols[:, t, 1152 + b * P:1152 + (b + 1) * P] for b in range(4)],
                       idx_qT[:, :, t * P:(t + 1) * P])
            for t in range(NT):
                yield ([twin[:, t, P:2 * P]], idx_kT[:, t * P:(t + 1) * P].unsqueeze(1))

        def spa_chunks():
            for t in range(NT):
                for b in (0, 4):
                    yield ([cols[:, t, bb * P:(bb + 1) * P] for bb in range(b, b + 4)],
                           spa_qT[:, b:b + 4, t * P:(t + 1) * P])
            for t in range(NT):
                yield ([twin[:, t, 0:P]], spa_kT[:, t * P:(t + 1) * P].unsqueeze(1))

        def x_chunks(which):
            src, dst = {"k": (kvb, x_kT), "q": (cols, x_qT)}[which]
            for b in (0, 4):
                for t in range(NT):
                    yield ([src[:, t, bb * P:(bb + 1) * P] for bb in range(b, b + 4)],
                           dst[:, b:b + 4, t * P:(t + 1) * P])

        def prob_chunks(tl, a):
            at = 1024 * (a % 2)
            for j in range(0, tl.blocks, 4):
                n = min(4, tl.blocks - j)
                yield ([scb[:, at + b * P:at + (b + 1) * P] for b in range(j, j + n)],
                       pTb[:, at + j * P:at + (j + n) * P].rearrange("p (b s) -> p b s", b=n))

        def plan_chunks():
            kinds, banks = [], []

            def heads(chunks):
                for i, _ in enumerate(chunks):
                    kinds.append(i % 2)
                    banks.append(("low", i % 4))

            def probs(tiles):
                for tl in tiles:
                    for _ in prob_chunks(tl, 0):
                        banks.append(("high", sum(1 for b in banks if b[0] == "high") % 2))
                        kinds.append(0)

            heads(mla_chunks()), probs(MLA_TILES), heads(dil_chunks()), probs(DIL_TILES)
            heads(x_chunks("k")), heads(x_chunks("q")), probs(X_TILES)
            heads(idx_chunks()), heads(spa_chunks()), probs(SPA_TILES)
            heads(x_chunks("k")), heads(x_chunks("q")), probs(X_TILES)
            plan = []
            for i, (k, b) in enumerate(zip(kinds, banks)):
                before = [j for j in range(i) if banks[j] == b]
                plan.append((k, kinds[:i + 1].count(k), (SC if b[0] == "low" else CK)[b[1]],
                             before[-1] if before else None))
            return plan

        def sums(pr, t, g):
            return acc(t, (pr.group0 + g) % 2)[:, 0:pr.groups[g][1]]

        def cols_pairs(pr, t, g):
            at, w, pieces, pitch = pr.groups[g]
            if pieces == 1:
                return [(cols[:, t, at:at + w], sums(pr, t, g))]
            w //= pieces
            return [(cols[:, t, at + i * pitch:at + i * pitch + w], sums(pr, t, g)[:, i * w:(i + 1) * w])
                    for i in range(pieces)]

        def uq_pairs(pr, t, g):
            at, w = pr.groups[g][0:2]
            return [(q_mla[:, t, at:at + w], sums(pr, t, g))]

        def ukv_pairs(pr, t, g):
            src = sums(pr, t, g).rearrange("p (h c) -> p h c", h=4)
            k = k_mla[:, t, :].rearrange("p (h c) -> p h c", h=MLA_H)[:, 4 * g:4 * g + 4, 0:HD]
            v = v_mla[:, t, 256 * g:256 * (g + 1)].rearrange("p (h c) -> p h c", h=4)
            return [(k, src[:, :, 0:HD]), (v, src[:, :, HD:])]

        def memkv_pairs(pr, t, g):
            return [(kvb[:, t, g * 512:(g + 1) * 512], sums(pr, t, g))]

        HEADS = {name: i + 1 for i, name in enumerate((
            "dil", "mla", "xk0", "xq0_0", "xq0_10", "xq0_11", "idx", "spa", "xk1", "xq1_0", "xq1_10", "xq1_11"))}
        CHUNKS = plan_chunks()

        block = ctx.enter_context(nc.Block())

        @block.sync
        def _(sp):
            def slot_free(n, i=None):
                if n >= RAW or i is not None:
                    sp.wait_ge(lo_done, val(max(1, n - RAW + 1), 12, i))
                    if i is not None:
                        sp.sem_inc(loader_turn, 1)

            def load_w13(l, n, c, g, i=None):
                src = ffn_w13[l].rearrange("(k p) (u f) -> p k u f", p=P, u=2)[:, 2 * g:2 * g + 2, :, :]
                col = val(c * CH, 2 * CH, i)
                dst = raw[:, n % RAW, :].rearrange("p (k u f) -> p k u f", k=2, u=2)
                slot_free(n, i)
                for u in range(2):
                    sp.dma_start(dst[:, :, u, :], src[:, :, u, bass.ds(col, CH)]).then_inc(unit_loaded[n % RAW], 16)

            def load_w2(l, n, c, b, i=None):
                slot_free(n, i)
                row = val(c * CH + b * P, 2 * CH, i)
                for h in range(2):
                    at = slice(h * 512, (h + 1) * 512)
                    sp.dma_start(raw[:, n % RAW, at], ffn_w2[l][bass.ds(row, P), at])\
                        .then_inc(unit_loaded[n % RAW], 16)

            def load_step(l, n, c, i=None):
                for g in range(4):
                    load_w13(l, n + g, c, g, i)
                for b in range(2):
                    load_w2(l, n + 4 + b, c - 1, b, i)

            def load_ffn(f):
                n = place[f"ffn{f}"]
                for g in range(4):
                    load_w13(f, n + g, 0, g)
                n += 4
                with sp.Fori(0, LOOPS) as i:
                    load_step(f, n, 1, i)
                    load_step(f, n + 6, 2, i)
                for c in range(1 + 2 * LOOPS, NCH):
                    load_step(f, n + 6 * (c - 1), c)
                for b in range(2):
                    load_w2(f, n + 6 * (NCH - 1) + b, NCH - 1, b)

            def load_projection(pr):
                w = weights[pr.name].rearrange("(k p) n -> p k n", p=P)
                n = pr.unit0
                if pr.wide:
                    slot_free(n)
                    for h in range(2):
                        at = slice(h * 512, (h + 1) * 512)
                        sp.dma_start(raw[:, n % RAW, at], w[:, 0, at]).then_inc(unit_loaded[n % RAW], 16)
                    return
                for at, width, pieces, pitch in pr.groups:
                    for u in range(pr.upg):
                        slot_free(n)
                        for k in range(2):
                            dst = raw[:, n % RAW, k * 512:k * 512 + width]
                            src = w[:, 2 * u + k, at:at + width]
                            if pieces > 1:
                                dst = dst.rearrange("p (i c) -> p i c", i=pieces)
                                src = w[:, 2 * u + k, at:at + pitch * pieces]\
                                    .rearrange("p (i c) -> p i c", i=pieces)[:, :, 0:width // pieces]
                            sp.dma_start(dst, src).then_inc(unit_loaded[n % RAW], 16)
                        n += 1

            for it in order:
                if isinstance(it, str):
                    load_ffn(int(it[3:]))
                else:
                    load_projection(it)
            for t in range(NT):
                sp.wait_ge(x_updated, X_UPDATES - NT + t + 1)
                sp.dma_start(y_out[t * P:(t + 1) * P, :], x[:, t, :]).then_inc(stored, 16)
            sp.wait_ge(stored, 16 * NT)

        @block.gpsimd
        def _(pool):
            nc.gpsimd.memset(minus_half[:, :], -0.5).then_inc(pool_step, 1)
            nc.gpsimd.memset(ident[:, :], 0.0).then_inc(pool_step, 1)
            nc.gpsimd.memset(causal[:, :], 0.0).then_inc(pool_step, 1)
            pool.wait_ge(pool_step, 3)
            nc.gpsimd.affine_select(out=ident[:, :], in_=ident[:, :], compare_op=ALU.not_equal, fill=1.0,
                                    base=0, pattern=[[-1, P]], channel_multiplier=1).then_inc(consts_made, 1)
            nc.gpsimd.memset(zeros[:, :], 0.0).then_inc(consts_made, 1)
            nc.gpsimd.memset(ident_b[:, :], 0.0).then_inc(pool_step, 1)
            nc.gpsimd.affine_select(out=causal[:, :], in_=causal[:, :], compare_op=ALU.is_ge, fill=NEG,
                                    base=P, pattern=[[-1, SEQ]], channel_multiplier=1).then_inc(consts_made, 1)
            nc.gpsimd.iota(pTb[:, 0:SEQ].bitcast(I32), pattern=[[-1, SEQ]], base=SEQ,
                           channel_multiplier=1).then_inc(consts_made, 1)
            pool.wait_ge(pool_step, 4)
            nc.gpsimd.affine_select(out=ident_b[:, :], in_=ident_b[:, :], compare_op=ALU.not_equal, fill=1.0,
                                    base=0, pattern=[[-1, P]], channel_multiplier=1).then_inc(pool_step, 1)
            pool.wait_ge(consts_made, 4)
            nc.gpsimd.affine_select(out=dil_mask[:, 0, :], in_=causal[:, :], compare_op=ALU.is_ge, fill=NEG,
                                    base=0, pattern=[[1, SEQ]], channel_multiplier=-1).then_inc(consts_made, 1)
            def serve(*names):
                for name in names:
                    i, c, w = rms[name]
                    pool.wait_ge(meansq_done, i + 1)
                    nc.gpsimd.tensor_tensor(rstd[:, c:c + w], meansq[:, c:c + w], minus_half[:, 0:w],
                                            ALU.pow).then_inc(rstd_done, 1)

            def both(name):
                return [f"{name}{t}" for t in range(NT)]

            def next_gain(n, name):
                pool.wait_ge(rows_ready, NT * (ROWS.index(name) + 1))
                pool.dma_start(gain[:, :], NORMS[n].to_broadcast([P, D])).then_inc(gain_loaded, 16)

            serve(*both("norm_ffn1_0_"))
            small = [(lora_gain[:, 0:Q_LORA], q_lora_norm.to_broadcast([P, Q_LORA])),
                      (lora_gain[:, Q_LORA:], kv_lora_norm.to_broadcast([P, KV_LORA])),
                      (nope_gain[:, 0, :], mla_q_gain[:, 0:HD].to_broadcast([P, HD])),
                      (nope_gain[:, 1, :], mla_k_gain[:, 0:HD].to_broadcast([P, HD])),
                      (head_gain[:, 0:ROPE], mla_q_gain[:, HD:].to_broadcast([P, ROPE])),
                      (head_gain[:, ROPE:2 * ROPE], mla_k_gain[:, HD:].to_broadcast([P, ROPE]))]
            small += [(head_gain[:, 64 + i * HD:64 + (i + 1) * HD], g.to_broadcast([P, HD]))
                      for i, g in enumerate((dil_q_gain, dil_k_gain, sparse_q_gain, sparse_k_gain))]
            assert len(small) == N_SMALL
            for dst, src in small:
                pool.dma_start(dst, src).then_inc(const_loaded, 16)

            for l in range(2):
                if l:
                    pool.wait_ge(out_read, TILE0["x0"] + len(X_TILES))
                for t in range(NT):
                    pool.dma_start(kvb[:, t, 0:D], mem_in[t * P:(t + 1) * P, :]).then_inc(mem_loaded[t], 16)
                pool.dma_start(x_gain[:, 0, :], xattn_q_gain[l:l + 1, :].to_broadcast([P, X_HD]))\
                    .then_inc(xgain_loaded, 16)
                pool.dma_start(x_gain[:, 1, :], xattn_k_gain[l:l + 1, :].to_broadcast([P, X_HD]))\
                    .then_inc(xgain_loaded, 16)
                if l:
                    serve(*both(f"norm_ffn1_{l}_"))
                next_gain(5 * l + 1, f"ffn{2 * l}")
                serve(*both(f"norm_mem_{l}_"))
                next_gain(5 * l + 2, f"memkv{l}")
                serve(*both(f"norm_mix_{l}_"))
                next_gain(5 * l + 3, ("even_in", "odd_in")[l])
                if l == 0:
                    for t in range(NT):
                        serve(f"lora_q{t}", f"lora_kv{t}")
                    serve(*[f"dil{g}_{t}" for g in range(3) for t in range(NT)])
                    for t in range(NT):
                        serve(f"mla_q{t}", f"mla_qr{t}", f"mla_k{t}", f"mla_kr{t}")
                else:
                    serve(*both("spa_k"), *both("spa_q0_"), *both("spa_q1_"))
                serve(*both(f"memk{l}_"))
                serve(*both(f"norm_x_{l}_"))
                next_gain(5 * l + 4, f"xq{l}")
                serve(*both(f"xq{l}_0"))
                serve(*both(f"xq{l}_1"))
                serve(*both(f"norm_ffn2_{l}_"))
                if l == 0:
                    next_gain(5, "ffn1")

        @block.scalar
        def _(act):
            done = [0]
            chunk = [0]
            tile = [0]
            warmed = [0]
            ends = [0, 0]

            def hi(n, i=None):
                act.wait_ge(unit_loaded[n % RAW], val(32 * (n // RAW + 1), 32 * 12 // RAW, i))
                if n >= SPLIT:
                    act.wait_ge(unit_used, val(n - SPLIT + 1, 12, i))
                nc.scalar.copy(w_hi[:, n % SPLIT, :], raw[:, n % RAW, :]).then_inc(hi_done, 1)

            def hi_until(n):
                while done[0] < min(n, UNITS):
                    hi(done[0])
                    done[0] += 1

            def square(name, src, junk, sem_, count):
                act.wait_ge(sem_, count)
                c = rms[name][1]
                nc.scalar.activation(junk, src, ACT.Square, accum_out=sumsq[:, c:c + 1]).then_inc(sumsq_done, 1)

            def square_heads(name, src, heads_, junk):
                c = rms[name][1]
                for h in range(heads_):
                    last = nc.scalar.activation(junk[h], src[:, h * X_HD:(h + 1) * X_HD], ACT.Square,
                                                accum_out=sumsq[:, c + h:c + h + 1])
                last.then_inc(sumsq_done, 1)

            def T_hi_tile(name, t):
                hi_, _ = T_dest(name)
                for c, t, b, nb in T_tile(name, t):
                    act.wait_ge(T_psum, c + 1)
                    nc.scalar.copy(hi_[:, b:b + nb, t * P:(t + 1) * P],
                                   SC[2 * t + b // 4][:, 0:nb * P].rearrange("p (b s) -> p b s", b=nb))\
                        .then_inc(T_hi, 1)

            def T_event(name):
                for t in range(NT):
                    T_hi_tile(name, t)

            def norm(rms_name, name, wait):
                for t in range(NT):
                    square(f"{rms_name}{t}", x[:, t, :], tm[:, t, :], *wait(t))
                    if t == 1:
                        hi_until(first_group(name))
                    T_hi_tile(name, t)
                    if t == 0:
                        hi_until(first_group(name) - 1)

            def silu(f, c, t, used, i=None):
                if t == 0 and i is None and (f"ffn{f}", c) in FIRST:
                    act.wait_ge(tile0_done, FIRST[f"ffn{f}", c])
                else:
                    act.wait_ge(unit_used, val(used, 12, i))
                nc.scalar.activation(silu_g[:, t, :], SC[t][:, 0:CH], ACT.Silu).then_inc(silu_done, 1)

            def gT_hi_step(f, c, i=None):
                act.wait_ge(gT_psum, val(GT_COUNT * f + c + 1, 2, i))
                nc.scalar.copy(gT_hi[:, 0:2, :], SC[2].rearrange("p (b s) -> p b s", b=2)).then_inc(gT_hi_done, 1)

            def gT_hi_last(f, t):
                act.wait_ge(gT_psum, GT_COUNT * f + NCH + t)
                nc.scalar.copy(act_hi[:, 0:2, t * P:(t + 1) * P],
                               SC[2 + t][:, 0:2 * P].rearrange("p (b s) -> p b s", b=2)).then_inc(gT_hi_done, 1)

            def ffn_step(f, n, c, i=None):
                gT_hi_step(f, c - 1, i)
                for u in range(6, 10):
                    hi(n + u, i)
                for t in range(NT):
                    silu(f, c, t, n + 4, i)
                for u in range(10, 12):
                    hi(n + u, i)

            def ffn_last(f, n):
                gT_hi_step(f, NCH - 2)
                silu(f, NCH - 1, 0, None)
                done[0] = n + 6
                hi_until(n + 9)
                silu(f, NCH - 1, 1, n + 4)
                gT_hi_last(f, 0)
                hi_until(n + 10)
                gT_hi_last(f, 1)

            def ffn(f):
                n = place[f"ffn{f}"]
                hi_until(n + 6)
                load_table(ACT.Silu)
                silu(f, 0, 0, None)
                hi_until(n + 9)
                silu(f, 0, 1, n + 4)
                hi_until(n + 10)
                if f % 2 == 0:
                    for t in range(NT):
                        square(f"norm_mem_{f // 2}_{t}", kvb[:, t, 0:D], kvb[:, t, D:2 * D], mem_loaded[t],
                               16 * (f // 2 + 1))
                n += 4
                with act.Fori(0, LOOPS) as i:
                    ffn_step(f, n, 1, i)
                    ffn_step(f, n + 6, 2, i)
                for c in range(1 + 2 * LOOPS, NCH - 1):
                    ffn_step(f, n + 6 * (c - 1), c)
                ffn_last(f, n + 6 * (NCH - 2))

            def project(pr, dst=None, after=None, before={}, ahead=SPLIT):
                for g in range(len(pr.groups)):
                    if g in before:
                        before[g]()
                    hi_until(pr.end(g) + 2)
                    for t in range(NT):
                        if dst is None:
                            continue
                        last_group = g == len(pr.groups) - 1
                        if g not in pr.tiled:
                            hi_until(pr.end(g) + (min(3, ahead) if last_group else 3))
                        elif t == NT - 1:
                            hi_until(pr.end(g) + (min(4, ahead) if last_group or pr.upg < 4 else 4))
                        if t == 0 and g in pr.tiled:
                            act.wait_ge(tile0_done, FIRST[pr.name, g])
                        else:
                            act.wait_ge(unit_used, pr.end(g))
                        for o, i_ in dst(pr, t, g):
                            last = nc.scalar.copy(o, i_)
                        last.then_inc(group_out[t], 1)
                        if after is not None:
                            act.wait_ge(group_out[t], pr.group0 + g + 1)
                            after(g, t)
                hi_until(pr.end(len(pr.groups) - 1) + (ahead if dst is not None else SPLIT - pr.upg))

            def move_chunks(chunks):
                for srcs, dst in chunks:
                    c = chunk[0]
                    if CHUNKS[c][0] == 1:
                        act.wait_ge(chunk_psum, c + 1)
                        n, rows = len(srcs), srcs[0].shape[1]
                        nc.scalar.copy(dst, CHUNKS[c][2][0:rows, 0:n * P].rearrange("p (b s) -> p b s", b=n))\
                            .then_inc(chunk_out[1], 1)
                    chunk[0] += 1

            def attend(tiles, spare):
                for tl in tiles:
                    a = tile[0]
                    act.wait_ge(max_ready, a + 1)
                    if ends[0]:
                        act.wait_ge(chunk_psum, ends[0])
                    ends[0], ends[1] = ends[1], chunk[0] + sum(1 for _ in prob_chunks(tl, a))
                    for r in range(tl.rows):
                        at = 1024 * (a % 2) + r * tl.width
                        s = 1024 * (a % 2) + r * tl.pitch
                        last = nc.scalar.activation(scb[:, at:at + tl.width], low[:, s:s + tl.width], ACT.Exp,
                                                    bias=negmax[:, a % 4, r:r + 1], scale=tl.scale,
                                                    accum_out=den[:, a % 4, r:r + 1])
                    last.then_inc(probs_ready, 1)
                    move_chunks(prob_chunks(tl, a))
                    next(spare, None)
                    tile[0] += 1

            def load_table(function):
                nc.scalar.activation(warm[:, warmed[0]:warmed[0] + 1], minus_half[:, 0:1], function)
                warmed[0] += 1

            def spare_steps(memkv):
                junk = [g[:, i, :] for g in (gT_hi, gT_lo) for i in range(3)] + [scr_a[:, 0:X_HD], scr_b[:, 0:X_HD]]
                steps_ = hi_steps(memkv.end(3) + SPLIT)
                for t in range(NT):
                    yield next(steps_, None)
                    square_heads(f"memk{l}_{t}", kvb[:, t, 0:D], X_H, junk[X_H * t:])
                    yield
                yield from steps_

            def hi_steps(ahead):
                while done[0] < ahead:
                    hi_until(done[0] + 1)
                    yield

            def update_wait(pr):
                return lambda t: (group_out[t], pr.group0 + len(pr.groups))

            for t in range(NT):
                act.dma_start(x[:, t, :], x_in[t * P:(t + 1) * P, :]).then_inc(x_loaded[t], 16)
            act.dma_start(gain[:, :], NORMS[0].to_broadcast([P, D])).then_inc(first_gain_loaded, 16)
            for t in range(NT):
                act.dma_start(pos_i[:, t:t + 1], positions[0:1, t * P:(t + 1) * P].rearrange("o p -> p o"))\
                    .then_inc(rope_loaded, 16)
            act.dma_start(freq[:, :], rope_freq[0:1, :].to_broadcast([P, 48])).then_inc(rope_loaded, 16)
            for t in range(NT):
                square(f"norm_ffn1_0_{t}", x[:, t, :], tm[:, t, :], x_loaded[t], 16)
            hi_until(2)
            T_hi_tile("ffn0", 0)
            hi_until(4)
            T_hi_tile("ffn0", 1)
            act.wait_ge(angle_ready, 1)
            nc.scalar.activation(sines[:, :, :, :], angle[:, :, :, :], ACT.Sin).then_inc(sin_ready, 1)
            for l in range(2):
                if l:
                    norm(f"norm_ffn1_{l}_", "ffn2", lambda t: (x_updated, (2 * l - 1) * NT + t + 1))
                ffn(2 * l)
                mixer_in = place[("even_in", "odd_in")[l]]
                mixer_out = place[("even_out", "odd_out")[l]]
                memkv, xq, xo = place[f"memkv{l}"], place[f"xq{l}"], place[f"xo{l}"]
                norm(f"norm_mix_{l}_", mixer_in.name, lambda t: (x_updated, 2 * l * NT + t + 1))
                if l == 0:
                    def square_dilated(g, t):
                        if 1 <= g <= 3:
                            if g == 3:
                                act.wait_ge(meansq_done, rms["dil0_1"][0] + 1)
                            nc.scalar.activation(square_place(g - 1, t), cols[:, t, DIL0 + 768 * (g - 1):][:, 0:512],
                                                 ACT.Square).then_inc(squares_ready, 1)

                    project(mixer_in, cols_pairs, after=square_dilated, before={LORA_AT: lambda: T_event("lora")})
                    T_event(memkv.name)
                    project(place["uq"], uq_pairs)
                    for t in range(NT):
                        act.wait_ge(group_out[t], place["uq"].group0 + 2)
                        nc.scalar.activation(mla_q_squares[:, t, :], q_mla[:, t, :], ACT.Square)\
                            .then_inc(squares_ready, 1)
                    project(place["ukv"], ukv_pairs)
                    for t in range(NT):
                        act.wait_ge(group_out[t], place["ukv"].group0 + 2)
                        nc.scalar.activation(mla_k_squares[:, t, :].rearrange("p (h e) -> p h e", h=MLA_H),
                                             k_mla[:, t, :].rearrange("p (h c) -> p h c", h=MLA_H)[:, :, 0:HD],
                                             ACT.Square).then_inc(squares_ready, 1)
                    project(memkv, memkv_pairs, ahead=2)
                    spare = spare_steps(memkv)
                    move_chunks(mla_chunks())
                    load_table(ACT.Exp)
                    attend(MLA_TILES, spare)
                    move_chunks(dil_chunks())
                    attend(DIL_TILES, spare)
                else:
                    def relu(qt):
                        keys = P * (qt + 1)
                        act.wait_ge(logits_ready, qt + 1)
                        nc.scalar.activation(relu_of(qt)[:, 0:IDX_H * keys], logits_of(qt), ACT.Relu,
                                             scale=HD ** -0.5).then_inc(relu_done, 1)

                    def square_sparse(g, t):
                        if g >= 2:
                            nc.scalar.activation(square_place(g - 2, t), cols[:, t, (g - 2) * 512:(g - 1) * 512],
                                                 ACT.Square).then_inc(squares_ready, 1)

                    project(mixer_in, cols_pairs, after=square_sparse, before={3: lambda: move_chunks(idx_chunks())})
                    T_hi_tile(memkv.name, 0)
                    relu(0)
                    T_hi_tile(memkv.name, 1)
                    project(memkv, memkv_pairs, before={1: lambda: relu(1)}, ahead=2)
                    move_chunks(spa_chunks())
                    load_table(ACT.Exp)
                    attend(SPA_TILES, spare_steps(memkv))
                T_event(mixer_out.name)
                project(mixer_out)
                norm(f"norm_x_{l}_", xq.name, update_wait(mixer_out))

                def square_queries(g, t):
                    square_heads(f"xq{l}_{g}{t}", cols[:, t, g * 512:(g + 1) * 512], 2,
                                 [tm[:, t, (2 * g + h) * X_HD:(2 * g + h + 1) * X_HD] for h in range(2)])

                project(xq, cols_pairs, after=square_queries, before={1: lambda: move_chunks(x_chunks("k"))}, ahead=2)
                move_chunks(x_chunks("q"))
                load_table(ACT.Exp)
                attend(X_TILES, hi_steps(xq.end(1) + SPLIT))
                T_event(xo.name)
                project(xo)
                norm(f"norm_ffn2_{l}_", f"ffn{2 * l + 1}", update_wait(xo))
                ffn(2 * l + 1)

        @block.vector
        def _(dve):
            done = [0]
            chunk = [0]
            tile = [0]
            steps = [0]
            row_events = [0]
            rms_events = [0]
            square_events = [0]

            def link(ins):
                steps[0] += 1
                ins.then_inc(dve_step, 1)
                dve.wait_ge(dve_step, steps[0])

            def lo(n, i=None):
                dve.wait_ge(hi_done, val(n + 1, 12, i))
                nc.vector.tensor_tensor(w_lo[:, n % SPLIT, :], raw[:, n % RAW, :],
                                        w_hi[:, n % SPLIT, :].bitcast(F32), ALU.subtract).then_inc(lo_done, 1)

            def lo_until(n):
                while done[0] < min(n, UNITS):
                    lo(done[0])
                    done[0] += 1

            def mean_square(name, width):
                i, c, w = rms[name]
                assert i == rms_events[0], name
                rms_events[0] += 1
                nc.vector.tensor_scalar(meansq[:, c:c + w], sumsq[:, c:c + w], 1.0 / width, EPS, ALU.mult,
                                        ALU.add).then_inc(meansq_done, 1)

            def rstd_of(name):
                i, c, w = rms[name]
                dve.wait_ge(rstd_done, i + 1)
                return rstd[:, c:c + w]

            def row_mean(name, t):
                square_events[0] += 1
                dve.wait_ge(sumsq_done, square_events[0])
                mean_square(f"{name}{t}", D)

            def norm_row(name, t, gains, src, dst):
                if gains == 1:
                    dve.wait_ge(first_gain_loaded, 16)
                else:
                    dve.wait_ge(gain_loaded, 16 * (gains - 1))
                nc.vector.scalar_tensor_tensor(out=dst[:, t, 0:D], in0=src[:, t, 0:D], scalar=rstd_of(f"{name}{t}"),
                                               in1=gain[:, :], op0=ALU.mult, op1=ALU.mult).then_inc(rows_ready, 1)

            def T_lo_tile(name, t):
                hi_, lo_ = T_dest(name)
                for c, t, b, nb in T_tile(name, t):
                    dve.wait_ge(T_hi, c + 1)
                    at = slice(t * P, (t + 1) * P)
                    nc.vector.tensor_tensor(lo_[:, b:b + nb, at],
                                            SC[2 * t + b // 4][:, 0:nb * P].rearrange("p (b s) -> p b s", b=nb),
                                            hi_[:, b:b + nb, at].bitcast(F32), ALU.subtract).then_inc(T_split, 1)

            def T_event(name):
                for t in range(NT):
                    T_lo_tile(name, t)

            def norm(rms_name, name, gains, update, updated):
                update(0)
                row_mean(rms_name, 0)
                dve.wait_ge(*updated(0))
                norm_row(rms_name, 0, gains, x, tm)
                update(1)
                T_lo_tile(name, 0)
                lo_until(first_group(name) - 1)
                row_mean(rms_name, 1)
                lo_until(first_group(name))
                dve.wait_ge(*updated(1))
                norm_row(rms_name, 1, gains, x, tm)
                T_lo_tile(name, 1)

            def gate(f, c, t, i=None):
                dve.wait_ge(silu_done, val(NT * (NCH * f + c) + t + 1, 2 * NT, i))
                nc.vector.tensor_tensor(gated[:, t, :], silu_g[:, t, :], SC[t][:, CH:2 * CH], ALU.mult)\
                    .then_inc(gated_done, 1)

            def gT_lo_step(f, c, i=None):
                dve.wait_ge(gT_hi_done, val(GT_COUNT * f + c + 1, 2, i))
                nc.vector.tensor_tensor(gT_lo[:, 0:2, :], SC[2].rearrange("p (b s) -> p b s", b=2),
                                        gT_hi[:, 0:2, :].bitcast(F32), ALU.subtract).then_inc(gT_split, 1)

            def gT_lo_last(f, t):
                dve.wait_ge(gT_hi_done, GT_COUNT * f + NCH + t)
                at = slice(t * P, (t + 1) * P)
                nc.vector.tensor_tensor(act_lo[:, 0:2, at],
                                        SC[2 + t][:, 0:2 * P].rearrange("p (b s) -> p b s", b=2),
                                        act_hi[:, 0:2, at].bitcast(F32), ALU.subtract).then_inc(gT_split, 1)

            def ffn_step(f, n, c, i=None):
                gT_lo_step(f, c - 1, i)
                for u in range(6, 10):
                    lo(n + u, i)
                for t in range(NT):
                    gate(f, c, t, i)
                for u in range(10, 12):
                    lo(n + u, i)

            def ffn_last(f, n):
                gT_lo_step(f, NCH - 2)
                gate(f, NCH - 1, 0)
                done[0] = n + 6
                lo_until(n + 9)
                gate(f, NCH - 1, 1)
                gT_lo_last(f, 0)
                lo_until(n + 10)
                gT_lo_last(f, 1)

            def ffn(f):
                n = place[f"ffn{f}"]
                lo_until(n + 6)
                gate(f, 0, 0)
                lo_until(n + 9)
                gate(f, 0, 1)
                lo_until(n + 10)
                if f % 2 == 0:
                    for t in range(NT):
                        row_mean(f"norm_mem_{f // 2}_", t)
                    for t in range(NT):
                        norm_row(f"norm_mem_{f // 2}_", t, 5 * (f // 2) + 2, kvb, kvb)
                n += 4
                with dve.Fori(0, LOOPS) as i:
                    ffn_step(f, n, 1, i)
                    ffn_step(f, n + 6, 2, i)
                for c in range(1 + 2 * LOOPS, NCH - 1):
                    ffn_step(f, n + 6 * (c - 1), c)
                if f == 0:
                    rope_tables()
                ffn_last(f, n + 6 * (NCH - 2))

            def ffn_update(f):
                def update(t):
                    if t == 0:
                        dve.wait_ge(ffn_sum, f + 1)
                    else:
                        dve.wait_ge(unit_used, place[f"ffn{f}"] + 6 * NCH)
                    for h in range(2):
                        xs = x[:, t, h * 512:(h + 1) * 512]
                        last = nc.vector.scalar_tensor_tensor(out=xs, in0=acc(t, h), scalar=0.5, in1=xs,
                                                              op0=ALU.mult, op1=ALU.add)
                    last.then_inc(x_updated, 1)
                return update

            def project_lo(limit):
                while done[0] < min(limit, UNITS):
                    lo_until(done[0] + 1)
                    yield

            def lo_of(pr, ahead=SPLIT):
                return project_lo(pr.end(len(pr.groups) - 1) + ahead)

            def run(steps_):
                for _ in steps_:
                    pass

            def half_update(pr, g, t):
                if t == 0:
                    dve.wait_ge(tile0_done, FIRST[pr.name, g])
                else:
                    dve.wait_ge(unit_used, pr.end(g))
                xs = x[:, t, g * 512:(g + 1) * 512]
                nc.vector.tensor_tensor(xs, sums(pr, t, g), xs, ALU.add).then_inc(group_out[t], 1)

            def project_update(pr):
                lo_until(pr.end(0) + 2)
                half_update(pr, 0, 0)
                lo_until(pr.end(0) + 3)
                half_update(pr, 0, 1)
                lo_until(pr.end(1))

                def update(t):
                    half_update(pr, 1, t)
                    if t == 0:
                        lo_until(pr.end(1) + 2)
                return update

            def update_wait(pr):
                return lambda t: (group_out[t], pr.group0 + len(pr.groups))

            def groups_out(pr, g):
                for t in range(NT):
                    dve.wait_ge(group_out[t], pr.group0 + g + 1)

            def head_squares(name, src, width):
                h = src.shape[1]
                sq = scr_a[:, 0:h * width].rearrange("p (h e) -> p h e", h=h)
                i, c, w = rms[name]
                link(nc.vector.tensor_tensor(sq, src, src, ALU.mult))
                link(nc.vector.tensor_reduce(sumsq[:, c:c + w], sq, AX, ALU.add))
                mean_square(name, width)

            def squared_heads(name, squares, width, event):
                i, c, w = rms[name]
                dve.wait_ge(squares_ready, event)
                link(nc.vector.tensor_reduce(sumsq[:, c:c + w], squares, AX, ALU.add))
                mean_square(name, width)

            def scale_heads(name, v):
                r = rstd_of(name)
                return nc.vector.tensor_tensor(v, v, r.unsqueeze(2).to_broadcast(list(v.shape)), ALU.mult)

            def rotate(v, c, s):
                shape = list(v.shape)
                e = shape[-1]
                size = int(np.prod(shape[1:]))
                names = {3: "p (a e) -> p a e", 4: "p (a b e) -> p a b e"}[len(shape)]
                kw = {3: dict(a=shape[1]), 4: dict(a=shape[1], b=shape[2] if len(shape) > 3 else 1)}[len(shape)]
                va = scr_a[:, 0:size].rearrange(names, **kw)
                vb = scr_b[:, 0:size].rearrange(names, **kw)
                nc.vector.tensor_tensor(va, v, c, ALU.mult)
                nc.vector.tensor_tensor(vb[..., 0:e // 2], v[..., e // 2:], s[..., 0:e // 2], ALU.mult)
                link(nc.vector.tensor_tensor(vb[..., e // 2:], v[..., 0:e // 2], s[..., e // 2:], ALU.mult))
                link(nc.vector.tensor_tensor(v, va, vb, ALU.add))

            def over_heads(table, h):
                return table.unsqueeze(1).to_broadcast([P, h, table.shape[-1]])

            def move_chunks(chunks):
                for srcs, dst in chunks:
                    c = chunk[0]
                    if CHUNKS[c][0] == 0:
                        dve.wait_ge(chunk_psum, c + 1)
                        n, rows = len(srcs), srcs[0].shape[1]
                        nc.vector.tensor_copy(dst, CHUNKS[c][2][0:rows, 0:n * P].rearrange("p (b s) -> p b s", b=n))\
                            .then_inc(chunk_out[0], 1)
                    chunk[0] += 1

            def row_max(tl, a):
                dve.wait_ge(scores_ready, a + 1)
                s = low[:, 1024 * (a % 2):1024 * (a % 2) + tl.rows * tl.pitch]
                link(nc.vector.tensor_reduce(rowmax[:, a % 2, 0:tl.rows],
                                             s.rearrange("p (r w) -> p r w", r=tl.rows)[:, :, 0:tl.width],
                                             AX, ALU.max))
                nc.vector.tensor_scalar(negmax[:, a % 4, 0:tl.rows], rowmax[:, a % 2, 0:tl.rows], -tl.scale, None,
                                        ALU.mult).then_inc(max_ready, 1)

            def normalise(tl, a):
                dve.wait_ge(probs_ready, a + 1)
                link(nc.vector.reciprocal(rden[:, a % 2, 0:tl.rows], den[:, a % 4, 0:tl.rows]))
                dve.wait_ge(out_ready, a + 1)
                n = tl.rows * tl.out
                at = (MLA_H * HD if tl.kind == "dil" else 0) + tl.first * tl.out
                two = 2 if tl.kind == "spa" else 1
                form = dict(j=two, q=tl.rows // two)
                r = rden[:, a % 2, 0:tl.rows].rearrange("p (j q) -> p q j", **form).unsqueeze(3)
                nc.vector.tensor_tensor(
                    tm[:, tl.qt, at:at + n].rearrange("p (q j e) -> p q j e", **form),
                    OB[a % 2][:, 0:n].rearrange("p (q j e) -> p q j e", **form),
                    r.to_broadcast([P, tl.rows // two, two, tl.out]), ALU.mult).then_inc(out_read, 1)

            def attend(tiles, spare):
                first = tile[0]
                row_max(tiles[0], first)
                row_max(tiles[1], first + 1)
                for j, tl in enumerate(tiles):
                    move_chunks(prob_chunks(tl, first + j))
                    if j:
                        normalise(tiles[j - 1], first + j - 1)
                    if j + 2 < len(tiles):
                        row_max(tiles[j + 2], first + j + 2)
                    if j + 1 < len(tiles):
                        next(spare, None)
                normalise(tiles[-1], first + len(tiles) - 1)
                tile[0] = first + len(tiles)

            def spare_steps(memkv):
                steps_ = project_lo(memkv.end(3) + SPLIT)
                for t in range(NT):
                    yield next(steps_, None)
                    wide_mean(f"memk{l}_{t}")
                    yield
                yield from steps_
                dve.wait_ge(xgain_loaded, 32 * (l + 1))
                for t in range(NT):
                    for h in range(0, X_H, 2):
                        last = wide_heads(f"memk{l}_{t}", kvb[:, t, 0:D], 1, h, 2)
                        if (t, h) == (NT - 1, X_H - 2):
                            last.then_inc(heads_ready, 1)
                        yield

            def dilated_masks():
                dve.wait_ge(consts_made, 5)
                off = pTb[:, 0:SEQ].bitcast(I32)
                for g, dilation in ((1, 4), (2, 16)):
                    rest = scr_a[:, 0:SEQ].bitcast(I32)
                    link(nc.vector.tensor_scalar(rest, off, dilation - 1, None, ALU.bitwise_and))
                    link(nc.vector.tensor_scalar(scr_b[:, 0:SEQ], rest, 0.0, NEG, ALU.is_gt, ALU.mult))
                    link(nc.vector.tensor_tensor(dil_mask[:, g, :], scr_b[:, 0:SEQ], causal[:, :], ALU.add))

            def angles():
                dve.wait_ge(rope_loaded, 16 * (NT + 1))
                link(nc.vector.tensor_copy(pos_f[:, :], pos_i[:, :]))
                product = scr_a[:, 0:48 * NT].rearrange("p (t f) -> p t f", t=NT)
                turns = scr_b[:, 0:48 * NT].rearrange("p (t f) -> p t f", t=NT)
                for t in range(NT):
                    ins = nc.vector.tensor_scalar(product[:, t, :], freq[:, :], pos_f[:, t:t + 1], None, ALU.mult)
                link(ins)
                for j, quarter in ((0, 0.25), (1, 0.0)):
                    a = angle[:, j, :, :]
                    link(nc.vector.tensor_scalar(turns, product, 1 / (2 * math.pi), quarter, ALU.mult, ALU.add))
                    link(nc.vector.tensor_scalar(turns, turns, ROUND, None, ALU.add))
                    link(nc.vector.tensor_scalar(turns, turns, ROUND, None, ALU.subtract))
                    link(nc.vector.scalar_tensor_tensor(out=a, in0=turns, scalar=-C1, in1=product,
                                                        op0=ALU.mult, op1=ALU.add))
                    link(nc.vector.scalar_tensor_tensor(out=a, in0=turns, scalar=-C2, in1=a,
                                                        op0=ALU.mult, op1=ALU.add))
                    link(nc.vector.scalar_tensor_tensor(out=a, in0=turns, scalar=-C3, in1=a,
                                                        op0=ALU.mult, op1=ALU.add))
                    if quarter:
                        link(nc.vector.tensor_scalar(a, a, math.pi / 2, None, ALU.add))
                    last = nc.vector.tensor_scalar(a, a, 3.1415925, -3.1415925, ALU.min, ALU.max)
                    if quarter:
                        link(last)
                last.then_inc(angle_ready, 1)

            def rope_tables():
                dve.wait_ge(sin_ready, 1)
                dve.wait_ge(const_loaded, 16 * N_SMALL)
                for t in range(NT):
                    cos, sin = sines[:, 0, t, :], sines[:, 1, t, :]
                    for h in range(2):
                        nc.vector.tensor_copy(rc64[:, t, h * 32:(h + 1) * 32], cos[:, 0:32])
                        nc.vector.tensor_scalar(rs64[:, t, h * 32:(h + 1) * 32], sin[:, 0:32], 2.0 * h - 1, None,
                                                ALU.mult)
                        nc.vector.tensor_copy(scr_a[:, h * 16:(h + 1) * 16], cos[:, 32:48])
                        last = nc.vector.tensor_scalar(scr_b[:, h * 16:(h + 1) * 16], sin[:, 32:48], 2.0 * h - 1,
                                                       None, ALU.mult)
                    link(last)
                    for j in range(2):
                        g = head_gain[:, j * ROPE:(j + 1) * ROPE]
                        nc.vector.tensor_tensor(gc32[:, t, j, :], scr_a[:, 0:32], g, ALU.mult)
                        nc.vector.tensor_tensor(gs32[:, t, j, 0:16], scr_b[:, 0:16], g[:, 16:], ALU.mult)
                        nc.vector.tensor_tensor(gs32[:, t, j, 16:], scr_b[:, 16:32], g[:, 0:16], ALU.mult)
                    for j in range(4):
                        g = head_gain[:, 64 + j * HD:64 + (j + 1) * HD]
                        nc.vector.tensor_tensor(gc64[:, t, j, :], rc64[:, t, :], g, ALU.mult)
                        nc.vector.tensor_tensor(gs64[:, t, j, 0:32], rs64[:, t, 0:32], g[:, 32:], ALU.mult)
                        last = nc.vector.tensor_tensor(gs64[:, t, j, 32:], rs64[:, t, 32:], g[:, 0:32], ALU.mult)
                    link(last)

            def heads(v, h):
                return v.rearrange("p (h e) -> p h e", h=h)

            def lora_rows():
                for t in range(NT):
                    for name, at, w in (("lora_q", 0, Q_LORA), ("lora_kv", Q_LORA, KV_LORA)):
                        head_squares(f"{name}{t}", cols[:, t, at:at + w].unsqueeze(1), w)
                for t in range(NT):
                    for name, at, w in (("lora_q", 0, Q_LORA), ("lora_kv", Q_LORA, KV_LORA)):
                        last = nc.vector.scalar_tensor_tensor(out=tm[:, t, at:at + w], in0=cols[:, t, at:at + w],
                                                              scalar=rstd_of(f"{name}{t}"),
                                                              in1=lora_gain[:, at:at + w], op0=ALU.mult, op1=ALU.mult)
                    last.then_inc(rows_ready, 1)

            def mla_heads(pump):
                for t in range(NT):
                    q = heads(q_mla[:, t, :], MLA_H)
                    k = heads(k_mla[:, t, :], MLA_H)
                    kr = cols[:, t, Q_LORA + KV_LORA:DIL0].unsqueeze(1)
                    q2 = heads(mla_q_squares[:, t, :], MLA_H)
                    squared_heads(f"mla_q{t}", q2[:, :, 0:HD], HD, 3 * NT + t + 1)
                    squared_heads(f"mla_qr{t}", q2[:, :, HD:], ROPE, 3 * NT + t + 1)
                    next(pump, None)
                    squared_heads(f"mla_k{t}", heads(mla_k_squares[:, t, :], MLA_H), HD, 4 * NT + t + 1)
                    head_squares(f"mla_kr{t}", kr, ROPE)
                    next(pump, None)
                    rotate(q[:, :, HD:], over_heads(gc32[:, t, 0, :], MLA_H), over_heads(gs32[:, t, 0, :], MLA_H))
                    next(pump, None)
                    rotate(kr, over_heads(gc32[:, t, 1, :], 1), over_heads(gs32[:, t, 1, :], 1))
                    scale_heads(f"mla_q{t}", q[:, :, 0:HD])
                    scale_heads(f"mla_qr{t}", q[:, :, HD:])
                    scale_heads(f"mla_k{t}", k[:, :, 0:HD])
                    link(scale_heads(f"mla_kr{t}", kr))
                    next(pump, None)
                    nc.vector.tensor_tensor(q[:, :, 0:HD], q[:, :, 0:HD], over_heads(nope_gain[:, 0, :], MLA_H),
                                            ALU.mult)
                    nc.vector.tensor_tensor(k[:, :, 0:HD], k[:, :, 0:HD], over_heads(nope_gain[:, 1, :], MLA_H),
                                            ALU.mult)
                    last = nc.vector.tensor_copy(k[:, :, HD:], kr.to_broadcast([P, MLA_H, ROPE]))
                    next(pump, None)
                last.then_inc(heads_ready, 1)

            def dil_heads(g, pump):
                for t in range(NT):
                    squared_heads(f"dil{g}_{t}", heads(square_place(g, t), 8), HD, NT * g + t + 1)
                    next(pump, None)
                for t in range(NT):
                    v = dil_cols(t)[:, g, 0:8, :]
                    rotate(v.rearrange("p (j h) e -> p j h e", j=2),
                           gc64[:, t, 0:2, :].unsqueeze(2).to_broadcast([P, 2, 4, HD]),
                           gs64[:, t, 0:2, :].unsqueeze(2).to_broadcast([P, 2, 4, HD]))
                    last = scale_heads(f"dil{g}_{t}", v)
                    next(pump, None)
                if g == 2:
                    last.then_inc(heads_ready, 1)

            def idx_heads():
                for t in range(NT):
                    qi = heads(cols[:, t, 1152:1664], IDX_H)
                    ki = cols[:, t, 1664:1728].unsqueeze(1)
                    rotate(qi, over_heads(rc64[:, t, :], IDX_H), over_heads(rs64[:, t, :], IDX_H))
                    rotate(ki, over_heads(rc64[:, t, :], 1), over_heads(rs64[:, t, :], 1))
                    nc.vector.tensor_copy(twin[:, t, P:2 * P].rearrange("p (j e) -> p j e", j=2),
                                          ki.to_broadcast([P, 2, HD]))
                    last = nc.vector.tensor_scalar(w_idx[:, t, :], cols[:, t, 1728:1736], IDX_H ** -0.5, None,
                                                   ALU.mult)
                last.then_inc(heads_ready, 1)

            def spa_keys():
                for t in range(NT):
                    head_squares(f"spa_k{t}", cols[:, t, 1024:1088].unsqueeze(1), HD)
                for t in range(NT):
                    k = cols[:, t, 1024:1088].unsqueeze(1)
                    rotate(k, over_heads(gc64[:, t, 3, :], 1), over_heads(gs64[:, t, 3, :], 1))
                    link(scale_heads(f"spa_k{t}", k))
                    nc.vector.tensor_copy(twin[:, t, 0:P].rearrange("p (j e) -> p j e", j=2),
                                          k.to_broadcast([P, 2, HD]))

            def spa_squares(j, pump):
                for t in range(NT):
                    squared_heads(f"spa_q{j}_{t}", heads(square_place(j, t), 8), HD, NT * (5 + j) + t + 1)
                    next(pump, None)

            def spa_rotated(j, t):
                q = heads(cols[:, t, j * 512:(j + 1) * 512], 8)
                rotate(q, over_heads(gc64[:, t, 2, :], 8), over_heads(gs64[:, t, 2, :], 8))
                last = scale_heads(f"spa_q{j}_{t}", q)
                if (j, t) == (1, 1):
                    last.then_inc(heads_ready, 1)

            def wide_mean(name):
                square_events[0] += 1
                dve.wait_ge(sumsq_done, square_events[0])
                mean_square(name, X_HD)

            def wide_heads(name, v, j, first=0, count=2):
                r = rstd_of(name)
                for h in range(first, first + count):
                    at = v[:, h * X_HD:(h + 1) * X_HD]
                    last = nc.vector.scalar_tensor_tensor(out=at, in0=at, scalar=r[:, h:h + 1],
                                                          in1=x_gain[:, j, :], op0=ALU.mult, op1=ALU.mult)
                return last

            def select_keys(pump):
                for t in range(NT):
                    keys = P * (t + 1)
                    s, l_ = score[:, t, 0:keys], left[:, t, 0:keys]
                    relu = relu_of(t)
                    dve.wait_ge(relu_done, t + 1)
                    link(nc.vector.tensor_scalar(s, relu[:, 0:keys], w_idx[:, t, 0:1], 0.0, ALU.mult, ALU.add))
                    for r in range(1, IDX_H):
                        h = half_first(r)
                        ins = nc.vector.scalar_tensor_tensor(out=s, in0=relu[:, r * keys:(r + 1) * keys],
                                                             scalar=w_idx[:, t, h:h + 1], in1=s,
                                                             op0=ALU.mult, op1=ALU.add)
                        link(ins)
                    link(nc.vector.tensor_tensor(s, s, causal[:, SEQ - keys:], ALU.add))
                    for n in range(TOPK // 8):
                        have = s if n == 0 else l_
                        link(nc.vector.max(top8[:, :], have))
                        link(nc.vector.match_replace(l_, top8[:, :], have, TAKEN))
                        if n % 3 == 2:
                            next(pump, None)
                    link(nc.vector.tensor_scalar(l_, l_, -1e38, NEG, ALU.is_gt, ALU.mult))
                    last = nc.vector.tensor_tensor(sel_mask[:, t, 0:keys], l_, causal[:, SEQ - keys:], ALU.add)
                    next(pump, None)
                last.then_inc(selected, 1)

            dilated_masks()
            for t in range(NT):
                row_mean("norm_ffn1_0_", t)
                norm_row("norm_ffn1_0_", t, 1, x, tm)
            lo_until(2)
            T_lo_tile("ffn0", 0)
            lo_until(4)
            angles()
            T_lo_tile("ffn0", 1)
            for l in range(2):
                if l:
                    norm(f"norm_ffn1_{l}_", "ffn2", 5 * l + 1, ffn_update(1), lambda t: (x_updated, NT + t + 1))
                ffn(2 * l)
                mixer_in = place[("even_in", "odd_in")[l]]
                mixer_out = place[("even_out", "odd_out")[l]]
                memkv, xq, xo = place[f"memkv{l}"], place[f"xq{l}"], place[f"xo{l}"]
                norm(f"norm_mix_{l}_", mixer_in.name, 5 * l + 3, ffn_update(2 * l),
                     lambda t: (x_updated, 2 * l * NT + t + 1))
                pump = lo_of(mixer_in)
                if l == 0:
                    run(project_lo(mixer_in.end(0) + 4))
                    groups_out(mixer_in, 0)
                    lora_rows()
                    for g in range(3):
                        run(project_lo(mixer_in.end(g + 1) + 3))
                        groups_out(mixer_in, g + 1)
                        if g == 2:
                            T_event("lora")
                        dil_heads(g, pump)
                    run(pump)
                    T_event(memkv.name)
                    run(lo_of(place["uq"]))
                    run(lo_of(place["ukv"]))
                    groups_out(place["ukv"], 1)
                    pump = lo_of(memkv, 2)
                    mla_heads(pump)
                    run(pump)
                    spare = spare_steps(memkv)
                    move_chunks(mla_chunks())
                    attend(MLA_TILES, spare)
                    move_chunks(dil_chunks())
                    attend(DIL_TILES, spare)
                else:
                    run(project_lo(mixer_in.end(1) + 3))
                    groups_out(mixer_in, 1)
                    idx_heads()
                    next(pump, None)
                    next(pump, None)
                    spa_keys()
                    run(project_lo(mixer_in.end(2) + 3))
                    move_chunks(idx_chunks())
                    groups_out(mixer_in, 2)
                    spa_squares(0, pump)
                    spa_rotated(0, 0)
                    run(pump)
                    T_lo_tile(memkv.name, 0)
                    spa_rotated(0, 1)
                    T_lo_tile(memkv.name, 1)
                    pump = lo_of(memkv, 2)
                    groups_out(mixer_in, 3)
                    spa_squares(1, pump)
                    for t in range(NT):
                        spa_rotated(1, t)
                        next(pump, None)
                    select_keys(pump)
                    run(pump)
                    spare = spare_steps(memkv)
                    move_chunks(spa_chunks())
                    attend(SPA_TILES, spare)
                T_event(mixer_out.name)
                norm(f"norm_x_{l}_", xq.name, 5 * l + 4, project_update(mixer_out), update_wait(mixer_out))
                run(spare)
                run(project_lo(xq.end(0) + 4))
                move_chunks(x_chunks("k"))
                for t in range(NT):
                    wide_mean(f"xq{l}_0{t}")
                for t in range(NT):
                    last = wide_heads(f"xq{l}_0{t}", cols[:, t, 0:512], 0)
                last.then_inc(heads_ready, 1)
                run(lo_of(xq, 2))
                for t in range(NT):
                    wide_mean(f"xq{l}_1{t}")
                    wide_heads(f"xq{l}_1{t}", cols[:, t, 512:1024], 0).then_inc(heads_ready, 1)
                move_chunks(x_chunks("q"))
                attend(X_TILES, project_lo(xq.end(1) + SPLIT))
                T_event(xo.name)
                norm(f"norm_ffn2_{l}_", f"ffn{2 * l + 1}", 5 * l + 5, project_update(xo), update_wait(xo))
                ffn(2 * l + 1)
            update = ffn_update(3)
            for t in range(NT):
                update(t)

        @block.tensor
        def _(pe):
            chunk = [0]
            tile = [0]

            def product(out, lh, ll, rh, rl, start, stop):
                nc.tensor.matmul(out, lh, rh, start=start, stop=False)
                nc.tensor.matmul(out, lh, rl, start=False, stop=False)
                return nc.tensor.matmul(out, ll, rh, start=False, stop=stop)

            def weight_block(n, k, width, pitch=512):
                at = slice(k * pitch, k * pitch + width)
                return w_hi[:, n % SPLIT, at], w_lo[:, n % SPLIT, at]

            def act_block(k, t, arrays_=(act_hi, act_lo)):
                at = slice(t * P, (t + 1) * P)
                return arrays_[0][:, k, at], arrays_[1][:, k, at]

            def T_tile_psum(name, src, ready, t):
                pe.wait_ge(*ready(t))
                for c, t, b, nb in T_tile(name, t):
                    for j in range(nb):
                        last = nc.tensor.transpose(SC[2 * t + b // 4][:, j * P:(j + 1) * P],
                                                   src[:, t, (b + j) * P:(b + j + 1) * P], ident[:, :])
                    last.then_inc(T_psum, 1)

            def T_split_of(name, t, block):
                c, kt, _ = T_first[name]
                per = 2 if kt > 4 else 1
                pe.wait_ge(T_split, c + t * per + (block // 4) + 1)

            def rows(name):
                return lambda t: (rows_ready, NT * ROWS.index(name) + t + 1)

            def up(f, n, c, i=None):
                if NCH * f + c > 0:
                    pe.wait_ge(gated_done, val(NT * (NCH * f + c), 2 * NT, i))
                for g in range(4):
                    pe.wait_ge(lo_done, val(n + g + 1, 12, i))
                    for k in range(2):
                        for t in range(NT):
                            last = product(SC[t], *act_block(2 * g + k, t), *weight_block(n + g, k, 512),
                                           g + k == 0, g == 3 and k == 1)
                    last.then_inc(unit_used, 1)

            def up_tile(f, n, t, event=None):
                if f + (event is None):
                    pe.wait_ge(gated_done, NT * NCH * f + (0 if event else NT * (NCH - 1)))
                for g in range(4):
                    if event and t == 0 and g == 3:
                        T_tile_psum(event, tm, rows(event), 1)
                    if event:
                        T_split_of(event, t, 2 * g + 1)
                    if t == 0:
                        pe.wait_ge(lo_done, n + g + 1)
                    for k in range(2):
                        last = product(SC[t], *act_block(2 * g + k, t), *weight_block(n + g, k, 512),
                                       g + k == 0, g == 3 and k == 1)
                    if t == 1:
                        last.then_inc(unit_used, 1)
                if t == 0:
                    last.then_inc(tile0_done, 1)

            def gate_transposes(f, c, i=None):
                for t in range(NT):
                    pe.wait_ge(gated_done, val(NT * (NCH * f + c) + t + 1, 2 * NT, i))
                    for b in range(2):
                        last = nc.tensor.transpose(SC[2][:, b * SEQ + t * P:b * SEQ + (t + 1) * P],
                                                   gated[:, t, b * P:(b + 1) * P], ident[:, :])
                last.then_inc(gT_psum, 1)

            def gate_transposes_last(f, t):
                pe.wait_ge(gated_done, NT * (NCH * f + NCH - 1) + t + 1)
                for b in range(2):
                    last = nc.tensor.transpose(SC[2 + t][:, b * P:(b + 1) * P], gated[:, t, b * P:(b + 1) * P],
                                               ident[:, :])
                last.then_inc(gT_psum, 1)

            def down(f, n, c, i=None):
                pe.wait_ge(gT_split, val(GT_COUNT * f + c + 1, 2, i))
                for b in range(2):
                    pe.wait_ge(lo_done, val(n + b + 1, 12, i))
                    for t in range(NT):
                        at = slice(t * P, (t + 1) * P)
                        for h in range(2):
                            last = product(acc(t, h), gT_hi[:, b, at], gT_lo[:, b, at],
                                           *weight_block(n + b, h, 512), False, False)
                    last.then_inc(unit_used, 1)

            def down_tile(n, t, hi_, lo_, stop):
                at = slice(t * P, (t + 1) * P)
                for b in range(2):
                    for h in range(2):
                        last = product(acc(t, h), hi_[:, b, at], lo_[:, b, at], *weight_block(n + b, h, 512),
                                       False, stop and b == 1)
                    if t == 1:
                        last.then_inc(unit_used, 1)
                return last

            def last_chunk(f, n):
                for t in range(NT):
                    up_tile(f, n, t)
                base = GT_COUNT * f + NCH
                pe.wait_ge(gT_split, base - 1)
                gate_transposes_last(f, 0)
                pe.wait_ge(lo_done, n + 6)
                down_tile(n + 4, 0, gT_hi, gT_lo, False)
                gate_transposes_last(f, 1)
                pe.wait_ge(gT_split, base)
                pe.wait_ge(lo_done, n + 8)
                down_tile(n + 6, 0, act_hi, act_lo, True).then_inc(ffn_sum, 1)
                down_tile(n + 4, 1, gT_hi, gT_lo, False)
                pe.wait_ge(gT_split, base + 1)
                down_tile(n + 6, 1, act_hi, act_lo, True)

            def ffn_step(f, n, c, i=None):
                up(f, n, c, i)
                down(f, n + 4, c - 1, i)
                gate_transposes(f, c, i)

            def ffn(f):
                n = place[f"ffn{f}"]
                name = f"ffn{f}"
                T_tile_psum(name, tm, rows(name), 0)
                for t in range(NT):
                    up_tile(f, n, t, name)
                for t in range(NT):
                    for h in range(2):
                        for b in range(2):
                            nc.tensor.matmul(acc(t, h)[:, b * SEQ:(b + 1) * SEQ], zeros[:, :],
                                             ident[:, :].bitcast(BF16), start=b == 0, stop=False)
                gate_transposes(f, 0)
                n += 4
                with pe.Fori(0, LOOPS) as i:
                    ffn_step(f, n, 1, i)
                    ffn_step(f, n + 6, 2, i)
                for c in range(1 + 2 * LOOPS, NCH - 1):
                    ffn_step(f, n + 6 * (c - 1), c)
                last_chunk(f, n + 6 * (NCH - 2))

            def project(pr, event, src=None, ready=None, k0=0, before={}, behind=None, between=None):
                arrays_ = T_dest(event)
                for g, (_, width, _, _) in enumerate(pr.groups):
                    if g in before:
                        before[g]()
                    G = pr.group0 + g
                    if g in pr.tiled:
                        for t in range(NT):
                            if g == 0 and t == 0 and src is not None:
                                T_tile_psum(event, src, ready, 0)
                                if behind is not None:
                                    behind()
                            if G >= 2:
                                pe.wait_ge(group_out[t], G - 1)
                            for u in range(pr.upg):
                                n = pr.unit0 + pr.upg * g + u
                                if g == 0 and t == 0 and u == pr.upg - 1 and src is not None:
                                    if between is not None:
                                        between()
                                    T_tile_psum(event, src, ready, 1)
                                T_split_of(event, t, 2 * u + 1)
                                if t == 0:
                                    pe.wait_ge(lo_done, n + 1)
                                for k in range(2 * u, 2 * u + 2):
                                    last = product(sums(pr, t, g), *act_block(k0 + k, t, arrays_),
                                                   *weight_block(n, k % 2, width), k == 0, k == pr.kt - 1)
                                if t == 1:
                                    last.then_inc(unit_used, 1)
                            if t == 0:
                                last.then_inc(tile0_done, 1)
                        continue
                    pe.wait_ge(T_split, T_done(event))
                    for t in range(NT):
                        if G >= 2:
                            pe.wait_ge(group_out[t], G - 1)
                    if pr.wide:
                        pe.wait_ge(lo_done, pr.unit0 + 1)
                        for t in range(NT):
                            last = product(sums(pr, t, g), *act_block(k0, t, arrays_),
                                           *weight_block(pr.unit0, g, width), True, True)
                        if g == len(pr.groups) - 1:
                            last.then_inc(unit_used, 1)
                        continue
                    for u in range(pr.upg):
                        n = pr.unit0 + pr.upg * g + u
                        pe.wait_ge(lo_done, n + 1)
                        for k in range(2 * u, 2 * u + 2):
                            for t in range(NT):
                                last = product(sums(pr, t, g), *act_block(k0 + k, t, arrays_),
                                               *weight_block(n, k % 2, width), k == 0, k == pr.kt - 1)
                        last.then_inc(unit_used, 1)

            def transpose_chunks(chunks):
                for srcs, dst in chunks:
                    c = chunk[0]
                    if CHUNKS[c][3] is not None:
                        who, count = CHUNKS[CHUNKS[c][3]][0:2]
                        pe.wait_ge(chunk_out[who], count)
                    for j, s in enumerate(srcs):
                        last = nc.tensor.transpose(CHUNKS[c][2][0:s.shape[1], j * P:(j + 1) * P], s, ident[:, :])
                    last.then_inc(chunk_psum, 1)
                    chunk[0] += 1

            def moved():
                for who in range(2):
                    count = sum(1 for c in CHUNKS[:chunk[0]] if c[0] == who)
                    if count:
                        pe.wait_ge(chunk_out[who], count)

            def operands(tl, r, s):
                q = slice(tl.qt * P, (tl.qt + 1) * P)
                h = tl.head(r)
                if tl.kind == "mla":
                    return [(mla_qT[0:MLA_QK, h, q], mla_kT[0:MLA_QK, h, 0:tl.keys])]
                half = slice((h % 2) * HD, (h % 2 + 1) * HD)
                if tl.kind == "dil":
                    return [(dil_qT[half, 2 * s + h // 2, q], dil_kT[half, 2 * s + h // 2, 0:tl.keys])]
                if tl.kind == "spa":
                    return [(spa_qT[half, h // 2, q], spa_kT[half, 0:tl.keys])]
                return [(x_qT[:, 2 * h + j, q], x_kT[:, 2 * h + j, 0:tl.keys]) for j in range(2)]

            def values(tl, r, s, kt):
                h = tl.head(r)
                return {"mla": lambda: v_mla[:, kt, h * HD:(h + 1) * HD],
                        "dil": lambda: dil_cols(kt)[:, s, 8 + h, :],
                        "spa": lambda: cols[:, kt, 1088:1152],
                        "x": lambda: kvb[:, kt, D + h * X_HD:D + (h + 1) * X_HD]}[tl.kind]()

            def mask_of(tl, r, s):
                if tl.kind == "mla":
                    return tl.keys - P, causal[:, P:SEQ]
                if tl.kind == "dil":
                    return 0, dil_mask[:, s, SEQ - tl.keys:]
                if tl.kind == "spa":
                    return 0, sel_mask[:, tl.qt, 0:tl.keys]
                return None

            def scores(tl, a):
                for r in range(tl.rows):
                    for s in range(tl.segs):
                        at = 1024 * (a % 2) + r * tl.pitch + s * tl.keys
                        parts = operands(tl, r, s)
                        for j, (q, k) in enumerate(parts):
                            last = nc.tensor.matmul(low[:, at:at + tl.keys], q, k, start=j == 0,
                                                    stop=mask_of(tl, r, s) is None and j == len(parts) - 1)
                        if mask_of(tl, r, s) is not None:
                            first, m = mask_of(tl, r, s)
                            last = nc.tensor.matmul(low[:, at + first:at + tl.keys], ident_b[:, :], m,
                                                    start=False, stop=True)
                last.then_inc(scores_ready, 1)

            def outputs(tl, a):
                if a >= 2:
                    pe.wait_ge(out_read, a - 1)
                moved()
                per = tl.width // P
                for r in range(tl.rows):
                    for j in range(per):
                        b = 1024 * (a % 2) + (r * per + j) * P
                        o = (tl.head(r) - tl.first) * tl.out
                        last = nc.tensor.matmul(OB[a % 2][:, o:o + tl.out], pTb[:, b:b + P],
                                                values(tl, r, j // (tl.keys // P), j % (tl.keys // P)),
                                                start=j == 0, stop=j == per - 1)
                last.then_inc(out_ready, 1)

            def attend(tiles):
                first = tile[0]
                scores(tiles[0], first)
                scores(tiles[1], first + 1)
                for j, tl in enumerate(tiles):
                    pe.wait_ge(probs_ready, first + j + 1)
                    transpose_chunks(prob_chunks(tl, first + j))
                    if j + 2 < len(tiles):
                        scores(tiles[j + 2], first + j + 2)
                    outputs(tl, first + j)
                tile[0] = first + len(tiles)

            def groups_read(pr):
                for t in range(NT):
                    pe.wait_ge(group_out[t], pr.group0 + len(pr.groups))

            pe.wait_ge(consts_made, 5)
            for l in range(2):
                ffn(2 * l)
                mixer_in = place[("even_in", "odd_in")[l]]
                mixer_out = place[("even_out", "odd_out")[l]]
                memkv, xq, xo = place[f"memkv{l}"], place[f"xq{l}"], place[f"xo{l}"]
                def T_memory():
                    for t in range(NT):
                        T_tile_psum(memkv.name, kvb, rows(memkv.name), t)

                if l == 0:
                    def T_lora():
                        for t in range(NT):
                            T_tile_psum("lora", tm, rows("lora"), t)

                    project(mixer_in, mixer_in.name, tm, rows(mixer_in.name), before={LORA_AT: T_lora})
                    pe.wait_ge(T_split, T_done("lora"))
                    T_memory()
                    project(place["uq"], "lora")
                    project(place["ukv"], "lora", k0=2)
                    project(memkv, memkv.name)
                    groups_read(memkv)
                    pe.wait_ge(heads_ready, HEADS["mla"])
                    transpose_chunks(mla_chunks())
                    moved()
                    attend(MLA_TILES)
                    transpose_chunks(dil_chunks())
                    moved()
                    attend(DIL_TILES)
                    out_count = [TILE0["dil"] + 2, TILE0["dil"] + len(DIL_TILES)]
                else:
                    def T_index():
                        pe.wait_ge(heads_ready, HEADS["idx"])
                        transpose_chunks(idx_chunks())

                    def logits(qt):
                        keys = P * (qt + 1)
                        for r in range(IDX_H):
                            h = half_first(r)
                            half = slice((h % 2) * HD, (h % 2 + 1) * HD)
                            last = nc.tensor.matmul(logits_of(qt)[:, r * keys:(r + 1) * keys],
                                                    idx_qT[half, h // 2, qt * P:(qt + 1) * P], idx_kT[half, 0:keys],
                                                    start=True, stop=True)
                        last.then_inc(logits_ready, 1)

                    project(mixer_in, mixer_in.name, tm, rows(mixer_in.name), before={3: T_index})
                    moved()
                    project(memkv, memkv.name, kvb, rows(memkv.name), before={1: lambda: logits(1)},
                            behind=lambda: logits(0), between=lambda: pe.wait_ge(relu_done, 1))
                    groups_read(memkv)
                    pe.wait_ge(relu_done, NT)
                    pe.wait_ge(heads_ready, HEADS["spa"])
                    transpose_chunks(spa_chunks())
                    moved()
                    pe.wait_ge(selected, 1)
                    attend(SPA_TILES)
                    out_count = [TILE0["spa"] + 2, TILE0["spa"] + len(SPA_TILES)]
                project(mixer_out, mixer_out.name, tm, lambda t: (out_read, out_count[t]))

                def T_keys():
                    pe.wait_ge(heads_ready, HEADS[f"xk{l}"])
                    transpose_chunks(x_chunks("k"))

                project(xq, xq.name, tm, rows(xq.name), before={1: T_keys})
                queries = list(x_chunks("q"))
                pe.wait_ge(heads_ready, HEADS[f"xq{l}_0"])
                transpose_chunks(queries[0:2])
                for t in range(NT):
                    pe.wait_ge(heads_ready, HEADS[f"xq{l}_1{t}"])
                    transpose_chunks(queries[2 + t:3 + t])
                moved()
                groups_read(xq)
                attend(X_TILES)
                project(xo, xo.name, tm, lambda t: (out_read, TILE0[f"x{l}"] + 2 * (t + 1)))
                ffn(2 * l + 1)


_F32 = ["mix_norm", "xattn_norm", "mem_norm", "xattn_wq", "xattn_wkv", "xattn_q_gain", "xattn_k_gain", "xattn_wo",
        "even_w_in", "mla_q_lora_norm", "mla_kv_lora_norm", "mla_w_uq", "mla_w_ukv", "mla_q_gain", "mla_k_gain",
        "dil_q_gain", "dil_k_gain", "even_w_out", "odd_w_in", "sparse_q_gain", "sparse_k_gain", "odd_w_out"]


def kernel(**inputs):
    import concourse.bacc as _bacc
    from concourse.bass_utils import run_bass_kernel_spmd as _run

    nc = _bacc.Bacc("TRN2", target_bir_lowering=False, num_devices=1)
    arrays = {}

    def give(name, a):
        a = np.ascontiguousarray(a)
        arrays["in_" + name] = a
        return nc.dram_tensor("in_" + name, a.shape, mybir.dt.from_np(a.dtype), kind="ExternalInput").ap()

    x_in = give("x", np.asarray(inputs["x"])[0])
    mem_in = give("mem", np.asarray(inputs["mem"])[0])
    positions = give("positions", inputs["positions"])
    norms = [give("ffn1_norm", inputs["ffn1_norm"]), give("ffn2_norm", inputs["ffn2_norm"])]
    w13 = [give("ffn1_w13", inputs["ffn1_w13"]), give("ffn2_w13", inputs["ffn2_w13"])]
    w2 = [give("ffn1_w2", inputs["ffn1_w2"]), give("ffn2_w2", inputs["ffn2_w2"])]
    all_w13 = [w13[f % 2][f // 2] for f in range(4)]
    all_w2 = [w2[f % 2][f // 2] for f in range(4)]
    rest = [give(name, inputs[name]) for name in _F32]
    inv = [np.exp(np.float32(-math.log(10000.0)) * np.arange(0, dim, 2, dtype=np.float32) / np.float32(dim))
           for dim in (HD, ROPE)]
    freq = give("rope_frequencies", np.concatenate(inv)[None].astype(np.float32))
    out = nc.dram_tensor("out", (SEQ, D), F32, kind="ExternalOutput").ap()
    build(nc, x_in, mem_in, positions, norms, all_w13, all_w2, *rest, freq, out)
    r = _run(nc, [arrays], core_ids=[0])
    return r.results[0]["out"].reshape(1, SEQ, D)
```
